# Optimizing a Trainium2 kernel written in Bass

```python
import math
import numpy as np
import jax
import jax.numpy as jnp
from jax import lax

D_MODEL = 1024
BATCH = 1
SEQ = 2048
DEPTH = 1

CTX_LEN = 256
GRID_W = 64

SSD_HEADS = 8
SSD_HEAD_DIM = 64
SSD_WIDTH = SSD_HEADS * SSD_HEAD_DIM
SSD_GROUPS = 2
SSD_STATE = 64
SSD_CONV = 5
SSD_CHUNK = 128
SSD_XBC = SSD_WIDTH + 2 * SSD_GROUPS * SSD_STATE
DT_MIN = 0.001
DT_MAX = 0.1

GLA_HEADS = 4
GLA_KEY_DIM = 64
GLA_VAL_DIM = 128
GLA_QK = GLA_HEADS * GLA_KEY_DIM
GLA_WIDTH = GLA_HEADS * GLA_VAL_DIM
GLA_GATE_RANK = 16
GLA_GATE_NORM = 16.0
GLA_CHUNK = 64

MIX_WIDTH = SSD_WIDTH + GLA_WIDTH
IN_DIM = SSD_WIDTH + SSD_XBC + SSD_HEADS + 2 * GLA_QK + 2 * GLA_WIDTH + GLA_GATE_RANK

N_EXPERTS = 32
N_EXPERT_GROUPS = 8
EXPERTS_PER_GROUP = N_EXPERTS // N_EXPERT_GROUPS
TOP_K = 2
EXPERT_FF = 512
MOE_BLOCK = 128

NORM_EPS = 1e-6

kernel_name = 'hybrid_ssd_gla_moe_prefix_dit'

def rmsnorm(x, gain):
    xf = x.astype(jnp.float32)
    y = xf * lax.rsqrt(jnp.mean(xf * xf, axis=-1, keepdims=True) + NORM_EPS)
    return (y * gain.astype(jnp.float32)).astype(x.dtype)

def modulate(h, shift, scale):
    return h * (1.0 + scale) + shift

def dwconv_centred(u, w, b):
    K, C = w.shape
    pad = K // 2
    y = lax.conv_general_dilated(u, w[:, None, :].astype(u.dtype), window_strides=(1,),
                                 padding=[(pad, K - 1 - pad)],
                                 dimension_numbers=('NWC', 'WIO', 'NWC'),
                                 feature_group_count=C)
    return y + b

def conv_latent(u, w, b):
    Bsz, L, C = u.shape
    rows = L // GRID_W
    y = dwconv_centred(u.reshape(Bsz * rows, GRID_W, C), w, b)
    return y.reshape(Bsz, L, C)

def ssd_scan(x, dt, Bm, Cm, A, h0, with_output):
    f32 = jnp.float32
    Bsz, L, H, P = x.shape
    G, N = Bm.shape[2], Bm.shape[3]
    Q = SSD_CHUNK
    nc = L // Q
    xc = x.astype(f32).reshape(Bsz, nc, Q, H, P)
    dtc = dt.astype(f32).reshape(Bsz, nc, Q, H)
    Bc = jnp.repeat(Bm.astype(f32), H // G, axis=2).reshape(Bsz, nc, Q, H, N)
    Cc = jnp.repeat(Cm.astype(f32), H // G, axis=2).reshape(Bsz, nc, Q, H, N)
    a_cs = jnp.cumsum(dtc * A.astype(f32), axis=2)
    a_end = a_cs[:, :, -1]
    w_end = jnp.exp(a_end[:, :, None] - a_cs) * dtc
    chunk_states = jnp.einsum('bcjh,bcjhn,bcjhp->bchpn', w_end, Bc, xc)

    def step(h, inp):
        decay, s = inp
        return decay[..., None, None] * h + s, h

    h_final, h_in = lax.scan(step, h0.astype(f32),
                             (jnp.moveaxis(jnp.exp(a_end), 1, 0), jnp.moveaxis(chunk_states, 1, 0)))
    if not with_output:
        return None, h_final
    h_in = jnp.moveaxis(h_in, 0, 1)
    causal = jnp.tril(jnp.ones((Q, Q), dtype=bool))
    seg = a_cs[:, :, :, None, :] - a_cs[:, :, None, :, :]
    decay_ij = jnp.exp(jnp.where(causal[None, None, :, :, None], seg, -jnp.inf))
    scores = jnp.einsum('bcihn,bcjhn->bcijh', Cc, Bc) * decay_ij * dtc[:, :, None, :, :]
    y = jnp.einsum('bcijh,bcjhp->bcihp', scores, xc)
    y = y + jnp.einsum('bcihn,bchpn->bcihp', Cc, h_in) * jnp.exp(a_cs)[..., None]
    return y.reshape(Bsz, L, H, P).astype(x.dtype), h_final

def gla_scan(q, k, v, g, S0, with_output):
    f32 = jnp.float32
    Bsz, L, H, K = q.shape
    V = v.shape[-1]
    Q = GLA_CHUNK
    nc = L // Q
    qc = (q.astype(f32) * (K ** -0.5)).reshape(Bsz, nc, Q, H, K)
    kc = k.astype(f32).reshape(Bsz, nc, Q, H, K)
    vc = v.astype(f32).reshape(Bsz, nc, Q, H, V)
    b = jnp.cumsum(g.astype(f32).reshape(Bsz, nc, Q, H, K), axis=2)
    b_end = b[:, :, -1]
    k_end = kc * jnp.exp(b_end[:, :, None] - b)
    chunk_states = jnp.einsum('bcjhk,bcjhv->bchkv', k_end, vc)

    def step(S, inp):
        decay, s = inp
        return decay[..., None] * S + s, S

    S_final, S_in = lax.scan(step, S0.astype(f32),
                             (jnp.moveaxis(jnp.exp(b_end), 1, 0), jnp.moveaxis(chunk_states, 1, 0)))
    if not with_output:
        return None, S_final
    S_in = jnp.moveaxis(S_in, 0, 1)
    q_dec = qc * jnp.exp(b)
    k_inv = kc * jnp.exp(-b)
    causal = jnp.tril(jnp.ones((Q, Q), dtype=bool))
    attn = jnp.where(causal, jnp.einsum('bcihk,bcjhk->bchij', q_dec, k_inv), 0.0)
    o = jnp.einsum('bchij,bcjhv->bcihv', attn, vc) + jnp.einsum('bcihk,bchkv->bcihv', q_dec, S_in)
    return o.reshape(Bsz, L, H, V).astype(q.dtype), S_final

def run_scan(scan_fn, seqs, params, state0, reverse, with_output):
    if reverse:
        seqs = [jnp.flip(s, axis=1) for s in seqs]
    y, state = scan_fn(*seqs, *params, state0, with_output)
    if reverse and with_output:
        y = jnp.flip(y, axis=1)
    return y, state

def mixer_inputs(h, p, conv_fn):
    f32 = jnp.float32
    Bsz, L, _ = h.shape
    sizes = [SSD_WIDTH, SSD_XBC, SSD_HEADS, GLA_QK, GLA_QK, GLA_WIDTH, GLA_WIDTH, GLA_GATE_RANK]
    offsets = np.cumsum(sizes)[:-1].tolist()
    z, xbc, dt_raw, q, k, v, g_out, gk_low = jnp.split(h @ p['w_in'], offsets, axis=-1)
    xbc = jax.nn.silu(conv_fn(xbc, p['conv_w'], p['conv_b']))
    xs, bm, cm = jnp.split(xbc, [SSD_WIDTH, SSD_WIDTH + SSD_GROUPS * SSD_STATE], axis=-1)
    gf = jax.nn.log_sigmoid((gk_low @ p['gk_up_f'] + p['gk_bias_f']).astype(f32)) / GLA_GATE_NORM
    gb = jax.nn.log_sigmoid((gk_low @ p['gk_up_b'] + p['gk_bias_b']).astype(f32)) / GLA_GATE_NORM

    def heads(t, n, d):
        return t.reshape(Bsz, L, n, d)

    return {
        'z': z,
        'g_out': g_out,
        'x': heads(xs, SSD_HEADS, SSD_HEAD_DIM),
        'B': heads(bm, SSD_GROUPS, SSD_STATE),
        'C': heads(cm, SSD_GROUPS, SSD_STATE),
        'dt_f': jax.nn.softplus((dt_raw + p['dt_bias_f']).astype(f32)),
        'dt_b': jax.nn.softplus((dt_raw + p['dt_bias_b']).astype(f32)),
        'q': heads(q, GLA_HEADS, GLA_KEY_DIM),
        'k': heads(k, GLA_HEADS, GLA_KEY_DIM),
        'v': heads(v, GLA_HEADS, GLA_VAL_DIM),
        'g_f': heads(gf, GLA_HEADS, GLA_KEY_DIM),
        'g_b': heads(gb, GLA_HEADS, GLA_KEY_DIM),
    }

def merge_heads(m, y_ssd, o_gla, p):
    Bsz, L = m['z'].shape[:2]
    y = (y_ssd + p['d_skip'][:, None] * m['x']).reshape(Bsz, L, SSD_WIDTH)
    y = rmsnorm(y * jax.nn.silu(m['z']), p['ssd_norm_g'])
    o = rmsnorm(o_gla, p['gla_norm_g']).reshape(Bsz, L, GLA_WIDTH) * jax.nn.silu(m['g_out'])
    return jnp.concatenate([y, o], axis=-1) @ p['w_out']

def token_mixers(h_ctx, h_lat, p, ctx_out):
    mc = mixer_inputs(h_ctx, p, dwconv_centred)
    ml = mixer_inputs(h_lat, p, conv_latent)
    a_f = -jnp.exp(p['a_log_f'].astype(jnp.float32))
    a_b = -jnp.exp(p['a_log_b'].astype(jnp.float32))
    Bsz = h_lat.shape[0]
    hs0 = jnp.zeros((Bsz, SSD_HEADS, SSD_HEAD_DIM, SSD_STATE), jnp.float32)
    gs0 = jnp.zeros((Bsz, GLA_HEADS, GLA_KEY_DIM, GLA_VAL_DIM), jnp.float32)
    ysc_f, hs_f = run_scan(ssd_scan, [mc['x'], mc['dt_f'], mc['B'], mc['C']], [a_f], hs0, False, ctx_out)
    ysc_b, hs_b = run_scan(ssd_scan, [mc['x'], mc['dt_b'], mc['B'], mc['C']], [a_b], hs0, True, ctx_out)
    ysl_f, _ = run_scan(ssd_scan, [ml['x'], ml['dt_f'], ml['B'], ml['C']], [a_f], hs_f, False, True)
    ysl_b, _ = run_scan(ssd_scan, [ml['x'], ml['dt_b'], ml['B'], ml['C']], [a_b], hs_b, True, True)
    goc_f, gs_f = run_scan(gla_scan, [mc['q'], mc['k'], mc['v'], mc['g_f']], [], gs0, False, ctx_out)
    goc_b, gs_b = run_scan(gla_scan, [mc['q'], mc['k'], mc['v'], mc['g_b']], [], gs0, True, ctx_out)
    gol_f, _ = run_scan(gla_scan, [ml['q'], ml['k'], ml['v'], ml['g_f']], [], gs_f, False, True)
    gol_b, _ = run_scan(gla_scan, [ml['q'], ml['k'], ml['v'], ml['g_b']], [], gs_b, True, True)
    out_lat = merge_heads(ml, ysl_f + ysl_b, gol_f + gol_b, p)
    out_ctx = merge_heads(mc, ysc_f + ysc_b, goc_f + goc_b, p) if ctx_out else None
    return out_ctx, out_lat

def route(t, w_router, router_bias):
    T = t.shape[0]
    s = jax.nn.sigmoid((t @ w_router).astype(jnp.float32))
    sel = (s + router_bias.astype(jnp.float32)).reshape(T, N_EXPERT_GROUPS, EXPERTS_PER_GROUP)
    group_score = lax.top_k(sel, 2)[0].sum(axis=-1)
    grp = jnp.argmax(group_score, axis=-1)
    in_grp = sel[jnp.arange(T), grp]
    _, local = lax.top_k(in_grp, TOP_K)
    ids = grp[:, None] * EXPERTS_PER_GROUP + local
    w = jnp.take_along_axis(s, ids, axis=1)
    return ids, w / jnp.sum(w, axis=-1, keepdims=True)

def moe(t, w_router, router_bias, w_gate, w_up, w_down):
    T, D = t.shape
    ids, gates = route(t, w_router, router_bias)
    flat_e = ids.reshape(-1)
    order = jnp.argsort(flat_e)
    e_sorted = flat_e[order]
    tok = order // TOP_K
    counts = jnp.zeros((N_EXPERTS,), jnp.int32).at[flat_e].add(1)
    padded = (counts + MOE_BLOCK - 1) // MOE_BLOCK * MOE_BLOCK
    start = jnp.cumsum(counts) - counts
    pend = jnp.cumsum(padded)
    pstart = pend - padded
    dest = pstart[e_sorted] + jnp.arange(T * TOP_K) - start[e_sorted]
    n_blocks = -(-(T * TOP_K) // MOE_BLOCK) + N_EXPERTS
    buf = jnp.zeros((n_blocks * MOE_BLOCK, D), t.dtype).at[dest].set(t[tok])
    block_e = jnp.minimum(jnp.searchsorted(pend, jnp.arange(n_blocks) * MOE_BLOCK, side='right'),
                          N_EXPERTS - 1)

    def expert_block(args):
        xb, e = args
        return (jax.nn.silu(xb @ w_gate[e]) * (xb @ w_up[e])) @ w_down[e]

    yb = lax.map(expert_block, (buf.reshape(n_blocks, MOE_BLOCK, D), block_e))
    y = yb.reshape(-1, D)[dest] * gates.reshape(-1)[order][:, None].astype(t.dtype)
    return jnp.zeros_like(t).at[tok].add(y)

def setup_inputs(seed: int = 0) -> dict:
    key = jax.random.key(seed)
    ks = jax.random.split(key, 32)
    f32 = jnp.float32

    def nrm(k, shape, scale):
        return jax.random.normal(k, shape, f32) * scale

    def gain(k, shape):
        return 1.0 + 0.05 * jax.random.normal(k, shape, f32)

    def dt_bias(k):
        dt = jnp.exp(jax.random.uniform(k, (DEPTH, SSD_HEADS), f32,
                                        minval=math.log(DT_MIN), maxval=math.log(DT_MAX)))
        return dt + jnp.log(-jnp.expm1(-dt))

    def a_log(k):
        return jnp.log(jax.random.uniform(k, (DEPTH, SSD_HEADS), f32, minval=1.0, maxval=16.0))

    return {
        'x': nrm(ks[0], (BATCH, SEQ, D_MODEL), 1.0),
        'c': nrm(ks[1], (BATCH, D_MODEL), 1.0),
        'ctx': nrm(ks[2], (BATCH, CTX_LEN, D_MODEL), 1.0),
        'c_ctx': nrm(ks[3], (D_MODEL,), 1.0),
        'w_mod': nrm(ks[4], (DEPTH, D_MODEL, 6 * D_MODEL), 0.5 * D_MODEL ** -0.5),
        'b_mod': nrm(ks[5], (DEPTH, 6 * D_MODEL), 0.02),
        'norm1_g': gain(ks[6], (DEPTH, D_MODEL)),
        'norm2_g': gain(ks[7], (DEPTH, D_MODEL)),
        'w_in': nrm(ks[8], (DEPTH, D_MODEL, IN_DIM), D_MODEL ** -0.5),
        'conv_w': nrm(ks[9], (DEPTH, SSD_CONV, SSD_XBC), SSD_CONV ** -0.5),
        'conv_b': nrm(ks[10], (DEPTH, SSD_XBC), 0.02),
        'dt_bias_f': dt_bias(ks[11]),
        'dt_bias_b': dt_bias(ks[12]),
        'a_log_f': a_log(ks[13]),
        'a_log_b': a_log(ks[14]),
        'd_skip': gain(ks[15], (DEPTH, SSD_HEADS)),
        'ssd_norm_g': gain(ks[16], (DEPTH, SSD_WIDTH)),
        'gk_up_f': nrm(ks[17], (DEPTH, GLA_GATE_RANK, GLA_QK), GLA_GATE_RANK ** -0.5),
        'gk_bias_f': nrm(ks[18], (DEPTH, GLA_QK), 0.02),
        'gk_up_b': nrm(ks[19], (DEPTH, GLA_GATE_RANK, GLA_QK), GLA_GATE_RANK ** -0.5),
        'gk_bias_b': nrm(ks[20], (DEPTH, GLA_QK), 0.02),
        'gla_norm_g': gain(ks[21], (DEPTH, GLA_VAL_DIM)),
        'w_out': nrm(ks[22], (DEPTH, MIX_WIDTH, D_MODEL), MIX_WIDTH ** -0.5),
        'w_router': nrm(ks[23], (D_MODEL, N_EXPERTS), D_MODEL ** -0.5),
        'router_bias': nrm(ks[24], (N_EXPERTS,), 0.01),
        'w_gate': nrm(ks[25], (DEPTH, N_EXPERTS, D_MODEL, EXPERT_FF), D_MODEL ** -0.5),
        'w_up': nrm(ks[26], (DEPTH, N_EXPERTS, D_MODEL, EXPERT_FF), D_MODEL ** -0.5),
        'w_down': nrm(ks[27], (DEPTH, N_EXPERTS, EXPERT_FF, D_MODEL), EXPERT_FF ** -0.5),
        'final_norm_g': gain(ks[28], (D_MODEL,)),
    }

def reference(x, c, ctx, c_ctx, w_mod, b_mod, norm1_g, norm2_g, w_in, conv_w, conv_b,
              dt_bias_f, dt_bias_b, a_log_f, a_log_b, d_skip, ssd_norm_g, gk_up_f, gk_bias_f,
              gk_up_b, gk_bias_b, gla_norm_g, w_out, w_router, router_bias, w_gate, w_up, w_down,
              final_norm_g):
    sc = jax.nn.silu(c)
    scc = jax.nn.silu(c_ctx)
    for l in range(DEPTH):
        last = l == DEPTH - 1
        p = {
            'w_in': w_in[l], 'conv_w': conv_w[l], 'conv_b': conv_b[l],
            'dt_bias_f': dt_bias_f[l], 'dt_bias_b': dt_bias_b[l],
            'a_log_f': a_log_f[l], 'a_log_b': a_log_b[l], 'd_skip': d_skip[l],
            'ssd_norm_g': ssd_norm_g[l], 'gk_up_f': gk_up_f[l], 'gk_bias_f': gk_bias_f[l],
            'gk_up_b': gk_up_b[l], 'gk_bias_b': gk_bias_b[l], 'gla_norm_g': gla_norm_g[l],
            'w_out': w_out[l],
        }
        m_lat = jnp.split((sc @ w_mod[l] + b_mod[l])[:, None, :], 6, axis=-1)
        m_ctx = jnp.split(scc @ w_mod[l] + b_mod[l], 6, axis=-1)
        h_lat = modulate(rmsnorm(x, norm1_g[l]), m_lat[0], m_lat[1])
        h_ctx = modulate(rmsnorm(ctx, norm1_g[l]), m_ctx[0], m_ctx[1])
        mix_ctx, mix_lat = token_mixers(h_ctx, h_lat, p, not last)
        x = x + m_lat[2] * mix_lat
        h2_lat = modulate(rmsnorm(x, norm2_g[l]), m_lat[3], m_lat[4])
        if last:
            ffn = moe(h2_lat.reshape(-1, D_MODEL), w_router, router_bias, w_gate[l], w_up[l], w_down[l])
            x = x + m_lat[5] * ffn.reshape(x.shape)
        else:
            ctx = ctx + m_ctx[2] * mix_ctx
            h2_ctx = modulate(rmsnorm(ctx, norm2_g[l]), m_ctx[3], m_ctx[4])
            n_ctx = h2_ctx.shape[0] * h2_ctx.shape[1]
            tokens = jnp.concatenate([h2_ctx.reshape(-1, D_MODEL), h2_lat.reshape(-1, D_MODEL)], axis=0)
            ffn = moe(tokens, w_router, router_bias, w_gate[l], w_up[l], w_down[l])
            ctx = ctx + m_ctx[5] * ffn[:n_ctx].reshape(ctx.shape)
            x = x + m_lat[5] * ffn[n_ctx:].reshape(x.shape)
    return rmsnorm(x, final_norm_g)


_drawn_inputs = setup_inputs


def setup_inputs(seed=0):
    import zlib

    import numpy as np

    out = dict(_drawn_inputs(seed))
    spreads = {}
    factors = {'ctx': 4.068,
     'c_ctx': 4.924,
     'conv_b': 3.537,
     'd_skip': 5.404,
     'gk_bias_f': 8.0,
     'gk_bias_b': 8.0,
     'gla_norm_g': 3.541}
    for name, (base, spread) in spreads.items():
        noise = np.random.default_rng([zlib.crc32(name.encode()), seed]).standard_normal(out[name].shape)
        drawn = base * np.exp(spread * noise) if base else spread * noise
        out[name] = jnp.asarray(drawn.astype(out[name].dtype))
    for name, factor in factors.items():
        out[name] = (out[name] * factor).astype(out[name].dtype)
    return out
```

```python
from contextlib import ExitStack

import concourse.bass as bass
from concourse import mybir

ALU = mybir.AluOpType
ACT = mybir.ActivationFunctionType
F32 = mybir.dt.float32
I32 = mybir.dt.int32
AX = mybir.AxisListType.X

P = 128
D = 1024
KT = D // P
SEQ = 2048
CTX = 256
GRP = 256
LAT_GROUPS = SEQ // GRP
TILES = (SEQ + CTX) // P
CT = CTX // P
LT = SEQ // P
SH, SP_, SN = 8, 64, 64
SW = SH * SP_
XBC = SW + 4 * SN
GH, GK, GV = 4, 64, 128
GQK = GH * GK
GW = GH * GV
RANK = 16
TAPS = 5
ROWW = 64
O_Z, O_XBC, O_DT = 0, SW, SW + XBC
O_Q = O_DT + SH
O_K = O_Q + GQK
O_V = O_K + GQK
O_G = O_V + GW
O_GK = O_G + GW
IN_DIM = O_GK + RANK
NE, NG, EG = 32, 8, 4
FF = 512
EPS = 1e-6
MAXB = 64
BIG = 1e30

R_C, R_CC = 0, KT
R_N1, R_N2 = 2 * KT, 3 * KT
R_BM = 4 * KT
R_CW = R_BM + 6 * KT
R_CB = R_CW + TAPS * (XBC // P)
R_SG = R_CB + XBC // P
R_GG = R_SG + SW // P
N_ROWS = R_GG + 1

T_X, T_B, T_K = 0, SW, SW + 2 * SN
T_V = T_K + GQK
T_DT = T_V + GW
T_GF = T_DT + 2 * SH
T_Z = T_GF + 2 * GQK
T_GO = T_Z + SW
T_LEN = T_GO + GW
F_TILES = 6


def hold(eng, sem, value, held):
    eng.wait_ge(sem, value)
    eng.sem_inc(held, 1)


class Names:

    def __init__(self, nc, ctx, prefix):
        self.nc, self.prefix, self.made = nc, prefix, []
        ctx.callback(self.clear)

    def __call__(self, name):
        self.made.append(self.nc.alloc_semaphore(f"{self.prefix}_{name}"))
        return self.made[-1]

    def clear(self):
        self.nc.clear_and_free_semaphores(self.made)
        self.nc.all_engine_barrier()


def build(nc, A, out, debug=()):
    def scratch(name, shape, dt=F32):
        kind = "ExternalOutput" if name in debug else "Internal"
        return nc.dram_tensor(name, shape, dt, kind=kind).ap()

    tok_rec = scratch("tok_rec", (TILES, P, T_LEN))
    feat_rec = scratch("feat_rec", (TILES, P, F_TILES * P))
    back_state = scratch("back_state", (TILES, P, 3 * 256))
    fwd_state = scratch("fwd_state", (1, P, 3 * 256))
    x_mid = scratch("x_mid", (LT, P, D))
    x_hat = scratch("x_hat", (SEQ, D))
    slot_tok = scratch("slot_tok", (TAB * P, 16), I32)
    y_slots = scratch("y_slots", (MAXB * P, D))

    with ExitStack() as top:
        def keep(name, shape, dt=F32):
            return top.enter_context(nc.sbuf_tensor(name, shape, dt))

        C = {n: keep(n, [P, P]) for n in ("ident", "ones", "gt", "lt", "gt_bd", "lt_bd")}
        C["incl"], C["incl_bd"] = keep("incl", [P, 2, P]), keep("incl_bd", [P, 2, P])
        for d, n in enumerate(("le", "ge")):
            C[n], C[n + "_bd"] = C["incl"][:, d, :], C["incl_bd"][:, d, :]
        C["halves"] = keep("halves", [P, 2])
        mod = keep("mod", [P, 6 * KT, 2])
        C["mod"] = mod
        C["cols"] = keep("cols", [P, N_ROWS])
        route = {
            "logits": keep("logits", [P, LT, NE]), "gate": keep("gate", [P, LT, 2]),
            "slot": keep("slot", [P, LT, 2], I32), "plan": keep("plan", [1, PL_LEN], I32),
        }
        constants(nc, C)
        modulation(nc, A, C)
        projection(nc, A, C, tok_rec, feat_rec)
        if "stop1" in debug:
            return
        scan_states(nc, A, C, tok_rec, 1, back_state)
        scan_states(nc, A, C, tok_rec, 0, fwd_state)
        if "stop2" in debug:
            return
        mixer(nc, A, C, route, tok_rec, feat_rec, back_state, fwd_state, x_mid, x_hat)
        if "stop3" in debug:
            return
        slots(nc, A, C, route, slot_tok)
        experts(nc, A, C, route, slot_tok, x_hat, y_slots)
        combine(nc, A, C, route, y_slots, x_mid, out)


def constants(nc, C):
    with ExitStack() as ctx:
        sem = Names(nc, ctx, "cst")
        block = ctx.enter_context(nc.Block())
        made, cut = sem("made"), sem("cut")
        H = P // 2

        @block.gpsimd
        def _(pool):
            n = 0
            for name in ("ident", "le_bd", "ge_bd", "gt_bd", "lt_bd"):
                pool.memset(C[name][:, :], 1.0 if name != "ident" else 0.0).then_inc(made, 1)
                n += 1
            for name in ("ones", "le", "ge", "gt", "lt", "halves"):
                pool.memset(C[name][:, :], 1.0).then_inc(made, 1)
                n += 1
            pool.wait_ge(made, n)
            def select(t, step, cm, base, op, fill=0.0, w=P):
                pool.affine_select(out=t, in_=t, compare_op=op, fill=fill, base=base,
                                   pattern=[[step, w]], channel_multiplier=cm).then_inc(cut, 1)
            select(C["ident"][:, :], -1, 1, 0, ALU.not_equal, 1.0)
            signs = {"le": (1, -1, ALU.is_ge), "ge": (-1, 1, ALU.is_ge),
                     "gt": (-1, 1, ALU.is_gt), "lt": (1, -1, ALU.is_gt)}
            m = 1
            for name, (step, cm, op) in signs.items():
                select(C[name][:, :], step, cm, 0, op)
                select(C[name + "_bd"][:, :], step, cm, 0, op)
                m += 2
            pool.wait_ge(cut, m)
            for name in signs:
                pool.memset(C[name + "_bd"][0:H, H:P], 0.0).then_inc(cut, 1)
                pool.memset(C[name + "_bd"][H:P, 0:H], 0.0).then_inc(cut, 1)
            pool.memset(C["halves"][0:H, 1:2], 0.0).then_inc(cut, 1)
            pool.memset(C["halves"][H:P, 0:1], 0.0).then_inc(cut, 1)
            pool.wait_ge(cut, m + 10)


def modulation(nc, A, C):
    mod = C["mod"]
    W = 512
    STEPS = 6 * D // W
    w_d = A["w_mod"].rearrange("l (k p) (n c) -> l n p k c", p=P, c=W)[0]
    with ExitStack() as ctx:
        sem = Names(nc, ctx, "mod")
        slab = [ctx.enter_context(nc.sbuf_tensor(f"w_mod{b}", [P, KT, W], F32)) for b in range(2)]
        rows = ctx.enter_context(nc.sbuf_tensor("rows", [N_ROWS, P], F32))
        cond = ctx.enter_context(nc.sbuf_tensor("cond_silu", [P, KT, 2], F32))
        rows_t = ctx.enter_context(nc.psum_tensor("rows_t", [P, N_ROWS], F32))
        cols = C["cols"]
        bias = cols[:, R_BM:R_BM + 6 * KT]
        acc = ctx.enter_context(nc.psum_tensor("mod_acc", [P, 6 * KT, 2], F32))
        loaded = [sem("slab0_loaded"), sem("slab1_loaded")]
        small, turned, copied, silu_done, slab_used, added, scaled = (
            sem(n) for n in ("small_loaded", "rows_transposed", "cols_copied", "silu_done", "slab_used", "added", "scaled"))
        block = ctx.enter_context(nc.Block())

        @block.sync
        def _(sp):
            for at, n, src in ((R_C, KT, A["c"].rearrange("b (k p) -> (b k) p", p=P)),
                               (R_CC, KT, A["c_ctx"].rearrange("(k p) -> k p", p=P)),
                               (R_N1, KT, A["norm1_g"].rearrange("l (k p) -> (l k) p", p=P)),
                               (R_N2, KT, A["norm2_g"].rearrange("l (k p) -> (l k) p", p=P)),
                               (R_BM, 6 * KT, A["b_mod"].rearrange("l (k p) -> (l k) p", p=P)),
                               (R_CW, TAPS * 6, A["conv_w"].rearrange("l t (k p) -> (l t k) p", p=P)),
                               (R_CB, 6, A["conv_b"].rearrange("l (k p) -> (l k) p", p=P)),
                               (R_SG, 4, A["ssd_norm_g"].rearrange("l (k p) -> (l k) p", p=P)),
                               (R_GG, 1, A["gla_norm_g"])):
                sp.dma_start(rows[at:at + n, :], src).then_inc(small, 16)
            sp.sem_inc(slab_used, 2)
            with sp.Fori(0, STEPS // 2) as r:
                for u in range(2):
                    sp.wait_ge(slab_used, r * 2 + (u + 1))
                    sp.dma_start(slab[u][:, :, :], w_d[r * 2 + u]).then_inc(loaded[u], 16)

        @block.scalar
        def _(act):
            act.wait_ge(copied, 1)
            for j in range(2):
                act.activation(cond[:, :, j], cols[:, KT * j:KT * (j + 1)], ACT.Silu).then_inc(silu_done, 1)

        @block.tensor
        def _(pe):
            pe.wait_ge(small, 16 * 9)
            pe.transpose(rows_t[:, :], rows[:, :], C["ident"][0:N_ROWS, 0:N_ROWS]).then_inc(turned, 1)
            pe.wait_ge(silu_done, 2)
            with pe.Fori(0, STEPS // 2) as r:
                for u in range(2):
                    pe.wait_ge(loaded[u], r * 16 + 16)
                    for m in range(W // P):
                        for k in range(KT):
                            mm = pe.matmul(acc[:, bass.ds(r * 8 + (u * 4 + m), 1), :], slab[u][:, k, m * P:(m + 1) * P],
                                           cond[:, k, :], start=(k == 0), stop=(k == KT - 1))
                    mm.then_inc(slab_used, 1)

        @block.vector
        def _(dve):
            dve.wait_ge(turned, 1)
            dve.tensor_copy(cols[:, :], rows_t[:, :]).then_inc(copied, 1)
            dve.wait_ge(copied, 1)
            dve.wait_ge(slab_used, 2 + STEPS)
            dve.tensor_tensor(mod[:, :, :], acc[:, :, :], bias.unsqueeze(2).to_broadcast([P, 6 * KT, 2]),
                              ALU.add).then_inc(added, 1)
            dve.wait_ge(added, 1)
            for n, part in enumerate((1, 4)):
                s = mod[:, part * KT:(part + 1) * KT, :]
                dve.scalar_tensor_tensor(out=s, in0=s, scalar=1.0, in1=cols[:, R_N1 + KT * n:R_N1 + KT * (n + 1)].unsqueeze(2).to_broadcast([P, KT, 2]),
                                         op0=ALU.add, op1=ALU.mult).then_inc(scaled, 1)
            dve.wait_ge(scaled, 2)


def projection(nc, A, C, tok_rec, feat_rec):
    mod, ident = C["mod"], C["ident"]
    x_d = A["x"].rearrange("b (g s p) d -> (b g) p s d", s=2, p=P)
    ctx_d = A["ctx"].rearrange("b (s p) d -> b p s d", p=P)[0]
    w_in = A["w_in"][0]
    tok_g = tok_rec.rearrange("(g s) p f -> g p s f", s=2)
    feat_g = feat_rec.rearrange("(g s) p (n c) -> g s p n c", s=2, c=P)
    NF = 10
    col = [O_XBC + i * P for i in range(6)] + [O_Q, O_Q + P, O_K, O_K + P]
    with ExitStack() as ctx:
        sem = Names(nc, ctx, "prj")

        def sb(name, shape, dt=F32):
            return ctx.enter_context(nc.sbuf_tensor(name, shape, dt))

        def ps(name, shape):
            return ctx.enter_context(nc.psum_tensor(name, shape, F32))

        w = sb("w_in_sb", [P, KT, IN_DIM])
        w_small = sb("w_small", [P, KT, 32])
        xg = sb("xg", [P, 2, D])
        junk = ps("sq_junk", [P, 512])
        hT = [sb(f"hT{b}", [P, KT, GRP]) for b in range(2)]
        u_raw = sb("u_raw", [P, 6, GRP])
        fm = sb("fm", [P, NF, GRP])
        tm = [sb(f"tm{b}", [P, 2, T_LEN]) for b in range(2)]
        soft = [sb(f"soft{b}", [P, 528]) for b in range(2)]
        small_sb = sb("small_sb", [P, 2, 32])
        gkT = sb("gkT", [RANK + 1, 2, P])
        up = sb("gk_up", [RANK + 1, 2 * GQK])
        dtb = sb("dt_bias", [1, 2 * SH])
        cols = C["cols"]
        ss = sb("ss", [P, 2, 2])
        rstd = sb("rstd", [P, 2])
        mhalf = sb("mhalf", [P, 2])
        pt = [ps(f"pt{b}", [P, 512]) for b in range(2)]
        pf = [ps(f"pf{b}", [P, 2, GRP]) for b in range(2)]
        pz = [ps(f"pz{b}", [P, 512]) for b in range(2)]
        psm = ps("psm", [P, 512])

        pool_held = sem("pool_held")
        w_loaded, small_loaded, x_loaded = sem("w_loaded"), sem("small_loaded"), sem("x_loaded")
        x_free, ss_done, rstd_done, xn_done = (sem(n) for n in ("x_free", "ss_done", "rstd_done", "xn_done"))
        ht_ps, ht_done = sem("ht_transposed"), sem("ht_done")
        feat_ps, u_done, qk_done, conv_done, silu_done = (
            sem(n) for n in ("feat_product", "u_done", "qk_done", "conv_done", "silu_done"))
        tok_ps, tok_done = sem("tok_product"), sem("tok_done")
        small_ps, small_done, gk_ps, gk_done, g_ps, abs_done, exp_done, ln_done, min_done, g_done = (
            sem(n) for n in ("small_product", "small_copied", "gk_transposed", "gk_copied", "g_product",
                             "abs_done", "exp_done", "ln_done", "min_done", "g_done"))
        back_ps, back_done = sem("back_transposed"), sem("back_copied")
        stored, feat_stored = [sem("tm0_stored"), sem("tm1_stored")], sem("fm_stored")
        const_done, wsm_done, junk_done = sem("const_done"), sem("w_small_done"), sem("junk_done")
        conv_step, hT_free = sem("conv_step"), sem("hT_free")
        block = ctx.enter_context(nc.Block())

        def steps(eng, body):
            body(0, 0, 0, True)
            with eng.Fori(0, LAT_GROUPS // 2) as r:
                body(r * 2 + 1, r, 1, False)
                body(r * 2 + 2, r + 1, 0, False)

        @block.sync
        def _(sp):
            sp.dma_start(dtb[:, 0:SH], A["dt_bias_f"]).then_inc(small_loaded, 16)
            sp.dma_start(dtb[:, SH:2 * SH], A["dt_bias_b"]).then_inc(small_loaded, 16)
            sp.dma_start(up[0:RANK, 0:GQK], A["gk_up_f"][0]).then_inc(small_loaded, 16)
            sp.dma_start(up[0:RANK, GQK:2 * GQK], A["gk_up_b"][0]).then_inc(small_loaded, 16)
            sp.dma_start(up[RANK:RANK + 1, 0:GQK], A["gk_bias_f"]).then_inc(small_loaded, 16)
            sp.dma_start(up[RANK:RANK + 1, GQK:2 * GQK], A["gk_bias_b"]).then_inc(small_loaded, 16)

            def body(it, use, buf, is_ctx):
                if is_ctx:
                    for k in range(KT):
                        sp.dma_start(w[:, k, :], w_in[k * P:(k + 1) * P, :]).then_inc(w_loaded, 16)
                sp.wait_ge(silu_done, it + 1)
                sp.wait_ge(qk_done, it * 2 + 2)
                for s in range(2):
                    sp.dma_start(feat_g[it][s], fm[:, 4:10, s * P:(s + 1) * P]).then_inc(feat_stored, 16)
                sp.wait_ge(tok_done, 2 if is_ctx else 2 + it * 6)
                sp.wait_ge(g_done, it * 2 + 2)
                sp.wait_ge(back_done, it * 4 + 4)
                if is_ctx:
                    sp.dma_start(tok_g[0][:, :, 0:T_Z], tm[buf][:, :, 0:T_Z]).then_inc(stored[buf], 16)
                else:
                    sp.dma_start(tok_g[it], tm[buf][:, :, :]).then_inc(stored[buf], 16)

            steps(sp, body)
            sp.wait_ge(feat_stored, 32 * (LAT_GROUPS + 1))
            sp.wait_ge(stored[0], 16 * (LAT_GROUPS // 2 + 1))
            sp.wait_ge(stored[1], 16 * (LAT_GROUPS // 2 + 1))

        @block.scalar
        def _(act):
            def body(it, use, buf, is_ctx):
                act.wait_ge(x_loaded, it * 16 + 16)
                for s in range(2):
                    for h in range(2):
                        if s + h:
                            act.wait_ge(junk_done, it * 4 + 2 * s + h)
                        elif not is_ctx:
                            act.wait_ge(junk_done, it * 4)
                        act.activation(junk[:, :], xg[:, s, h * 512:(h + 1) * 512], ACT.Square,
                                       accum_out=ss[:, s, h:h + 1]).then_inc(junk_done, 1)
                act.wait_ge(junk_done, it * 4 + 4)
                act.sem_inc(ss_done, 1)
                for n in range(5):
                    act.wait_ge(feat_ps, it * 5 + (n + 1))
                    if n < 3:
                        if n == 0 and not is_ctx:
                            act.wait_ge(conv_done, it)
                        act.activation(u_raw[:, 2 * n:2 * n + 2, :], pf[(n) % 2][:, :, :], ACT.Copy).then_inc(u_done, 1)
                    else:
                        if n == 3 and not is_ctx:
                            act.wait_ge(feat_stored, it * 32)
                            act.wait_ge(back_done, it * 4)
                        act.activation(fm[:, 2 * n:2 * n + 2, :], pf[(n) % 2][:, :, :], ACT.Copy,
                                       scale=GK ** -0.5 if n == 3 else 1.0).then_inc(qk_done, 1)
                act.wait_ge(conv_done, it + 1)
                act.activation(fm[:, 0:6, :], fm[:, 0:6, :], ACT.Silu).then_inc(silu_done, 1)
                n = 0
                per = 2 if is_ctx else 6
                base = 0 if is_ctx else 2 + (it - 1) * 6
                for s in range(2):
                    for part in ("v",) if is_ctx else ("z", "g", "v"):
                        act.wait_ge(tok_ps, base + (n + 1))
                        if n == 0 and not is_ctx:
                            act.wait_ge(stored[buf], use * 16 + 16 * buf)
                        o = {"z": T_Z, "g": T_GO, "v": T_V}[part]
                        act.activation(tm[buf][:, s, o:o + 512], pz[n % 2][:, :],
                                       ACT.Copy if part == "v" else ACT.Silu).then_inc(tok_done, 1)
                        n += 1
                for s in range(2):
                    act.wait_ge(g_ps, it * 2 + (s + 1))
                    if not is_ctx:
                        act.wait_ge(g_done, it * 2)
                    act.activation(soft[s][:, 0:512], pz[s][:, :], ACT.Abs).then_inc(abs_done, 1)
                    act.activation(soft[s][:, 512:528], small_sb[:, s, 0:16], ACT.Abs).then_inc(abs_done, 1)
                for s in range(2):
                    act.wait_ge(abs_done, it * 4 + 2 * s + 2)
                    act.activation(soft[s][:, :], soft[s][:, :], ACT.Exp, scale=-1.0).then_inc(exp_done, 1)
                for s in range(2):
                    act.wait_ge(exp_done, it * 2 + (s + 1))
                    act.activation(soft[s][:, :], soft[s][:, :], ACT.Ln, bias=1.0).then_inc(ln_done, 1)
            act.sem_inc(stored[1], 16)
            steps(act, body)

        @block.gpsimd
        def _(pool):
            pool.memset(mhalf[:, :], -0.5).then_inc(const_done, 1)
            pool.memset(gkT[:, :, :], 1.0).then_inc(const_done, 1)
            pool.wait_ge(const_done, 2)

            def body(it, use, buf, is_ctx):
                if not is_ctx:
                    hold(pool, x_free, it, pool_held)
                pool.dma_start(xg[:, :, :], ctx_d if is_ctx else x_d[it - 1]).then_inc(x_loaded, 16)
                pool.wait_ge(ss_done, it + 1)
                if not is_ctx:
                    pool.wait_ge(xn_done, it)
                pool.tensor_tensor(rstd[:, :], ss[:, :, 0], ss[:, :, 1], ALU.add).then_inc(rstd_done, 1)
                hold(pool, rstd_done, it * 3 + 1, pool_held)
                pool.tensor_scalar(rstd[:, :], rstd[:, :], 1.0 / D, EPS, ALU.mult, ALU.add).then_inc(rstd_done, 1)
                pool.wait_ge(rstd_done, it * 3 + 2)
                pool.tensor_tensor(rstd[:, :], rstd[:, :], mhalf[:, :], ALU.pow).then_inc(rstd_done, 1)
            steps(pool, body)

        @block.tensor
        def _(pe):
            pe.wait_ge(wsm_done, 2)
            pe.wait_ge(const_done, 2)
            pe.wait_ge(small_loaded, 16 * 6)

            def body(it, use, buf, is_ctx):
                pe.wait_ge(xn_done, it + 1)
                for q in range(4):
                    if q >= 2:
                        pe.wait_ge(ht_done, it * 4 + (q - 1))
                    elif not is_ctx:
                        pe.wait_ge(back_done, it * 4)
                    for kk in range(2):
                        for s in range(2):
                            mm = pe.transpose(pt[q % 2][:, kk * GRP + s * P:kk * GRP + (s + 1) * P],
                                              xg[:, s, (2 * q + kk) * P:(2 * q + kk + 1) * P], ident[:, :])
                    mm.then_inc(ht_ps, 1)
                pe.wait_ge(ht_done, it * 4 + 4)
                h = hT[buf]
                for n in range(5):
                    if n >= 2 or not is_ctx:
                        m = n - 2
                        if m >= 0:
                            pe.wait_ge(u_done if m < 3 else qk_done, it * 3 + (m + 1) if m < 3 else it * 2 + (m - 2))
                        elif n == 0:
                            pe.wait_ge(qk_done, it * 2)
                    for f in range(2):
                        for k in range(KT):
                            c0 = col[2 * n + f]
                            mm = pe.matmul(pf[n % 2][:, f, :], w[:, k, c0:c0 + P], h[:, k, :],
                                           start=(k == 0), stop=(k == KT - 1))
                    mm.then_inc(feat_ps, 1)
                if not is_ctx:
                    pe.wait_ge(gk_done, it)
                    pe.wait_ge(small_done, it)
                for s in range(2):
                    for k in range(KT):
                        pe.matmul(psm[:, s * 32:s * 32 + 32], h[:, k, s * P:(s + 1) * P], w_small[:, k, :],
                                  start=(k == 0), stop=False)
                    mm = pe.matmul(psm[:, s * 32:s * 32 + 16], C["ones"][0:1, :], dtb[0:1, :], start=False, stop=True)
                mm.then_inc(small_ps, 1)
                n = 0
                base = 0 if is_ctx else 2 + (it - 1) * 6
                for s in range(2):
                    for part in ("v",) if is_ctx else ("z", "g", "v"):
                        if n >= 2:
                            pe.wait_ge(tok_done, base + (n - 1))
                        elif n == 0 and not is_ctx:
                            pe.wait_ge(min_done, it * 4)
                            pe.wait_ge(abs_done, it * 4)
                        o = {"z": O_Z, "g": O_G, "v": O_V}[part]
                        for k in range(KT):
                            mm = pe.matmul(pz[n % 2][:, :], h[:, k, s * P:(s + 1) * P], w[:, k, o:o + 512],
                                           start=(k == 0), stop=(k == KT - 1))
                        mm.then_inc(tok_ps, 1)
                        n += 1
                pe.wait_ge(small_done, it + 1)
                for s in range(2):
                    mm = pe.transpose(psm[0:RANK, 128 + s * P:256 + s * P], small_sb[:, s, 16:32], ident[:, :])
                mm.then_inc(gk_ps, 1)
                pe.wait_ge(gk_done, it + 1)
                pe.wait_ge(tok_done, base + n)
                for s in range(2):
                    pe.matmul(pz[s][:, :], gkT[:, s, :], up[:, :], start=True, stop=True).then_inc(g_ps, 1)
                pe.wait_ge(silu_done, it + 1)
                pe.wait_ge(qk_done, it * 2 + 2)
                for s in range(2):
                    for half in range(2):
                        q = 2 * s + half
                        if q >= 2:
                            pe.wait_ge(back_done, it * 4 + (q - 1))
                        tiles = (0, 1, 2, 3) if half == 0 else (4, 8, 9)
                        for j, f in enumerate(tiles):
                            mm = pe.transpose(pt[q % 2][:, j * P:(j + 1) * P], fm[:, f, s * P:(s + 1) * P], ident[:, :])
                        mm.then_inc(back_ps, 1)
            steps(pe, body)

        @block.vector
        def _(dve):
            dve.wait_ge(w_loaded, 16 * KT)
            for j in range(2):
                dve.tensor_copy(w_small[:, :, 8 * j:8 * j + 8], w[:, :, O_DT:O_DT + 8])
            dve.tensor_copy(w_small[:, :, 16:32], w[:, :, O_GK:O_GK + 16]).then_inc(wsm_done, 2)
            dve.wait_ge(small_loaded, 16 * 6)

            def body(it, use, buf, is_ctx):
                dve.wait_ge(rstd_done, it * 3 + 3)
                for s in range(2):
                    i = dve.tensor_scalar(xg[:, s, :], xg[:, s, :], rstd[:, s:s + 1], None, ALU.mult)
                i.then_inc(xn_done, 1)
                who = 1 if is_ctx else 0
                for q in range(4):
                    dve.wait_ge(ht_ps, it * 4 + (q + 1))
                    for kk in range(2):
                        k = 2 * q + kk
                        i = dve.tensor_scalar(hT[buf][:, k, :], pt[q % 2][:, kk * GRP:(kk + 1) * GRP],
                                              mod[:, KT + k, who:who + 1], mod[:, k, who:who + 1], ALU.mult, ALU.add)
                    i.then_inc(ht_done, 1)
                    if q == 3:
                        dve.sem_inc(x_free, 1)
                wide = GRP if is_ctx else ROWW
                dve.wait_ge(u_done, it * 3 + 3)
                if not is_ctx:
                    dve.wait_ge(feat_stored, it * 32)
                    dve.wait_ge(back_done, it * 4)
                for n, tap in enumerate((2, 0, 1, 3, 4)):
                    if n:
                        dve.wait_ge(conv_step, it * 4 + n)
                    for f in range(6):
                        a = fm[:, f, :].rearrange("p (r t) -> p r t", t=wide)
                        b = u_raw[:, f, :].rearrange("p (r t) -> p r t", t=wide)
                        wt = cols[:, R_CW + 6 * tap + f:R_CW + 6 * tap + f + 1]
                        if tap == 2:
                            i = dve.tensor_scalar(a, b, wt, cols[:, R_CB + f:R_CB + f + 1], ALU.mult, ALU.add)
                            continue
                        sh = tap - 2
                        to, fr = (a[:, :, -sh:], b[:, :, :wide + sh]) if sh < 0 else (a[:, :, :wide - sh], b[:, :, sh:])
                        i = dve.scalar_tensor_tensor(out=to, in0=fr, scalar=wt, in1=to, op0=ALU.mult, op1=ALU.add)
                    i.then_inc(conv_done if n == 4 else conv_step, 1)
                dve.wait_ge(small_ps, it + 1)
                if not is_ctx:
                    dve.wait_ge(abs_done, it * 4)
                    dve.wait_ge(min_done, it * 4)
                dve.tensor_copy(small_sb[:, :, :], psm[:, 0:64].rearrange("p (s c) -> p s c", s=2)).then_inc(small_done, 1)
                dve.wait_ge(gk_ps, it + 1)
                dve.tensor_copy(gkT[0:RANK, :, :], psm[0:RANK, 128:384].rearrange("p (s c) -> p s c", s=2)).then_inc(gk_done, 1)
                t = tm[buf]
                if not is_ctx:
                    dve.wait_ge(stored[buf], use * 16 + (0 if buf == 0 else 16))
                for s in range(2):
                    dve.wait_ge(g_ps, it * 2 + (s + 1))
                    dve.wait_ge(abs_done, it * 4 + (2 * s + 1))
                    dve.tensor_scalar(t[:, s, T_GF:T_GF + 512], pz[s][:, :], 0.0, 1 / 16.0, ALU.min, ALU.mult).then_inc(min_done, 1)
                    dve.tensor_scalar(t[:, s, T_DT:T_DT + 16], small_sb[:, s, 0:16], 0.0, None, ALU.max).then_inc(min_done, 1)
                for s in range(2):
                    for half in range(2):
                        q = 2 * s + half
                        dve.wait_ge(back_ps, it * 4 + (q + 1))
                        if half == 0:
                            dve.tensor_copy(t[:, s, T_X:T_X + 512], pt[q % 2][:, :]).then_inc(back_done, 1)
                        else:
                            dve.tensor_copy(t[:, s, T_B:T_B + 384], pt[q % 2][:, 0:384]).then_inc(back_done, 1)
                for s in range(2):
                    dve.wait_ge(ln_done, it * 2 + (s + 1))
                    dve.wait_ge(min_done, it * 4 + 4)
                    dve.scalar_tensor_tensor(out=t[:, s, T_GF:T_GF + 512], in0=soft[s][:, 0:512], scalar=-1 / 16.0,
                                             in1=t[:, s, T_GF:T_GF + 512], op0=ALU.mult, op1=ALU.add)
                    dve.tensor_tensor(t[:, s, T_DT:T_DT + 16], t[:, s, T_DT:T_DT + 16], soft[s][:, 512:528],
                                      ALU.add).then_inc(g_done, 1)
            steps(dve, body)


def direction(C, d):
    return (C["le"], C["gt"], C["le_bd"], C["gt_bd"]) if d == 0 else (C["ge"], C["lt"], C["ge_bd"], C["lt_bd"])


def state_products(pe, C, d, rec, dta, small):
    _, past, _, past_bd = direction(C, d)
    g0 = T_GF + d * GQK
    pe.matmul(small[:, 0:GQK], past_bd[:, :], rec[:, g0:g0 + GQK], start=True, stop=True)
    pe.matmul(small[:, 256:264], past[:, :], dta, start=True, stop=True)
    for g in range(2):
        pe.matmul(small[64 * g:64 * g + 64, 264:268], C["ones"][:, 0:64], dta[:, 4 * g:4 * g + 4], start=True, stop=True)
    for pair in range(2):
        mm = pe.matmul(small[:, 268 + 2 * pair:270 + 2 * pair], rec[:, g0 + P * pair:g0 + P * (pair + 1)],
                       C["halves"][:, :], start=True, stop=True)
    return mm


def scan_states(nc, A, C, tok_rec, d, state_out):
    first, second = (1, 0) if d else (0, 1)
    with ExitStack() as ctx:
        sem = Names(nc, ctx, f"sc{d}")

        def sb(name, shape, dt=F32):
            return ctx.enter_context(nc.sbuf_tensor(f"{name}_s{d}", shape, dt))

        def ps(name, shape):
            return ctx.enter_context(nc.psum_tensor(f"{name}_s{d}", shape, F32))

        rec = [sb(f"rec{b}", [P, T_Z]) for b in range(2)]
        st = [sb(f"st{b}", [P, 3, 256]) for b in range(2)]
        nega = sb("nega", [P, SH])
        dta, wend, xw, kend, ex = sb("dta", [P, SH]), sb("wend", [P, SH]), sb("xw", [P, SW]), sb("kend", [P, GQK]), sb("ex", [P, 272])
        small, p_ssd, p_gla = ps("small", [P, 512]), ps("p_ssd", [P, 512]), [ps(f"p_gla{c}", [P, 2, P]) for c in range(2)]
        pool_held, sp_held = sem("pool_held"), sem("sp_held")
        loaded = [sem("rec0_loaded"), sem("rec1_loaded")]
        saved = [sem("st0_saved"), sem("st1_saved")]
        (a_loaded, a_exp, a_done, zeroed, dta_done, small_ps, ex_done, wend_done, scaled, kend_done,
         states_ps, decayed, mid_done, next_done, rec_free) = (sem(n) for n in (
             "a_loaded", "a_exp", "a_done", "zeroed", "dta_done", "small_product", "exp_done", "wend_done", "x_scaled",
             "kend_done", "state_products", "decayed", "mid_state", "next_state", "rec_free"))
        block = ctx.enter_context(nc.Block())
        a_d = A["a_log_b" if d else "a_log_f"]

        def tile(it, is_ctx):
            if is_ctx:
                return (1 - it) if d else it
            return (TILES + 1) - it

        def steps(eng, body):
            body(0, 0, 0, True)
            body(1, 0, 1, True)
            if d:
                with eng.Fori(0, LT // 2) as r:
                    body(r * 2 + 2, r + 1, 0, False)
                    body(r * 2 + 3, r + 1, 1, False)

        @block.sync
        def _(sp):
            sp.dma_start(nega[:, :], a_d.to_broadcast([P, SH])).then_inc(a_loaded, 16)

            def body(it, use, buf, is_ctx):
                if not is_ctx:
                    hold(sp, rec_free, it - 1, sp_held)
                sp.dma_start(rec[buf][:, :], tok_rec[tile(it, is_ctx)][:, 0:T_Z]).then_inc(loaded[buf], 16)
            steps(sp, body)

        @block.gpsimd
        def _(pool):
            if d:
                with pool.Fori(0, LT // 2) as r:
                    for b in range(2):
                        hold(pool, mid_done, r * 2 + (3 + b), pool_held)
                        pool.dma_start(state_out[TILES - 1 - b - r * 2],
                                       st[b][:, :, :].rearrange("p a b -> p (a b)")).then_inc(saved[b], 16)
                for b in range(2):
                    pool.wait_ge(saved[b], 16 * (LT // 2))
            else:
                pool.wait_ge(next_done, 2)
                pool.dma_start(state_out[0], st[0][:, :, :].rearrange("p a b -> p (a b)")).then_inc(saved[0], 16)
                pool.wait_ge(saved[0], 16)

        @block.scalar
        def _(act):
            act.wait_ge(a_loaded, 16)
            act.activation(nega[:, :], nega[:, :], ACT.Exp).then_inc(a_exp, 1)

            def body(it, use, buf, is_ctx):
                act.wait_ge(small_ps, it + 1)
                if not is_ctx or it:
                    act.wait_ge(kend_done, it)
                    act.wait_ge(next_done, it)
                act.activation(ex[:, :], small[:, 0:272], ACT.Exp).then_inc(ex_done, 1)
            steps(act, body)

        @block.tensor
        def _(pe):
            def body(it, use, buf, is_ctx):
                pe.wait_ge(dta_done, it + 1)
                if not is_ctx or it:
                    pe.wait_ge(ex_done, it)
                state_products(pe, C, d, rec[buf], dta[:, :], small).then_inc(small_ps, 1)
                pe.wait_ge(scaled, it + 1)
                pe.wait_ge(kend_done, it + 1)
                if not is_ctx or it:
                    pe.wait_ge(next_done, it)
                state_matmuls(pe, rec[buf], xw, kend, p_ssd, p_gla).then_inc(states_ps, 1)
            steps(pe, body)

        @block.vector
        def _(dve):
            dve.memset(st[0][:, :, :], 0.0).then_inc(zeroed, 1)
            dve.memset(st[1][:, :, :], 0.0).then_inc(zeroed, 1)
            dve.wait_ge(a_exp, 1)
            dve.tensor_scalar(nega[:, :], nega[:, :], -1.0, None, ALU.mult).then_inc(a_done, 1)
            dve.wait_ge(a_done, 1)
            dve.wait_ge(zeroed, 2)

            def body(it, use, buf, is_ctx):
                dt = rec[buf][:, T_DT + SH * d:T_DT + SH * (d + 1)]
                dve.wait_ge(loaded[buf], use * 16 + 16)
                dve.tensor_tensor(dta[:, :], dt, nega[:, :], ALU.mult).then_inc(dta_done, 1)
                dve.wait_ge(ex_done, it + 1)
                dve.tensor_tensor(wend[:, :], ex[:, 256:264], dt, ALU.mult).then_inc(wend_done, 1)
                dve.tensor_tensor(kend[:, :], rec[buf][:, T_K:T_K + GQK], ex[:, 0:256], ALU.mult).then_inc(kend_done, 1)
                dve.wait_ge(wend_done, it + 1)
                dve.tensor_tensor(xw[:, :].rearrange("p (h c) -> p h c", h=SH),
                                  rec[buf][:, 0:SW].rearrange("p (h c) -> p h c", h=SH),
                                  wend[:, :].unsqueeze(2).to_broadcast([P, SH, SP_]), ALU.mult).then_inc(scaled, 1)
                dve.wait_ge(states_ps, it + 1)
                if not is_ctx and buf == 1:
                    dve.wait_ge(saved[0], use * 16)
                update_states(dve, it, ex, p_ssd, p_gla, st[buf], st[1 - buf], first, second, decayed, mid_done, next_done)
                dve.sem_inc(rec_free, 1)

            if not d:
                steps(dve, body)
            else:
                body(0, 0, 0, True)
                body(1, 0, 1, True)
                body(2, 1, 0, False)
                body(3, 1, 1, False)
                with dve.Fori(1, LT // 2) as r:
                    dve.wait_ge(saved[1], r * 16)
                    body(r * 2 + 2, r + 1, 0, False)
                    body(r * 2 + 3, r + 1, 1, False)


def state_matmuls(pe, rec, xw, kend, p_ssd, p_gla):
    for g in range(2):
        pe.matmul(p_ssd[64 * g:64 * g + 64, 0:256], rec[:, T_B + 64 * g:T_B + 64 * g + 64],
                  xw[:, 256 * g:256 * g + 256], start=True, stop=True)
    for c in range(2):
        for h in range(GH):
            mm = pe.matmul(p_gla[c][64 * (h % 2):64 * (h % 2) + 64, h // 2, :], kend[64 * c:64 * c + 64, 64 * h:64 * h + 64],
                           rec[64 * c:64 * c + 64, T_V + GV * h:T_V + GV * (h + 1)], start=True, stop=True)
    return mm


def update_states(dve, it, ex, p_ssd, p_gla, now, nxt, first, second, decayed, mid_done, next_done):
    for pair in range(2):
        i = dve.scalar_tensor_tensor(out=now[:, 1 + second, P * pair:P * (pair + 1)],
                                     in0=now[:, 1 + first, P * pair:P * (pair + 1)],
                                     scalar=ex[:, 268 + 2 * pair + first:269 + 2 * pair + first],
                                     in1=p_gla[first][:, pair, :], op0=ALU.mult, op1=ALU.add)
    i.then_inc(mid_done, 1)
    h = now[:, 0, :].rearrange("p (h c) -> p h c", h=4)
    n = nxt[:, 0, :].rearrange("p (h c) -> p h c", h=4)
    dve.tensor_tensor(n, h, ex[:, 264:268].unsqueeze(2).to_broadcast([P, 4, SP_]), ALU.mult).then_inc(decayed, 1)
    dve.wait_ge(mid_done, it + 1)
    for pair in range(2):
        dve.scalar_tensor_tensor(out=nxt[:, 1 + first, P * pair:P * (pair + 1)],
                                 in0=now[:, 1 + second, P * pair:P * (pair + 1)],
                                 scalar=ex[:, 268 + 2 * pair + second:269 + 2 * pair + second],
                                 in1=p_gla[second][:, pair, :], op0=ALU.mult, op1=ALU.add)
    dve.wait_ge(decayed, it + 1)
    dve.tensor_tensor(nxt[:, 0, :], nxt[:, 0, :], p_ssd[:, 0:256], ALU.add).then_inc(next_done, 1)


class Step:

    def __init__(self, it, use, buf, later, reused):
        self.it, self.use, self.buf, self.later, self.reused = it, use, buf, later, reused


def pipeline(eng, front, proj, output, tail):
    def at(n):
        return Step(n, n // 2, n % 2, n >= 1, n >= 2)

    front(at(0))
    output(at(0))
    front(at(1))
    proj(at(0))
    output(at(1))
    tail(at(0))
    with eng.Fori(0, LT // 2 - 1) as r:
        for u in range(2):
            now = Step(r * 2 + (2 + u), r + 1, u, True, True)
            before = Step(r * 2 + (1 + u), r + u, 1 - u, True, True)
            front(now)
            proj(before)
            output(now)
            tail(before)
    proj(at(LT - 1))
    tail(at(LT - 1))


def mixer(nc, A, C, route, tok_rec, feat_rec, back_state, fwd_state, x_mid, x_hat):
    mod, ident = C["mod"], C["ident"]
    FRONT = ["v", "v", "v", "v", "v", "v", "a", "v", "v", "v", "v", "v", "v", "v"]
    TAIL = ["a", "a", "v", "v", "a", "a", "v"]
    R_SC, R_BC, R_BT, R_AT, R_PI, R_PS, R_PG = 0, 2, 6, 7, 9, 11, 12
    R_MT, R_OP, R_XT, R_RT = 0, 2, 4, 6
    x_t = A["x"].rearrange("b (t p) d -> (b t) p d", p=P)
    xh_t = x_hat.rearrange("(t p) d -> t p d", p=P)
    with ExitStack() as ctx:
        sem = Names(nc, ctx, "mix")

        def sb(name, shape, dt=F32):
            return ctx.enter_context(nc.sbuf_tensor(f"{name}_m", shape, dt))

        def ps(name, shape):
            return ctx.enter_context(nc.psum_tensor(f"{name}_m", shape, F32))

        rec = [sb(f"rec{b}", [P, T_LEN]) for b in range(2)]
        feat = [sb(f"feat{b}", [P, F_TILES, P]) for b in range(2)]
        bst = [sb(f"bst{b}", [P, 3, 256]) for b in range(2)]
        xres = [sb(f"xres{b}", [P, D]) for b in range(2)]
        st = [sb(f"st{b}", [P, 3, 256]) for b in range(2)]
        w_out, w_rt = sb("w_out", [P, KT, D]), sb("w_rt", [P, KT, NE])
        gate_bc = sb("gate_bc", [P, D])
        nega, skip = sb("nega", [P, 2 * SH]), sb("skip", [P, SH])
        inv, mhalf = sb("inv", [P, 8]), sb("mhalf", [P, 8])
        dta, ex, a_sb = sb("dta", [P, 2 * SH]), sb("ex", [P, 288]), sb("a_sb", [P, 2 * SH])
        scm = sb("scm", [P, 2, 2, P])
        seg = [sb(f"seg{b}", [P, 4, P]) for b in range(2)]
        M = [sb(f"M{n}", [P, 4, P]) for n in range(4)]
        xd, xw, xD = sb("xd", [P, 2, SW]), sb("xw", [P, SW]), sb("xD", [P, SW])
        wend, kend = sb("wend", [P, SH]), sb("kend", [P, GQK])
        eb, enb, qd, ki = (sb(n, [P, 4, P]) for n in ("eb", "enb", "qd", "ki"))
        am = [sb(f"am{b}", [P, 4, P]) for b in range(2)]
        yi, y, junk = sb("yi", [P, 2, SW]), sb("y", [P, SW]), sb("junk", [P, D])
        m, mT = sb("m", [P, D]), sb("mT", [P, KT, P])
        x1 = [sb(f"x1{b}", [P, D]) for b in range(2)]
        xh = [sb(f"xh{b}", [P, D]) for b in range(2)]
        h2T = sb("h2T", [P, KT, P])
        ssm, ssx, rsx = sb("ssm", [P, 8]), sb("ssx", [P, 1]), sb("rsx", [P, 1])
        small, py = ps("small", [P, 512]), ps("py", [P, 512])
        po = [ps(f"po{b}", [P, 2, P]) for b in range(2)]
        fr = [ps(f"fr{b}", [P, 512]) for b in range(2)]
        tr = [ps(f"tr{b}", [P, 512]) for b in range(2)]

        rec_loaded, x_loaded = [sem(f"rec{b}_loaded") for b in range(2)], [sem(f"x{b}_loaded") for b in range(2)]
        x1_stored, xh_stored = [sem(f"x1{b}_stored") for b in range(2)], [sem(f"xh{b}_stored") for b in range(2)]
        (setup, a_exp, setup_done, gate_ps, gate_done, setup_pool, dta_done, small_ps, ex_done, a_copied, scm_done, seg_done,
         seg_exp, m_ready, eb_done, qk_done, xd_done, wend_done, xw_done, kend_done, xD_done, am_done, pi_done,
         decayed, mid_done, next_done, y_ps, o_ps, ysum1, ysum_done, y_raw, y_gated, sq_done, r_step, r_done, m_step, mix_done,
         xg_done, xadd_done, sx_done, rx_step, rx_done, xh_done, h2_done, log_done) = (sem(n) for n in (
             "setup", "a_exp", "setup_done", "gate_spread", "gate_done", "setup_pool", "dta_done", "small_product", "exp_done",
             "a_copied", "masked_scores", "seg_done", "seg_exp", "decayed_scores", "eb_done", "qk_decayed", "xd_done", "wend_done",
             "xw_done", "kend_done", "x_skip", "attn_masked", "inter_scaled", "decayed", "mid_state", "next_state", "y_product",
             "o_product", "y_sum1", "y_sum", "y_raw", "y_gated", "squares", "r_step", "r_done", "m_step", "mix_done", "x_gated",
             "x_added", "x_square", "rx_step", "rx_done", "xh_done", "h2T_done", "logits_done"))
        pool_held = sem("pool_held")
        pe_held = sem("pe_held")
        x_buf_free = sem("x_buffer_free")
        f_ps, t_ps = sem("front_product"), sem("tail_product")
        f_v, f_a, t_v, t_a = sem("front_freed_v"), sem("front_freed_a"), sem("tail_freed_v"), sem("tail_freed_a")
        block = ctx.enter_context(nc.Block())

        def count(rounds, n, who, it):
            return it * rounds.count(who) + rounds[:n + 1].count(who)

        def bank_free(pe, rounds, n, s, by_v, by_a):
            last = n - 2 if n >= 2 else max(i for i in range(len(rounds)) if i % 2 == n % 2)
            if n < 2 and not s.later:
                return
            it = s.it if n >= 2 else s.it - 1
            who = rounds[last]
            hold(pe, by_v if who == "v" else by_a, count(rounds, last, who, it), pe_held)

        @block.sync
        def _(sp):
            for k in range(KT):
                sp.dma_start(w_out[:, k, :], A["w_out"][0, k * P:(k + 1) * P, :]).then_inc(setup, 16)
            sp.dma_start(w_rt[:, :, :], A["w_router"].rearrange("(k p) e -> p k e", p=P)).then_inc(setup, 16)
            sp.dma_start(nega[:, 0:SH], A["a_log_f"].to_broadcast([P, SH])).then_inc(setup, 16)
            sp.dma_start(nega[:, SH:], A["a_log_b"].to_broadcast([P, SH])).then_inc(setup, 16)
            sp.dma_start(skip[:, :], A["d_skip"].to_broadcast([P, SH])).then_inc(setup, 16)
            sp.dma_start(st[0][:, :, :].rearrange("p a b -> p (a b)"), fwd_state[0]).then_inc(setup, 16)
            def front(s):
                if s.reused:
                    sp.wait_ge(mix_done, s.it - 1)
                sp.dma_start(rec[s.buf][:, :], tok_rec[s.it + CT]).then_inc(rec_loaded[s.buf], 16)
                sp.dma_start(feat[s.buf][:, :, :].rearrange("p a b -> p (a b)"), feat_rec[s.it + CT]).then_inc(rec_loaded[s.buf], 16)
                sp.dma_start(bst[s.buf][:, :, :].rearrange("p a b -> p (a b)"), back_state[s.it + CT]).then_inc(rec_loaded[s.buf], 16)
                if s.reused:
                    sp.wait_ge(xadd_done, s.it - 1)
                sp.dma_start(xres[s.buf][:, :], x_t[s.it]).then_inc(x_loaded[s.buf], 16)

            def none(s):
                pass

            pipeline(sp, front, none, none, none)

        @block.gpsimd
        def _(pool):
            pool.sem_inc(x_buf_free, 1)
            pool.memset(mhalf[:, :], -0.5).then_inc(setup_pool, 1)
            pool.memset(inv[:, 0:4], 1.0 / GV).then_inc(setup_pool, 1)
            pool.memset(inv[:, 4:8], 1.0 / SW).then_inc(setup_pool, 1)
            pool.memset(ssm[:, :], 1.0).then_inc(setup_pool, 1)
            pool.wait_ge(setup_pool, 4)
            pool.wait_ge(setup, 16 * (KT + 5))

            def spread(out, x, by):
                return pool.tensor_tensor(out.rearrange("p (h c) -> p h c", h=SH), x.rearrange("p (h c) -> p h c", h=SH),
                                          by.unsqueeze(2).to_broadcast([P, SH, SP_]), ALU.mult)

            def front(s):
                r, it = rec[s.buf], s.it
                pool.wait_ge(rec_loaded[s.buf], s.use * 48 + 48)
                if s.later:
                    pool.wait_ge(y_ps, it)
                for d in range(2):
                    spread(xd[:, d, :], r[:, 0:SW], r[:, T_DT + SH * d:T_DT + SH * (d + 1)]).then_inc(xd_done, 1)
                spread(xD[:, :], r[:, 0:SW], skip[:, :]).then_inc(xD_done, 1)
                pool.wait_ge(ex_done, it + 1)
                pool.tensor_tensor(wend[:, :], ex[:, 256:264], r[:, T_DT:T_DT + SH], ALU.mult).then_inc(wend_done, 1)
                pool.tensor_tensor(kend[:, :], r[:, T_K:T_K + GQK], ex[:, 0:256], ALU.mult).then_inc(kend_done, 1)
                pool.wait_ge(wend_done, it + 1)
                spread(xw[:, :], r[:, 0:SW], wend[:, :]).then_inc(xw_done, 1)

            def proj(s):
                it = s.it
                pool.wait_ge(xg_done, it * 2 + 2)
                pool.wait_ge(x_loaded[s.buf], s.use * 16 + 16)
                pool.tensor_tensor(x1[s.buf][:, :], x1[s.buf][:, :], xres[s.buf][:, :], ALU.add).then_inc(xadd_done, 1)
                pool.wait_ge(sx_done, it + 1)
                if s.later:
                    hold(pool, xh_done, it, pool_held)
                pool.tensor_scalar(rsx[:, :], ssx[:, :], 1.0 / D, EPS, ALU.mult, ALU.add).then_inc(rx_step, 1)
                pool.wait_ge(rx_step, it + 1)
                pool.tensor_tensor(rsx[:, :], rsx[:, :], mhalf[:, 0:1], ALU.pow).then_inc(rx_done, 1)
                if s.later:
                    prior_use = s.use if s.buf == 1 else s.use - 1
                    pool.wait_ge(x1_stored[1 - s.buf], prior_use * 16 + 16)
                    pool.wait_ge(xh_stored[1 - s.buf], prior_use * 16 + 16)
                    pool.sem_inc(x_buf_free, 1)
                pool.dma_start(x_mid[it], x1[s.buf][:, :]).then_inc(x1_stored[s.buf], 16)
                hold(pool, xh_done, it + 1, pool_held)
                pool.dma_start(xh_t[it], xh[s.buf][:, :]).then_inc(xh_stored[s.buf], 16)

            def output(s):
                it = s.it
                pool.wait_ge(pi_done, it * 2 + 2)
                pool.wait_ge(xD_done, it + 1)
                pool.tensor_tensor(yi[:, 0, :], yi[:, 0, :], yi[:, 1, :], ALU.add).then_inc(ysum1, 1)
                pool.wait_ge(ysum1, it + 1)
                pool.tensor_tensor(yi[:, 0, :], yi[:, 0, :], xD[:, :], ALU.add).then_inc(ysum_done, 1)
                pool.wait_ge(sq_done, it * 5 + 5)
                pool.tensor_tensor(ssm[:, :], ssm[:, :], inv[:, :], ALU.mult).then_inc(r_step, 1)
                hold(pool, r_step, it * 2 + 1, pool_held)
                pool.tensor_scalar(ssm[:, :], ssm[:, :], EPS, None, ALU.add).then_inc(r_step, 1)
                pool.wait_ge(r_step, it * 2 + 2)
                pool.tensor_tensor(ssm[:, :], ssm[:, :], mhalf[:, :], ALU.pow).then_inc(r_done, 1)

            def tail(s):
                pass

            pipeline(pool, front, proj, output, tail)
            for b in range(2):
                pool.wait_ge(x1_stored[b], 16 * (LT // 2))
                pool.wait_ge(xh_stored[b], 16 * (LT // 2))

        @block.scalar
        def _(act):
            act.wait_ge(setup, 16 * (KT + 5))
            act.activation(nega[:, :], nega[:, :], ACT.Exp).then_inc(a_exp, 1)

            def front(s):
                it = s.it
                act.wait_ge(small_ps, it + 1)
                if s.later:
                    act.wait_ge(next_done, it)
                act.activation(ex[:, :], small[:, 0:288], ACT.Exp).then_inc(ex_done, 1)
                act.activation(a_sb[:, :], small[:, 272:288], ACT.Copy).then_inc(a_copied, 1)
                for r in range(4):
                    act.wait_ge(seg_done, it * 4 + (r + 1))
                    act.activation(seg[r % 2][:, :, :], seg[r % 2][:, :, :], ACT.Exp).then_inc(seg_exp, 1)
                act.wait_ge(f_ps, it * 14 + (R_BT + 1))
                if s.later:
                    act.wait_ge(qk_done, it * 2)
                act.activation(eb[:, :, :], fr[R_BT % 2][:, :].rearrange("p (a b) -> p a b", a=4), ACT.Exp).then_inc(eb_done, 1)
                act.activation(enb[:, :, :], fr[R_BT % 2][:, :].rearrange("p (a b) -> p a b", a=4), ACT.Exp, scale=-1.0).then_inc(eb_done, 1)
                act.wait_ge(eb_done, it * 2 + 2)
                act.sem_inc(f_a, 1)

            def proj(s):
                it = s.it
                for n in range(2):
                    act.wait_ge(t_ps, it * 7 + (n + 1))
                    for j in range(4):
                        g = R_SG + j if n == 0 else R_GG
                        i = act.activation(mT[:, 4 * n + j, :], tr[n][:, P * j:P * (j + 1)], ACT.Copy,
                                           scale=C["cols"][:, g:g + 1])
                    i.then_inc(t_a, 1)
                act.wait_ge(xadd_done, it + 1)
                if s.later:
                    act.wait_ge(rx_step, it)
                act.activation(junk[:, :], x1[s.buf][:, :], ACT.Square, accum_out=ssx[:, :]).then_inc(sx_done, 1)
                act.wait_ge(rx_done, it + 1)
                if s.later:
                    act.wait_ge(x_buf_free, it)
                act.activation(xh[s.buf][:, :], x1[s.buf][:, :], ACT.Copy, scale=rsx[:, :]).then_inc(xh_done, 1)

            def output(s):
                it = s.it
                act.wait_ge(o_ps, it * 2 + 2)
                if s.later:
                    act.wait_ge(mix_done, it)
                    act.wait_ge(xh_done, it)
                for h in range(GH):
                    if h or s.later:
                        act.wait_ge(sq_done, it * 5 + h)
                    act.activation(junk[:, 0:GV], po[h % 2][:, h // 2, :], ACT.Square, accum_out=ssm[:, h:h + 1]).then_inc(sq_done, 1)
                act.wait_ge(y_gated, it + 1)
                act.wait_ge(sq_done, it * 5 + 4)
                act.activation(junk[:, 0:SW], y[:, :], ACT.Square, accum_out=ssm[:, 4:5]).then_inc(sq_done, 1)

            def tail(s):
                it = s.it
                if s.later:
                    act.wait_ge(log_done, it)
                for n in range(2):
                    act.wait_ge(t_ps, it * 7 + (R_XT + n + 1))
                    for j in range(4):
                        k = 4 * n + j
                        i = act.activation(h2T[:, k, :], tr[n][:, P * j:P * (j + 1)], ACT.Identity,
                                           scale=mod[:, 4 * KT + k, 0:1], bias=mod[:, 3 * KT + k, 0:1])
                    i.then_inc(t_a, 1)

            pipeline(act, front, proj, output, tail)

        @block.tensor
        def _(pe):
            for j in range(KT):
                pe.matmul(tr[j // 4][:, P * (j % 4):P * (j % 4 + 1)], mod[:, 2 * KT + j, 0:1].to_broadcast([P, P]), ident[:, :],
                          start=True, stop=True).then_inc(gate_ps, 1)
            pe.wait_ge(gate_done, 2)
            pe.wait_ge(setup, 16 * (KT + 5))

            def front(s):
                it, r, f = s.it, rec[s.buf], feat[s.buf]
                pe.wait_ge(rec_loaded[s.buf], s.use * 48 + 48)
                pe.wait_ge(dta_done, it + 1)
                if s.later:
                    pe.wait_ge(a_copied, it)
                state_products(pe, C, 0, r, dta[:, 0:SH], small)
                pe.matmul(small[:, 272:280], C["le"][:, :], dta[:, 0:SH], start=True, stop=True)
                pe.matmul(small[:, 280:288], C["ge"][:, :], dta[:, SH:], start=True, stop=True).then_inc(small_ps, 1)
                for g in range(2):
                    bank_free(pe, FRONT, R_SC + g, s, f_v, f_a)
                    pe.matmul(fr[g][:, 0:P], f[64 * g:64 * g + 64, 0, :], f[64 * g:64 * g + 64, 1, :],
                              start=True, stop=True).then_inc(f_ps, 1)
                for d in range(2):
                    for g in range(2):
                        bank_free(pe, FRONT, R_BC + 2 * d + g, s, f_v, f_a)
                        for h in range(4):
                            c = SH * d + 4 * g + h
                            mm = pe.matmul(fr[g][:, P * h:P * (h + 1)], dta[:, c:c + 1].to_broadcast([P, P]),
                                           C["ge" if d else "le"][:, :], start=True, stop=True)
                        mm.then_inc(f_ps, 1)
                bank_free(pe, FRONT, R_BT, s, f_v, f_a)
                for d in range(2):
                    for pair in range(2):
                        c0 = T_GF + GQK * d + P * pair
                        mm = pe.matmul(fr[R_BT % 2][:, P * (2 * d + pair):P * (2 * d + pair + 1)], r[:, c0:c0 + P],
                                       C["ge_bd" if d else "le_bd"][:, :], start=True, stop=True)
                mm.then_inc(f_ps, 1)

            def proj(s):
                it = s.it
                pe.wait_ge(mix_done, it + 1)
                for n in range(2):
                    bank_free(pe, TAIL, R_MT + n, s, t_v, t_a)
                    for j in range(4):
                        mm = pe.transpose(tr[n][:, P * j:P * (j + 1)], m[:, P * (4 * n + j):P * (4 * n + j + 1)], ident[:, :])
                    mm.then_inc(t_ps, 1)
                pe.wait_ge(t_a, it * 4 + 2)
                for n in range(2):
                    for k in range(KT):
                        mm = pe.matmul(tr[n][:, :], mT[:, k, :], w_out[:, k, 512 * n:512 * (n + 1)], start=(k == 0), stop=(k == KT - 1))
                    mm.then_inc(t_ps, 1)

            def output(s):
                it, r, f = s.it, rec[s.buf], feat[s.buf]
                pe.wait_ge(qk_done, it * 2 + 2)
                for hh in range(2):
                    bank_free(pe, FRONT, R_AT + hh, s, f_v, f_a)
                    for dp in range(4):
                        mm = pe.matmul(fr[(R_AT + hh) % 2][:, P * dp:P * (dp + 1)], ki[64 * hh:64 * hh + 64, dp, :],
                                       qd[64 * hh:64 * hh + 64, dp, :], start=True, stop=True)
                    mm.then_inc(f_ps, 1)
                if s.later:
                    pe.wait_ge(next_done, it)
                for g in range(2):
                    bank_free(pe, FRONT, R_PI + g, s, f_v, f_a)
                    for d, h_in in enumerate((st[s.buf], bst[s.buf])):
                        mm = pe.matmul(fr[(R_PI + g) % 2][:, 256 * d:256 * d + 256], f[64 * g:64 * g + 64, 1, :],
                                       h_in[64 * g:64 * g + 64, 0, :], start=True, stop=True)
                    mm.then_inc(f_ps, 1)
                pe.wait_ge(xw_done, it + 1)
                bank_free(pe, FRONT, R_PS, s, f_v, f_a)
                for g in range(2):
                    mm = pe.matmul(fr[R_PS % 2][64 * g:64 * g + 64, 0:256], r[:, T_B + 64 * g:T_B + 64 * g + 64],
                                   xw[:, 256 * g:256 * g + 256], start=True, stop=True)
                mm.then_inc(f_ps, 1)
                pe.wait_ge(kend_done, it + 1)
                for c in range(2):
                    bank_free(pe, FRONT, R_PG + c, s, f_v, f_a)
                    for h in range(GH):
                        mm = pe.matmul(fr[(R_PG + c) % 2][64 * (h % 2):64 * (h % 2) + 64, P * (h // 2):P * (h // 2 + 1)],
                                       kend[64 * c:64 * c + 64, 64 * h:64 * h + 64],
                                       r[64 * c:64 * c + 64, T_V + GV * h:T_V + GV * (h + 1)], start=True, stop=True)
                    mm.then_inc(f_ps, 1)
                pe.wait_ge(m_ready, it * 4 + 4)
                pe.wait_ge(xd_done, it * 2 + 2)
                if s.later:
                    pe.wait_ge(y_raw, it)
                for h in range(SH):
                    for d in range(2):
                        mm = pe.matmul(py[:, 64 * h:64 * h + 64], M[2 * d + h // 4][:, h % 4, :], xd[:, d, 64 * h:64 * h + 64],
                                       start=(d == 0), stop=(d == 1))
                mm.then_inc(y_ps, 1)
                pe.wait_ge(am_done, it * 2 + 2)
                pe.wait_ge(mid_done, it + 1)
                if s.later:
                    pe.wait_ge(mix_done, it)
                for hh in range(2):
                    for pair in range(2):
                        h = 2 * pair + hh
                        for d in range(2):
                            pe.matmul(po[hh][:, pair, :], am[hh][:, 2 * d + pair, :], r[:, T_V + GV * h:T_V + GV * (h + 1)],
                                      start=(d == 0), stop=False, skip_group_check=True)
                        for d, s_in in enumerate((st[s.buf], bst[s.buf])):
                            for c in range(2):
                                mm = pe.matmul(po[hh][64 * c:64 * c + 64, pair, :],
                                               qd[64 * hh:64 * hh + 64, 2 * d + pair, 64 * c:64 * c + 64],
                                               s_in[64 * hh:64 * hh + 64, 1 + c, P * pair:P * (pair + 1)],
                                               start=False, stop=(d == 1), skip_group_check=True)
                    mm.then_inc(o_ps, 1)

            def tail(s):
                it = s.it
                pe.wait_ge(xh_done, it + 1)
                for n in range(2):
                    bank_free(pe, TAIL, R_XT + n, s, t_v, t_a)
                    for j in range(4):
                        mm = pe.transpose(tr[n][:, P * j:P * (j + 1)], xh[s.buf][:, P * (4 * n + j):P * (4 * n + j + 1)], ident[:, :])
                    mm.then_inc(t_ps, 1)
                pe.wait_ge(t_a, it * 4 + 4)
                for k in range(KT):
                    mm = pe.matmul(tr[R_RT % 2][:, 0:NE], h2T[:, k, :], w_rt[:, k, :], start=(k == 0), stop=(k == KT - 1))
                mm.then_inc(t_ps, 1)

            pipeline(pe, front, proj, output, tail)

        @block.vector
        def _(dve):
            dve.wait_ge(a_exp, 1)
            dve.tensor_scalar(nega[:, :], nega[:, :], -1.0, None, ALU.mult).then_inc(setup_done, 1)
            for n in range(2):
                dve.wait_ge(gate_ps, KT)
                dve.tensor_copy(gate_bc[:, 512 * n:512 * n + 512], tr[n][:, :]).then_inc(gate_done, 1)
            dve.wait_ge(setup_done, 1)
            dve.wait_ge(gate_done, 2)
            dve.wait_ge(setup_pool, 4)
            incl = C["incl"]
            incl_bd = C["incl_bd"]

            def front(s):
                it, r = s.it, rec[s.buf]
                dve.wait_ge(rec_loaded[s.buf], s.use * 48 + 48)
                dve.tensor_tensor(dta[:, :], r[:, T_DT:T_DT + 2 * SH], nega[:, :], ALU.mult).then_inc(dta_done, 1)
                for g in range(2):
                    dve.wait_ge(f_ps, it * 14 + (R_SC + g + 1))
                    dve.tensor_tensor(scm[:, :, g, :], fr[g][:, 0:P].unsqueeze(1).to_broadcast([P, 2, P]), incl[:, :, :],
                                      ALU.mult).then_inc(f_v, 1)

                def segment(n):
                    d, g = n // 2, n % 2
                    dve.wait_ge(f_ps, it * 14 + (R_BC + n + 1))
                    if n == 0:
                        dve.wait_ge(a_copied, it + 1)
                    if n >= 2:
                        dve.wait_ge(m_ready, it * 4 + (n - 1))
                    for h in range(4):
                        c = SH * d + 4 * g + h
                        i = dve.tensor_scalar(seg[n % 2][:, h, :], fr[g][:, P * h:P * (h + 1)], a_sb[:, c:c + 1], 0.0,
                                              ALU.subtract, ALU.min)
                    i.then_inc(seg_done, 1)
                    dve.wait_ge(seg_done, it * 4 + (n + 1))
                    dve.sem_inc(f_v, 1)

                def decay(n):
                    d, g = n // 2, n % 2
                    dve.wait_ge(seg_exp, it * 4 + (n + 1))
                    if n == 0:
                        dve.wait_ge(f_v, it * 13 + 2)
                    dve.tensor_tensor(M[n][:, :, :], seg[n % 2][:, :, :], scm[:, d, g, :].unsqueeze(1).to_broadcast([P, 4, P]),
                                      ALU.mult).then_inc(m_ready, 1)
                segment(0)
                segment(1)
                decay(0)
                segment(2)
                decay(1)
                segment(3)
                decay(2)
                decay(3)
                f = feat[s.buf]
                dve.wait_ge(eb_done, it * 2 + 2)
                for dst, e, lo in ((qd, eb, 2), (ki, enb, 4)):
                    src = f[:, lo:lo + 2, :].rearrange("p a b -> p (a b)").unsqueeze(1).to_broadcast([P, 2, 2 * P])
                    dve.tensor_tensor(dst[:, :, :].rearrange("p (d a) b -> p d (a b)", d=2), src,
                                      e[:, :, :].rearrange("p (d a) b -> p d (a b)", d=2), ALU.mult).then_inc(qk_done, 1)

            def proj(s):
                it = s.it
                if s.later:
                    dve.wait_ge(x_buf_free, it)
                for n in range(2):
                    dve.wait_ge(t_ps, it * 7 + (R_OP + n + 1))
                    dve.tensor_tensor(x1[s.buf][:, 512 * n:512 * n + 512], tr[n][:, :], gate_bc[:, 512 * n:512 * n + 512],
                                      ALU.mult).then_inc(xg_done, 1)
                    dve.wait_ge(xg_done, it * 2 + (n + 1))
                    dve.sem_inc(t_v, 1)

            def output(s):
                it, r = s.it, rec[s.buf]
                for hh in range(2):
                    dve.wait_ge(f_ps, it * 14 + (R_AT + hh + 1))
                    mask = incl_bd[:, :, :].unsqueeze(2).to_broadcast([P, 2, 2, P])
                    dve.tensor_tensor(am[hh][:, :, :].rearrange("p (d a) b -> p d a b", d=2),
                                      fr[(R_AT + hh) % 2][:, :].rearrange("p (d a b) -> p d a b", d=2, a=2), mask,
                                      ALU.mult).then_inc(am_done, 1)
                    dve.wait_ge(am_done, it * 2 + (hh + 1))
                    dve.sem_inc(f_v, 1)
                for g in range(2):
                    dve.wait_ge(f_ps, it * 14 + (R_PI + g + 1))
                    ea = ex[:, 272:288].rearrange("p (d h) -> p d h", d=2)[:, :, 4 * g:4 * g + 4].unsqueeze(3).to_broadcast([P, 2, 4, SP_])
                    dve.tensor_tensor(yi[:, :, 256 * g:256 * g + 256].rearrange("p d (h c) -> p d h c", h=4),
                                      fr[(R_PI + g) % 2][:, :].rearrange("p (d h c) -> p d h c", d=2, h=4), ea,
                                      ALU.mult).then_inc(pi_done, 1)
                    dve.wait_ge(pi_done, it * 2 + (g + 1))
                    dve.sem_inc(f_v, 1)
                now, nxt = st[s.buf], st[1 - s.buf]
                dve.tensor_tensor(nxt[:, 0, :].rearrange("p (h c) -> p h c", h=4), now[:, 0, :].rearrange("p (h c) -> p h c", h=4),
                                  ex[:, 264:268].unsqueeze(2).to_broadcast([P, 4, SP_]), ALU.mult).then_inc(decayed, 1)
                dve.wait_ge(f_ps, it * 14 + (R_PS + 1))
                dve.wait_ge(decayed, it + 1)
                dve.tensor_tensor(nxt[:, 0, :], nxt[:, 0, :], fr[R_PS % 2][:, 0:256], ALU.add).then_inc(f_v, 1)
                for c in range(2):
                    dve.wait_ge(f_ps, it * 14 + (R_PG + c + 1))
                    if c:
                        dve.wait_ge(mid_done, it + 1)
                    to = now[:, 2, :] if c == 0 else nxt[:, 1, :]
                    for pair in range(2):
                        cs = slice(P * pair, P * (pair + 1))
                        i = dve.scalar_tensor_tensor(out=to[:, cs], in0=now[:, 1 + c, cs],
                                                     scalar=ex[:, 268 + 2 * pair + c:269 + 2 * pair + c],
                                                     in1=fr[(R_PG + c) % 2][:, cs], op0=ALU.mult, op1=ALU.add)
                    i.then_inc(next_done if c else mid_done, 1)
                    dve.wait_ge(next_done if c else mid_done, it + 1)
                    dve.sem_inc(f_v, 1)
                dve.wait_ge(y_ps, it + 1)
                dve.wait_ge(ysum_done, it + 1)
                dve.tensor_tensor(y[:, :], py[:, :], yi[:, 0, :], ALU.add).then_inc(y_raw, 1)
                dve.wait_ge(y_raw, it + 1)
                dve.tensor_tensor(y[:, :], y[:, :], r[:, T_Z:T_Z + SW], ALU.mult).then_inc(y_gated, 1)
                dve.wait_ge(r_done, it + 1)
                dve.tensor_scalar(m[:, 0:SW], y[:, :], ssm[:, 4:5], None, ALU.mult)
                for hh in range(2):
                    mo = m[:, SW:D].rearrange("p (a b c) -> p a b c", a=2, b=2)[:, :, hh, :]
                    rs = ssm[:, 0:4].rearrange("p (a b) -> p a b", b=2)[:, :, hh:hh + 1].to_broadcast([P, 2, P])
                    dve.tensor_tensor(mo, po[hh][:, :, :], rs, ALU.mult).then_inc(m_step, 1)
                dve.wait_ge(m_step, it * 2 + 2)
                dve.tensor_tensor(m[:, SW:D], m[:, SW:D], r[:, T_GO:T_GO + GW], ALU.mult).then_inc(mix_done, 1)

            def tail(s):
                dve.wait_ge(t_ps, s.it * 7 + (R_RT + 1))
                dve.tensor_copy(route["logits"][:, bass.ds(s.it, 1), :], tr[R_RT % 2][:, 0:NE].unsqueeze(1)).then_inc(log_done, 1)
                dve.wait_ge(log_done, s.it + 1)
                dve.sem_inc(t_v, 1)

            pipeline(dve, front, proj, output, tail)


PL_PAR, PL_HALF, PL_UP, PL_END, PL_PAIRS = 0, MAXB, 2 * MAXB, 3 * MAXB, 3 * MAXB + NE
PL_LEN = PL_PAIRS + 1
TAB = MAXB + 2


def slots(nc, A, C, route, slot_tok):
    logits, plan = route["logits"], route["plan"]
    with ExitStack() as ctx:
        sem = Names(nc, ctx, "slt")

        def sb(name, shape, dt=F32):
            return ctx.enter_context(nc.sbuf_tensor(f"{name}_r", shape, dt))

        def ps(name, shape):
            return ctx.enter_context(nc.psum_tensor(f"{name}_r", shape, F32))

        s, sel, selm, eq = (sb(n, [P, LT, NE]) for n in ("sig", "sel", "selm", "eq"))
        hot = [sb(f"hot{j}", [P, LT, NE]) for j in range(2)]
        both, base = sb("both", [P, LT, NE]), sb("base", [P, LT, NE])
        bias = sb("bias", [P, NE])
        hi, lo = sb("hi", [P, LT * NG, 2]), sb("lo", [P, LT * NG, 2])
        gscore, geq, goff = (sb(n, [P, LT, NG]) for n in ("gscore", "geq", "goff"))
        t1, t2 = sb("t1", [P, LT * NG]), sb("t2", [P, LT * NG])
        down_g, down_e = sb("down_g", [P, NG]), sb("down_e", [P, NE])
        best = sb("best", [P, LT])
        wsum = sb("wsum", [P, LT])
        prior = sb("prior", [P, LT + 1, NE])
        limits = sb("limits", [P, 16])
        over = sb("over", [P, NE, 16])
        nblk, bend, bstart = sb("nblk", [P, NE]), sb("bend", [P, NE]), sb("bstart", [P, NE])
        diag, ncol, lec = sb("diag", [NE, NE]), sb("ncol", [NE, 1]), sb("lec", [NE, NE])
        past = sb("past", [1, MAXB, NE])
        eb = sb("eb", [1, MAXB])
        ei, ei1 = sb("ei", [1, MAXB], I32), sb("ei1", [1, MAXB], I32)
        bnum = sb("bnum", [1, MAXB])
        npf = sb("npf", [1, MAXB // 2])
        slot_f = sb("slot_f", [P, LT, 2])
        zero_i = sb("zero_i", [P, TAB * 16], I32)
        tok_id = sb("tok_id", [P, LT, 16], I32)
        excl, tot, pb = ps("excl", [P, LT, NE]), ps("tot", [P, LT, NE]), ps("pb", [P, 512])
        bias_loaded, made, sig_done, both_done, ranks_ps, lec_done, bend_ps, slot_done, cleared, scattered, chain = (
            sem(n) for n in ("bias_loaded", "made", "sigmoid_done", "both_done", "ranks_product", "lec_done", "bend_product",
                             "slots_done", "table_cleared", "scattered", "chain"))
        block = ctx.enter_context(nc.Block())

        @block.sync
        def _(sp):
            sp.dma_start(bias[:, :], A["router_bias"].rearrange("(a e) -> a e", a=1).to_broadcast([P, NE])).then_inc(bias_loaded, 16)

        @block.scalar
        def _(act):
            act.activation(s[:, :, :], logits[:, :, :], ACT.Sigmoid).then_inc(sig_done, 1)

        @block.tensor
        def _(pe):
            pe.wait_ge(both_done, 1)
            pe.matmul(excl[:, :, :], C["lt"][:, :], both[:, :, :], start=True, stop=True)
            pe.matmul(tot[:, :, :], C["ones"][:, :], both[:, :, :], start=True, stop=True).then_inc(ranks_ps, 1)
            pe.wait_ge(lec_done, 1)
            pe.matmul(pb[:, 0:NE], C["ones"][0:NE, :], lec[:, :], start=True, stop=True).then_inc(bend_ps, 1)

        @block.gpsimd
        def _(pool):
            pool.iota(down_g[:, :], pattern=[[-1, NG]], base=NG, channel_multiplier=0,
                      allow_small_or_imprecise_dtypes=True).then_inc(made, 1)
            pool.iota(down_e[:, :], pattern=[[-1, NE]], base=NE, channel_multiplier=0,
                      allow_small_or_imprecise_dtypes=True).then_inc(made, 1)
            pool.iota(limits[:, :], pattern=[[P, 16]], base=0, channel_multiplier=0,
                      allow_small_or_imprecise_dtypes=True).then_inc(made, 1)
            pool.iota(bnum[:, :], pattern=[[1, MAXB]], base=0, channel_multiplier=0,
                      allow_small_or_imprecise_dtypes=True).then_inc(made, 1)
            pool.iota(tok_id[:, :, :], pattern=[[P, LT], [0, 16]], base=0, channel_multiplier=1).then_inc(made, 1)
            pool.memset(zero_i[:, :], 0).then_inc(made, 1)
            pool.wait_ge(made, 6)
            pool.dma_start(slot_tok.rearrange("(b p) c -> p b c", p=P), zero_i[:, :].rearrange("p (b c) -> p b c", c=16)).then_inc(cleared, 16)
            pool.wait_ge(cleared, 16)
            pool.wait_ge(slot_done, 1)
            for t in range(LT):
                for j in range(2):
                    pool.indirect_dma_start(out=slot_tok, out_offset=bass.IndirectOffsetOnAxis(ap=route["slot"][:, t, j:j + 1], axis=0),
                                            in_=tok_id[:, t, :], in_offset=None).then_inc(scattered, 16)
            pool.wait_ge(scattered, 16 * 2 * LT)

        @block.vector
        def _(dve):
            done = [0]

            def then(ins):
                done[0] += 1
                ins.then_inc(chain, 1)
                dve.wait_ge(chain, done[0])

            def over_e(x):
                return x.unsqueeze(2).to_broadcast([P, LT, NE])

            dve.wait_ge(made, 6)
            dve.wait_ge(bias_loaded, 16)
            dve.wait_ge(sig_done, 1)
            then(dve.tensor_tensor(sel[:, :, :], s[:, :, :], bias[:, :].unsqueeze(1).to_broadcast([P, LT, NE]), ALU.add))
            g4 = sel[:, :, :].rearrange("p t (g e) -> p (t g) e", e=EG)
            then(dve.tensor_tensor(hi[:, :, :], g4[:, :, 0:2], g4[:, :, 2:4], ALU.max))
            then(dve.tensor_tensor(lo[:, :, :], g4[:, :, 0:2], g4[:, :, 2:4], ALU.min))
            then(dve.tensor_tensor(t1[:, :], hi[:, :, 0], hi[:, :, 1], ALU.min))
            then(dve.tensor_tensor(t2[:, :], lo[:, :, 0], lo[:, :, 1], ALU.max))
            then(dve.tensor_tensor(t1[:, :], t1[:, :], t2[:, :], ALU.max))
            then(dve.tensor_tensor(t2[:, :], hi[:, :, 0], hi[:, :, 1], ALU.max))
            gs = gscore[:, :, :].rearrange("p t g -> p (t g)")
            then(dve.tensor_tensor(gs, t1[:, :], t2[:, :], ALU.add))
            then(dve.tensor_reduce(best[:, :], gscore[:, :, :], AX, ALU.max))
            bg = best[:, :].unsqueeze(2).to_broadcast([P, LT, NG])
            then(dve.tensor_tensor(geq[:, :, :], gscore[:, :, :], bg, ALU.is_equal))
            then(dve.tensor_tensor(geq[:, :, :], geq[:, :, :], down_g[:, :].unsqueeze(1).to_broadcast([P, LT, NG]), ALU.mult))
            then(dve.tensor_reduce(best[:, :], geq[:, :, :], AX, ALU.max))
            then(dve.tensor_tensor(geq[:, :, :], geq[:, :, :], bg, ALU.is_equal))
            then(dve.tensor_scalar(goff[:, :, :], geq[:, :, :], -1.0, BIG, ALU.add, ALU.mult))
            in_group = geq[:, :, :].rearrange("p t g -> p (t g)").unsqueeze(2).to_broadcast([P, LT * NG, EG])
            off_group = goff[:, :, :].rearrange("p t g -> p (t g)").unsqueeze(2).to_broadcast([P, LT * NG, EG])
            sm4 = selm[:, :, :].rearrange("p t (g e) -> p (t g) e", e=EG)
            then(dve.tensor_tensor(sm4, g4, in_group, ALU.mult))
            then(dve.tensor_tensor(sm4, sm4, off_group, ALU.add))
            for j in range(2):
                then(dve.tensor_reduce(best[:, :], selm[:, :, :], AX, ALU.max))
                then(dve.tensor_tensor(eq[:, :, :], selm[:, :, :], over_e(best[:, :]), ALU.is_equal))
                then(dve.tensor_tensor(eq[:, :, :], eq[:, :, :], down_e[:, :].unsqueeze(1).to_broadcast([P, LT, NE]), ALU.mult))
                then(dve.tensor_reduce(best[:, :], eq[:, :, :], AX, ALU.max))
                then(dve.tensor_tensor(hot[j][:, :, :], eq[:, :, :], over_e(best[:, :]), ALU.is_equal))
                if j == 0:
                    then(dve.scalar_tensor_tensor(out=selm[:, :, :], in0=hot[0][:, :, :], scalar=-2.0 * BIG, in1=selm[:, :, :],
                                                  op0=ALU.mult, op1=ALU.add))
            dve.tensor_tensor(both[:, :, :], hot[0][:, :, :], hot[1][:, :, :], ALU.add).then_inc(both_done, 1)
            for j in range(2):
                then(dve.tensor_tensor(eq[:, :, :], hot[j][:, :, :], s[:, :, :], ALU.mult))
                then(dve.tensor_reduce(route["gate"][:, :, j], eq[:, :, :], AX, ALU.add))
            then(dve.tensor_tensor(wsum[:, :], route["gate"][:, :, 0], route["gate"][:, :, 1], ALU.add))
            then(dve.reciprocal(wsum[:, :], wsum[:, :]))
            then(dve.tensor_tensor(route["gate"][:, :, :], route["gate"][:, :, :], wsum[:, :].unsqueeze(2).to_broadcast([P, LT, 2]), ALU.mult))
            then(dve.memset(prior[:, 0, :], 0.0))
            dve.wait_ge(ranks_ps, 1)
            for t in range(LT):
                then(dve.tensor_tensor(prior[:, t + 1, :], prior[:, t, :], tot[:, t, :], ALU.add))
            then(dve.tensor_tensor(over[:, :, :], prior[:, LT, :].unsqueeze(2).to_broadcast([P, NE, 16]),
                                   limits[:, :].unsqueeze(1).to_broadcast([P, NE, 16]), ALU.is_gt))
            then(dve.tensor_reduce(nblk[:, :], over[:, :, :], AX, ALU.add))
            then(dve.tensor_tensor(diag[:, :], nblk[0:NE, :], C["ident"][0:NE, 0:NE], ALU.mult))
            then(dve.tensor_reduce(ncol[:, :], diag[:, :], AX, ALU.add))
            dve.tensor_scalar(lec[:, :], C["le"][0:NE, 0:NE], ncol[:, :], None, ALU.mult).then_inc(lec_done, 1)
            dve.wait_ge(bend_ps, 1)
            then(dve.tensor_copy(bend[:, :], pb[:, 0:NE]))
            then(dve.tensor_tensor(bstart[:, :], bend[:, :], nblk[:, :], ALU.subtract))
            then(dve.tensor_scalar(bstart[:, :], bstart[:, :], float(P), None, ALU.mult))
            then(dve.tensor_tensor(base[:, :, :], excl[:, :, :], prior[:, 0:LT, :], ALU.add))
            then(dve.tensor_tensor(base[:, :, :], base[:, :, :], bstart[:, :].unsqueeze(1).to_broadcast([P, LT, NE]), ALU.add))
            for j in range(2):
                then(dve.tensor_tensor(eq[:, :, :], hot[j][:, :, :], base[:, :, :], ALU.mult))
                then(dve.tensor_reduce(slot_f[:, :, j], eq[:, :, :], AX, ALU.add))
            then(dve.tensor_copy(route["slot"][:, :, :], slot_f[:, :, :]))
            dve.sem_inc(slot_done, 1)
            then(dve.tensor_tensor(past[:, :, :], bnum[:, :].unsqueeze(2).to_broadcast([1, MAXB, NE]),
                                   bend[0:1, :].unsqueeze(1).to_broadcast([1, MAXB, NE]), ALU.is_ge))
            then(dve.tensor_reduce(eb[:, :], past[:, :, :], AX, ALU.add))
            then(dve.tensor_scalar(eb[:, :], eb[:, :], float(NE - 1), None, ALU.min))
            then(dve.tensor_copy(ei[:, :], eb[:, :]))
            then(dve.tensor_scalar(eb[:, :], eb[:, :], 1.0, None, ALU.add))
            then(dve.tensor_copy(ei1[:, :], eb[:, :]))
            then(dve.tensor_scalar(plan[:, PL_PAR:PL_PAR + MAXB], ei[:, :], 1, None, ALU.bitwise_and))
            then(dve.tensor_scalar(plan[:, PL_HALF:PL_HALF + MAXB], ei[:, :], 1, None, ALU.arith_shift_right))
            then(dve.tensor_scalar(plan[:, PL_UP:PL_UP + MAXB], ei1[:, :], 1, None, ALU.arith_shift_right))
            then(dve.tensor_copy(plan[:, PL_END:PL_END + NE], bend[0:1, :]))
            then(dve.tensor_tensor(npf[:, :], bnum[:, :].rearrange("p (a b) -> p a b", b=2)[:, :, 0],
                                   bend[0:1, NE - 1:NE].to_broadcast([1, MAXB // 2]), ALU.is_lt))
            then(dve.tensor_reduce(eb[:, 0:1], npf[:, :], AX, ALU.add))
            then(dve.tensor_copy(plan[:, PL_PAIRS:PL_PAIRS + 1], eb[:, 0:1]))


def experts(nc, A, C, route, slot_tok, x_hat, y_slots):
    mod, ident, plan = C["mod"], C["ident"], route["plan"]
    KF = FF // P
    tok_b = slot_tok.rearrange("(b p) c -> b p c", p=P)
    y_b = y_slots.rearrange("(b p) d -> b p d", p=P)
    with ExitStack() as ctx:
        sem = Names(nc, ctx, "exp")

        def sb(name, shape, dt=F32):
            return ctx.enter_context(nc.sbuf_tensor(f"{name}_e", shape, dt))

        def ps(name, shape):
            return ctx.enter_context(nc.psum_tensor(f"{name}_e", shape, F32))

        wg, wu, wd = sb("wg", [P, 2, KT, FF]), sb("wu", [P, 2, KT, FF]), sb("wd", [P, 2, KF, D])
        idx = [sb(f"idx{b}", [P, 16], I32) for b in range(2)]
        xg = [sb(f"xg{b}", [P, D]) for b in range(2)]
        xT = [sb(f"xT{b}", [P, KT, P]) for b in range(2)]
        hs, h, hT = sb("hs", [P, FF]), sb("h", [P, FF]), sb("hT", [P, KF, P])
        yb = [sb(f"yb{b}", [P, D]) for b in range(2)]
        gate_bc, zero = sb("gate_bc", [P, D]), sb("zero", [P, D])
        pool_held = sem("pool_held")
        zero_done = sem("zero_done")
        tx = [ps(f"tx{b}", [P, 512]) for b in range(2)]
        pg, pu, ph = ps("pg", [P, 512]), ps("pu", [P, 512]), ps("ph", [P, 512])
        pd = [ps(f"pd{b}", [P, 512]) for b in range(2)]
        w_loaded = [sem("even_expert_loaded"), sem("odd_expert_loaded")]
        idx_loaded = [sem(f"idx{b}_loaded") for b in range(2)]
        gathered = [sem(f"x{b}_gathered") for b in range(2)]
        stored = [sem(f"y{b}_stored") for b in range(2)]
        (gate_ps, gate_done, xt_ps, xt_done, gp_ps, up_ps, silu_done, h_done, ht_ps, ht_done, dn_ps, y_done,
         y_free) = (sem(n) for n in ("gate_spread", "gate_done", "x_transposed", "xT_done", "gate_product", "up_product",
                                     "silu_done", "h_done", "h_transposed", "hT_done", "down_product", "y_done",
                                     "y_buffer_free"))
        block = ctx.enter_context(nc.Block())
        first = plan[0:1, PL_PAIRS:PL_PAIRS + 1]

        def pairs(eng, body, unused=None):
            n = eng.value_load(first, min_val=1, max_val=MAXB // 2)
            with eng.Fori(0, MAXB // 2) as r:
                with eng.If(r < n):
                    for u in range(2):
                        body(r, u)
                if unused is not None:
                    with eng.Else():
                        for u in range(2):
                            unused(r, u)
            return n

        @block.sync
        def _(sp):
            def load(e, u):
                sp.dma_start(wg[:, u, :, :], A["w_gate"][0][e].rearrange("(k p) f -> p k f", p=P)).then_inc(w_loaded[u], 16)
                sp.dma_start(wu[:, u, :, :], A["w_up"][0][e].rearrange("(k p) f -> p k f", p=P)).then_inc(w_loaded[u], 16)
                sp.dma_start(wd[:, u, :, :], A["w_down"][0][e].rearrange("(k p) f -> p k f", p=P)).then_inc(w_loaded[u], 16)
            sp.sem_inc(w_loaded[1], 48)
            for u in range(2):
                load(u, u)
            with sp.Fori(1, NE // 2) as r:
                for u in range(2):
                    end = sp.value_load(plan[0:1, bass.ds(r * 2 + (PL_END + u - 2), 1)], min_val=0, max_val=MAXB)
                    sp.wait_ge(y_done, end * 2 + 2)
                    load(r * 2 + u, u)

        @block.gpsimd
        def _(pool):
            def fetch(b, use, u):
                pool.dma_start(idx[u][:, :], tok_b[b]).then_inc(idx_loaded[u], 16)
                hold(pool, idx_loaded[u], use * 16 + 16, pool_held)
                pool.indirect_dma_start(out=xg[u][:, :], out_offset=None, in_=x_hat,
                                        in_offset=bass.IndirectOffsetOnAxis(ap=idx[u][:, 0:1], axis=0)).then_inc(gathered[u], 16)
            pool.memset(zero[:, :], 0.0).then_inc(zero_done, 1)
            pool.wait_ge(zero_done, 1)
            fetch(0, 0, 0)
            fetch(1, 0, 1)

            def body(r, u):
                pool.wait_ge(xt_ps, r * 4 + 2 * (u + 1))
                pool.wait_ge(gathered[u], r * 16 + 16)
                fetch(r * 2 + (2 + u), r + 1, u)
                hold(pool, y_done, r * 4 + 2 * (u + 2), pool_held)
                pool.dma_start(y_b[r * 2 + u], yb[u][:, :]).then_inc(stored[u], 16)
                pool.wait_ge(stored[u], r * 16 + 16)
                pool.sem_inc(y_free, 1)

            def unused(r, u):
                pool.dma_start(y_b[r * 2 + u], zero[:, :]).then_inc(stored[u], 16)
            n = pairs(pool, body, unused)
            for u in range(2):
                pool.wait_ge(gathered[u], n * 16 + 16)
                pool.wait_ge(stored[u], (MAXB // 2) * 16)

        @block.scalar
        def _(act):
            act.sem_inc(y_free, 2)

            def features(b, u):
                for q in range(2):
                    act.wait_ge(xt_ps, b * 2 + (q + 1))
                    for j in range(4):
                        k = 4 * q + j
                        i = act.activation(xT[u][:, k, :], tx[q][:, P * j:P * (j + 1)], ACT.Identity,
                                           scale=mod[:, 4 * KT + k, 0:1], bias=mod[:, 3 * KT + k, 0:1])
                    i.then_inc(xt_done, 1)
            features(0, 0)

            def body(r, u):
                b = r * 2 + u
                act.wait_ge(gp_ps, b + 1)
                act.activation(hs[:, :], pg[:, :], ACT.Silu).then_inc(silu_done, 1)
                act.wait_ge(up_ps, b + 1)
                features(b + 1, 1 - u)
            pairs(act, body)

        @block.tensor
        def _(pe):
            for j in range(KT):
                pe.matmul(pd[j // 4][:, P * (j % 4):P * (j % 4 + 1)], mod[:, 5 * KT + j, 0:1].to_broadcast([P, P]), ident[:, :],
                          start=True, stop=True).then_inc(gate_ps, 1)
            pe.wait_ge(gate_done, 2)

            def turn(b, use, u, peeled=False):
                pe.wait_ge(gathered[u], use * 16 + 16)
                for q in range(2):
                    if not peeled:
                        pe.wait_ge(xt_done, b * 2 + (q - 1))
                    for j in range(4):
                        mm = pe.transpose(tx[q][:, P * j:P * (j + 1)], xg[u][:, P * (4 * q + j):P * (4 * q + j + 1)], ident[:, :])
                    mm.then_inc(xt_ps, 1)
            turn(0, 0, 0, True)

            def body(r, u):
                b = r * 2 + u
                par = pe.value_load(plan[0:1, bass.ds(b + PL_PAR, 1)], min_val=0, max_val=1)
                half = pe.value_load(plan[0:1, bass.ds(b + PL_HALF, 1)], min_val=0, max_val=15)
                up = pe.value_load(plan[0:1, bass.ds(b + PL_UP, 1)], min_val=0, max_val=16)
                pe.wait_ge(w_loaded[0], half * 48 + 48)
                pe.wait_ge(w_loaded[1], up * 48 + 48)
                pe.wait_ge(xt_done, b * 2 + 2)
                for w, acc, ready in ((wg, pg, gp_ps), (wu, pu, up_ps)):
                    for k in range(KT):
                        mm = pe.matmul(acc[:, :], xT[u][:, k, :], w[:, bass.ds(par, 1), k, :], start=(k == 0), stop=(k == KT - 1))
                    mm.then_inc(ready, 1)
                turn(b + 1, r + u, 1 - u)
                pe.wait_ge(h_done, b + 1)
                for j in range(KF):
                    mm = pe.transpose(ph[:, P * j:P * (j + 1)], h[:, P * j:P * (j + 1)], ident[:, :])
                mm.then_inc(ht_ps, 1)
                pe.wait_ge(ht_done, b + 1)
                pe.wait_ge(y_done, b * 2 + 2)
                for n in range(2):
                    for k in range(KF):
                        mm = pe.matmul(pd[n][:, :], hT[:, k, :], wd[:, bass.ds(par, 1), k, 512 * n:512 * (n + 1)],
                                       start=(k == 0), stop=(k == KF - 1))
                    mm.then_inc(dn_ps, 1)
            pairs(pe, body)

        @block.vector
        def _(dve):
            for n in range(2):
                dve.wait_ge(gate_ps, KT)
                dve.tensor_copy(gate_bc[:, 512 * n:512 * n + 512], pd[n][:, :]).then_inc(gate_done, 1)
            dve.wait_ge(gate_done, 2)
            dve.sem_inc(y_done, 2)

            def body(r, u):
                b = r * 2 + u
                dve.wait_ge(up_ps, b + 1)
                dve.wait_ge(silu_done, b + 1)
                dve.tensor_tensor(h[:, :], pu[:, :], hs[:, :], ALU.mult).then_inc(h_done, 1)
                dve.wait_ge(ht_ps, b + 1)
                dve.tensor_copy(hT[:, :, :], ph[:, :].rearrange("p (k c) -> p k c", k=KF)).then_inc(ht_done, 1)
                dve.wait_ge(y_free, b + 1)
                for n in range(2):
                    dve.wait_ge(dn_ps, b * 2 + (n + 1))
                    dve.tensor_tensor(yb[u][:, 512 * n:512 * n + 512], pd[n][:, :], gate_bc[:, 512 * n:512 * n + 512],
                                      ALU.mult).then_inc(y_done, 1)
            pairs(dve, body)


def combine(nc, A, C, route, y_slots, x_mid, out):
    out_t = out.rearrange("b (t p) d -> (b t) p d", p=P)
    with ExitStack() as ctx:
        sem = Names(nc, ctx, "cmb")

        def sb(name, shape, dt=F32):
            return ctx.enter_context(nc.sbuf_tensor(f"{name}_c", shape, dt))

        idx = [sb(f"idx{b}", [P, 2], I32) for b in range(2)]
        gates = [sb(f"gates{b}", [P, 2]) for b in range(2)]
        yr = [[sb(f"y{b}{j}", [P, D]) for j in range(2)] for b in range(2)]
        xr = [sb(f"x{b}", [P, D]) for b in range(2)]
        o = [sb(f"o{b}", [P, D]) for b in range(2)]
        junk, fg = sb("junk", [P, D]), sb("fg", [P, D])
        ss = [sb(f"ss{b}", [P, 1]) for b in range(2)]
        mhalf = sb("mhalf", [P, 1])
        sp_held = sem("sp_held")
        pool_held = sem("pool_held")
        x_loaded, gathered, stored = ([sem(f"{n}{b}") for b in range(2)] for n in ("x_loaded", "gathered", "stored"))
        (fg_loaded, half_done, idx_done, added, sum_done, ss_done, r_step, r_done, o_done, o_free) = (sem(n) for n in (
            "fg_loaded", "half_done", "idx_done", "added", "sum_done", "ss_done", "r_step", "r_done", "o_done", "o_free"))
        block = ctx.enter_context(nc.Block())

        def tiles(eng, body):
            with eng.Fori(0, LT // 2 - 1) as r:
                for u in range(2):
                    body(r, u, True)
            for u in range(2):
                body(LT // 2 - 1, u, False)

        @block.sync
        def _(sp):
            sp.dma_start(fg[:, :], A["final_norm_g"].rearrange("(a d) -> a d", a=1).to_broadcast([P, D])).then_inc(fg_loaded, 16)
            sp.sem_inc(o_free, 2)
            for u in range(2):
                sp.dma_start(xr[u][:, :], x_mid[u]).then_inc(x_loaded[u], 16)

            def body(r, u, more):
                it = r * 2 + u
                hold(sp, o_done, it + 1, sp_held)
                if more:
                    sp.dma_start(xr[u][:, :], x_mid[it + 2]).then_inc(x_loaded[u], 16)
                sp.dma_start(out_t[it], o[u][:, :]).then_inc(stored[u], 16)
                sp.wait_ge(stored[u], r * 16 + 16)
                sp.sem_inc(o_free, 1)
            tiles(sp, body)

        @block.gpsimd
        def _(pool):
            pool.memset(mhalf[:, :], -0.5).then_inc(half_done, 1)
            pool.wait_ge(half_done, 1)

            def gather(it, u):
                hold(pool, idx_done, it + 1, pool_held)
                for j in range(2):
                    pool.indirect_dma_start(out=yr[u][j][:, :], out_offset=None, in_=y_slots,
                                            in_offset=bass.IndirectOffsetOnAxis(ap=idx[u][:, j:j + 1], axis=0)).then_inc(gathered[u], 16)

            for u in range(2):
                gather(u, u)

            def body(r, u, more):
                it = r * 2 + u
                hold(pool, ss_done, it + 1, pool_held)
                pool.tensor_scalar(ss[u][:, :], ss[u][:, :], 1.0 / D, EPS, ALU.mult, ALU.add).then_inc(r_step, 1)
                pool.wait_ge(r_step, it + 1)
                pool.tensor_tensor(ss[u][:, :], ss[u][:, :], mhalf[:, :], ALU.pow).then_inc(r_done, 1)
                if more:
                    gather(it + 2, u)
            tiles(pool, body)

        @block.scalar
        def _(act):
            def body(r, u, more):
                it = r * 2 + u
                act.wait_ge(sum_done, it + 1)
                act.activation(junk[:, :], xr[u][:, :], ACT.Square, accum_out=ss[u][:, :]).then_inc(ss_done, 1)
                act.wait_ge(ss_done, it + 1)
            tiles(act, body)

        @block.vector
        def _(dve):
            def indices(it, u):
                dve.tensor_copy(idx[u][:, :], route["slot"][:, bass.ds(it, 1), :].rearrange("p a b -> p (a b)"))
                dve.tensor_copy(gates[u][:, :], route["gate"][:, bass.ds(it, 1), :].rearrange("p a b -> p (a b)")).then_inc(idx_done, 1)

            for u in range(2):
                indices(u, u)
            dve.wait_ge(fg_loaded, 16)

            def body(r, u, more):
                it = r * 2 + u
                dve.wait_ge(idx_done, it + 1)
                dve.wait_ge(x_loaded[u], r * 16 + 16)
                dve.wait_ge(gathered[u], r * 32 + 32)
                dve.scalar_tensor_tensor(out=xr[u][:, :], in0=yr[u][0][:, :], scalar=gates[u][:, 0:1], in1=xr[u][:, :],
                                         op0=ALU.mult, op1=ALU.add).then_inc(added, 1)
                dve.wait_ge(added, it + 1)
                dve.scalar_tensor_tensor(out=xr[u][:, :], in0=yr[u][1][:, :], scalar=gates[u][:, 1:2], in1=xr[u][:, :],
                                         op0=ALU.mult, op1=ALU.add).then_inc(sum_done, 1)
                dve.wait_ge(sum_done, it + 1)
                if more:
                    indices(it + 2, u)
                dve.wait_ge(r_done, it + 1)
                dve.wait_ge(o_free, it + 1)
                dve.scalar_tensor_tensor(out=o[u][:, :], in0=xr[u][:, :], scalar=ss[u][:, :], in1=fg[:, :],
                                         op0=ALU.mult, op1=ALU.mult).then_inc(o_done, 1)
            tiles(dve, body)


_INS = ['x', 'c', 'ctx', 'c_ctx', 'w_mod', 'b_mod', 'norm1_g', 'norm2_g', 'w_in', 'conv_w', 'conv_b', 'dt_bias_f', 'dt_bias_b',
        'a_log_f', 'a_log_b', 'd_skip', 'ssd_norm_g', 'gk_up_f', 'gk_bias_f', 'gk_up_b', 'gk_bias_b', 'gla_norm_g', 'w_out',
        'w_router', 'router_bias', 'w_gate', 'w_up', 'w_down', 'final_norm_g']
_OUTS = [((1, SEQ, D), 'float32')]


def kernel(**inputs):
    import numpy as _np
    import concourse.bacc as _bacc
    from concourse import mybir as _mybir
    from concourse.bass_utils import run_bass_kernel_spmd as _run

    nc = _bacc.Bacc("TRN2", target_bir_lowering=False, num_devices=1)
    arrays, args = {}, {}
    for name in _INS:
        a = _np.ascontiguousarray(inputs[name])
        arrays[f"in_{name}_dram"] = a
        args[name] = nc.dram_tensor(f"in_{name}_dram", a.shape, _mybir.dt.from_np(a.dtype), kind="ExternalInput").ap()
    shape, dtype = _OUTS[0]
    out = nc.dram_tensor("out_0_dram", shape, _mybir.dt.from_np(_np.dtype(dtype)), kind="ExternalOutput").ap()
    build(nc, args, out)
    r = _run(nc, [arrays], core_ids=[0])
    return r.results[0]["out_0_dram"]
```

```python
from contextlib import ExitStack

import concourse.bass as bass
from concourse import mybir

ALU = mybir.AluOpType
ACT = mybir.ActivationFunctionType
F32 = mybir.dt.float32
I32 = mybir.dt.int32
AX = mybir.AxisListType.X

P = 128
D = 1024
KT = D // P
SEQ = 2048
CTX = 256
GRP = 256
LAT_GROUPS = SEQ // GRP
TILES = (SEQ + CTX) // P
CT = CTX // P
LT = SEQ // P
SH, SP_, SN = 8, 64, 64
SW = SH * SP_
XBC = SW + 4 * SN
GH, GK, GV = 4, 64, 128
GQK = GH * GK
GW = GH * GV
RANK = 16
TAPS = 5
ROWW = 64
O_Z, O_XBC, O_DT = 0, SW, SW + XBC
O_Q = O_DT + SH
O_K = O_Q + GQK
O_V = O_K + GQK
O_G = O_V + GW
O_GK = O_G + GW
IN_DIM = O_GK + RANK
NE, NG, EG = 32, 8, 4
FF = 512
EPS = 1e-6
MAXB = 64
BIG = 1e30

R_C, R_CC = 0, KT
R_N1, R_N2 = 2 * KT, 3 * KT
R_BM = 4 * KT
R_CW = R_BM + 6 * KT
R_CB = R_CW + TAPS * (XBC // P)
R_SG = R_CB + XBC // P
R_GG = R_SG + SW // P
N_ROWS = R_GG + 1

T_X, T_B, T_K = 0, SW, SW + 2 * SN
T_V = T_K + GQK
T_DT = T_V + GW
T_GF = T_DT + 2 * SH
T_Z = T_GF + 2 * GQK
T_GO = T_Z + SW
T_LEN = T_GO + GW
F_TILES = 6


def hold(eng, sem, value, held):
    eng.wait_ge(sem, value)
    eng.sem_inc(held, 1)


class Names:

    def __init__(self, nc, ctx, prefix):
        self.nc, self.prefix, self.made = nc, prefix, []
        ctx.callback(self.clear)

    def __call__(self, name):
        self.made.append(self.nc.alloc_semaphore(f"{self.prefix}_{name}"))
        return self.made[-1]

    def clear(self):
        self.nc.clear_and_free_semaphores(self.made)
        self.nc.all_engine_barrier()


def build(nc, A, out, debug=()):
    def scratch(name, shape, dt=F32):
        kind = "ExternalOutput" if name in debug else "Internal"
        return nc.dram_tensor(name, shape, dt, kind=kind).ap()

    tok_rec = scratch("tok_rec", (TILES, P, T_LEN))
    feat_rec = scratch("feat_rec", (TILES, P, F_TILES * P))
    back_state = scratch("back_state", (TILES, P, 3 * 256))
    fwd_state = scratch("fwd_state", (1, P, 3 * 256))
    x_mid = scratch("x_mid", (LT, P, D))
    x_hat = scratch("x_hat", (SEQ, D))
    slot_tok = scratch("slot_tok", (TAB * P, 16), I32)
    y_slots = scratch("y_slots", (MAXB * P, D))

    with ExitStack() as top:
        def keep(name, shape, dt=F32):
            return top.enter_context(nc.sbuf_tensor(name, shape, dt))

        C = {n: keep(n, [P, P]) for n in ("ident", "ones", "gt", "lt", "gt_bd", "lt_bd")}
        C["incl"], C["incl_bd"] = keep("incl", [P, 2, P]), keep("incl_bd", [P, 2, P])
        for d, n in enumerate(("le", "ge")):
            C[n], C[n + "_bd"] = C["incl"][:, d, :], C["incl_bd"][:, d, :]
        C["halves"] = keep("halves", [P, 2])
        mod = keep("mod", [P, 6 * KT, 2])
        C["mod"] = mod
        C["cols"] = keep("cols", [P, N_ROWS])
        route = {
            "logits": keep("logits", [P, LT, NE]), "gate": keep("gate", [P, LT, 2]),
            "slot": keep("slot", [P, LT, 2], I32), "plan": keep("plan", [1, PL_LEN], I32),
        }
        constants(nc, C)
        with ExitStack() as ctx:
            w = ctx.enter_context(nc.sbuf_tensor("w_in_sb", [P, KT, IN_DIM], F32))
            w_loaded = Names(nc, ctx, "inp")("w_in_loaded")
            modulation(nc, A, C, w, w_loaded)
            projection(nc, A, C, w, w_loaded, tok_rec, feat_rec)
        if "stop1" in debug:
            return
        scan_states(nc, A, C, tok_rec, 1, back_state)
        scan_states(nc, A, C, tok_rec, 0, fwd_state)
        if "stop2" in debug:
            return
        mixer(nc, A, C, route, tok_rec, feat_rec, back_state, fwd_state, x_mid, x_hat)
        if "stop3" in debug:
            return
        slots(nc, A, C, route, slot_tok)
        experts(nc, A, C, route, slot_tok, x_hat, y_slots)
        combine(nc, A, C, route, y_slots, x_mid, out)


def constants(nc, C):
    with ExitStack() as ctx:
        sem = Names(nc, ctx, "cst")
        block = ctx.enter_context(nc.Block())
        made, cut = sem("made"), sem("cut")
        H = P // 2

        @block.gpsimd
        def _(pool):
            n = 0
            for name in ("ident", "le_bd", "ge_bd", "gt_bd", "lt_bd"):
                pool.memset(C[name][:, :], 1.0 if name != "ident" else 0.0).then_inc(made, 1)
                n += 1
            for name in ("ones", "le", "ge", "gt", "lt", "halves"):
                pool.memset(C[name][:, :], 1.0).then_inc(made, 1)
                n += 1
            pool.wait_ge(made, n)
            def select(t, step, cm, base, op, fill=0.0, w=P):
                pool.affine_select(out=t, in_=t, compare_op=op, fill=fill, base=base,
                                   pattern=[[step, w]], channel_multiplier=cm).then_inc(cut, 1)
            select(C["ident"][:, :], -1, 1, 0, ALU.not_equal, 1.0)
            signs = {"le": (1, -1, ALU.is_ge), "ge": (-1, 1, ALU.is_ge),
                     "gt": (-1, 1, ALU.is_gt), "lt": (1, -1, ALU.is_gt)}
            m = 1
            for name, (step, cm, op) in signs.items():
                select(C[name][:, :], step, cm, 0, op)
                select(C[name + "_bd"][:, :], step, cm, 0, op)
                m += 2
            pool.wait_ge(cut, m)
            for name in signs:
                pool.memset(C[name + "_bd"][0:H, H:P], 0.0).then_inc(cut, 1)
                pool.memset(C[name + "_bd"][H:P, 0:H], 0.0).then_inc(cut, 1)
            pool.memset(C["halves"][0:H, 1:2], 0.0).then_inc(cut, 1)
            pool.memset(C["halves"][H:P, 0:1], 0.0).then_inc(cut, 1)
            pool.wait_ge(cut, m + 10)


def modulation(nc, A, C, w_in_sb, w_in_loaded):
    mod = C["mod"]
    W = 512
    STEPS = 6 * D // W
    w_d = A["w_mod"].rearrange("l (k p) (n c) -> l n p k c", p=P, c=W)[0]
    with ExitStack() as ctx:
        sem = Names(nc, ctx, "mod")
        slab = [ctx.enter_context(nc.sbuf_tensor(f"w_mod{b}", [P, KT, W], F32)) for b in range(3)]
        rows = ctx.enter_context(nc.sbuf_tensor("rows", [N_ROWS, P], F32))
        cond = ctx.enter_context(nc.sbuf_tensor("cond_silu", [P, KT, 2], F32))
        line = [ctx.enter_context(nc.sbuf_tensor(f"line{b}", [2, W], F32)) for b in range(3)]
        rows_t = ctx.enter_context(nc.psum_tensor("rows_t", [P, N_ROWS], F32))
        cols = C["cols"]
        bias = cols[:, R_BM:R_BM + 6 * KT]
        acc = [ctx.enter_context(nc.psum_tensor(f"mod_acc{b}", [2, W], F32)) for b in range(3)]
        turn = ctx.enter_context(nc.psum_tensor("mod_turn", [P, 6 * KT, 2], F32))
        loaded = [sem(f"slab{b}_loaded") for b in range(3)]
        small, turned, copied, silu_done, slab_used, line_done, lines_turned, added, scaled = (
            sem(n) for n in ("small_loaded", "rows_transposed", "cols_copied", "silu_done", "slab_used", "line_done",
                             "lines_turned", "added", "scaled"))
        block = ctx.enter_context(nc.Block())

        @block.sync
        def _(sp):
            for at, n, src in ((R_C, KT, A["c"].rearrange("b (k p) -> (b k) p", p=P)),
                               (R_CC, KT, A["c_ctx"].rearrange("(k p) -> k p", p=P)),
                               (R_N1, KT, A["norm1_g"].rearrange("l (k p) -> (l k) p", p=P)),
                               (R_N2, KT, A["norm2_g"].rearrange("l (k p) -> (l k) p", p=P)),
                               (R_BM, 6 * KT, A["b_mod"].rearrange("l (k p) -> (l k) p", p=P)),
                               (R_CW, TAPS * 6, A["conv_w"].rearrange("l t (k p) -> (l t k) p", p=P)),
                               (R_CB, 6, A["conv_b"].rearrange("l (k p) -> (l k) p", p=P)),
                               (R_SG, 4, A["ssd_norm_g"].rearrange("l (k p) -> (l k) p", p=P)),
                               (R_GG, 1, A["gla_norm_g"])):
                sp.dma_start(rows[at:at + n, :], src).then_inc(small, 16)
            sp.sem_inc(slab_used, 3)
            with sp.Fori(0, STEPS // 3) as r:
                for u in range(3):
                    sp.wait_ge(slab_used, r * 3 + (u + 1))
                    sp.dma_start(slab[u][:, :, :], w_d[r * 3 + u]).then_inc(loaded[u], 16)
            for k in range(KT):
                sp.dma_start(w_in_sb[:, k, :], A["w_in"][0][k * P:(k + 1) * P, :]).then_inc(w_in_loaded, 16)

        @block.scalar
        def _(act):
            act.wait_ge(copied, 1)
            for j in range(2):
                act.activation(cond[:, :, j], cols[:, KT * j:KT * (j + 1)], ACT.Silu).then_inc(silu_done, 1)

        @block.tensor
        def _(pe):
            pe.wait_ge(small, 16 * 9)
            pe.transpose(rows_t[:, :], rows[:, :], C["ident"][0:N_ROWS, 0:N_ROWS]).then_inc(turned, 1)
            pe.wait_ge(silu_done, 2)
            with pe.Fori(0, STEPS // 3) as r:
                for u in range(3):
                    pe.wait_ge(loaded[u], r * 16 + 16)
                    pe.wait_ge(line_done, r * 3 + (u + 1))
                    for k in range(KT):
                        mm = pe.matmul(acc[u][:, :], cond[:, k, :], slab[u][:, k, :], start=(k == 0), stop=(k == KT - 1))
                    mm.then_inc(slab_used, 1)
                for u in range(3):
                    pe.wait_ge(line_done, r * 3 + (u + 4))
                    for m in range(W // P):
                        mm = pe.matmul(turn[:, bass.ds(r * 12 + (4 * u + m), 1), :], line[u][:, m * P:(m + 1) * P], C["ident"][0:2, 0:2],
                                       start=True, stop=True)
                    mm.then_inc(lines_turned, 1)

        @block.vector
        def _(dve):
            dve.wait_ge(turned, 1)
            dve.tensor_copy(cols[:, :], rows_t[:, :]).then_inc(copied, 1)
            dve.wait_ge(copied, 1)
            dve.sem_inc(line_done, 3)
            dve.sem_inc(lines_turned, 3)
            with dve.Fori(0, STEPS // 3) as r:
                for u in range(3):
                    dve.wait_ge(slab_used, r * 3 + (u + 4))
                    dve.wait_ge(lines_turned, r * 3 + (u + 1))
                    dve.tensor_copy(line[u][:, :], acc[u][:, :]).then_inc(line_done, 1)
            dve.wait_ge(lines_turned, 3 + STEPS)
            dve.tensor_tensor(mod[:, :, :], turn[:, :, :], bias.unsqueeze(2).to_broadcast([P, 6 * KT, 2]),
                              ALU.add).then_inc(added, 1)
            dve.wait_ge(added, 1)
            for n, part in enumerate((1, 4)):
                s = mod[:, part * KT:(part + 1) * KT, :]
                dve.scalar_tensor_tensor(out=s, in0=s, scalar=1.0, in1=cols[:, R_N1 + KT * n:R_N1 + KT * (n + 1)].unsqueeze(2).to_broadcast([P, KT, 2]),
                                         op0=ALU.add, op1=ALU.mult).then_inc(scaled, 1)
            dve.wait_ge(scaled, 2)


def projection(nc, A, C, w, w_loaded, tok_rec, feat_rec):
    mod, ident = C["mod"], C["ident"]
    x_d = A["x"].rearrange("b (g s p) d -> (b g) p s d", s=2, p=P)
    ctx_d = A["ctx"].rearrange("b (s p) d -> b p s d", p=P)[0]
    tok_g = tok_rec.rearrange("(g s) p f -> g p s f", s=2)
    feat_g = feat_rec.rearrange("(g s) p (n c) -> g s p n c", s=2, c=P)
    NF = 10
    col = [O_XBC + i * P for i in range(6)] + [O_Q, O_Q + P, O_K, O_K + P]
    with ExitStack() as ctx:
        sem = Names(nc, ctx, "prj")

        def sb(name, shape, dt=F32):
            return ctx.enter_context(nc.sbuf_tensor(name, shape, dt))

        def ps(name, shape):
            return ctx.enter_context(nc.psum_tensor(name, shape, F32))

        w_small = sb("w_small", [P, KT, 32])
        xg = sb("xg", [P, 2, D])
        junk = ps("sq_junk", [P, 512])
        hT = [sb(f"hT{b}", [P, KT, GRP]) for b in range(2)]
        u_raw = sb("u_raw", [P, 6, GRP])
        fm = sb("fm", [P, NF, GRP])
        tm = [sb(f"tm{b}", [P, 2, T_LEN]) for b in range(2)]
        soft = [sb(f"soft{b}", [P, 528]) for b in range(2)]
        small_sb = sb("small_sb", [P, 2, 32])
        gkT = sb("gkT", [RANK + 1, 2, P])
        up = sb("gk_up", [RANK + 1, 2 * GQK])
        dtb = sb("dt_bias", [1, 2 * SH])
        cols = C["cols"]
        ss = sb("ss", [P, 2, 2])
        rstd = sb("rstd", [P, 2])
        mhalf = sb("mhalf", [P, 2])
        pt = [ps(f"pt{b}", [P, 512]) for b in range(2)]
        pf = [ps(f"pf{b}", [P, 2, GRP]) for b in range(2)]
        pz = [ps(f"pz{b}", [P, 512]) for b in range(2)]
        psm = ps("psm", [P, 512])

        pool_held = sem("pool_held")
        small_loaded, x_loaded = sem("small_loaded"), sem("x_loaded")
        x_free, ss_done, rstd_done, xn_done = (sem(n) for n in ("x_free", "ss_done", "rstd_done", "xn_done"))
        ht_ps, ht_done = sem("ht_transposed"), sem("ht_done")
        feat_ps, u_done, qk_done, conv_done, silu_done = (
            sem(n) for n in ("feat_product", "u_done", "qk_done", "conv_done", "silu_done"))
        tok_ps, tok_done = sem("tok_product"), sem("tok_done")
        small_ps, small_done, gk_ps, gk_done, g_ps, abs_done, exp_done, ln_done, min_done, g_done = (
            sem(n) for n in ("small_product", "small_copied", "gk_transposed", "gk_copied", "g_product",
                             "abs_done", "exp_done", "ln_done", "min_done", "g_done"))
        back_ps, back_done = sem("back_transposed"), sem("back_copied")
        stored, feat_stored = [sem("tm0_stored"), sem("tm1_stored")], sem("fm_stored")
        const_done, wsm_done, junk_done = sem("const_done"), sem("w_small_done"), sem("junk_done")
        conv_step, hT_free = sem("conv_step"), sem("hT_free")
        block = ctx.enter_context(nc.Block())

        def steps(eng, body):
            body(0, 0, 0, True)
            with eng.Fori(0, LAT_GROUPS // 2) as r:
                body(r * 2 + 1, r, 1, False)
                body(r * 2 + 2, r + 1, 0, False)

        @block.sync
        def _(sp):
            sp.dma_start(dtb[:, 0:SH], A["dt_bias_f"]).then_inc(small_loaded, 16)
            sp.dma_start(dtb[:, SH:2 * SH], A["dt_bias_b"]).then_inc(small_loaded, 16)
            sp.dma_start(up[0:RANK, 0:GQK], A["gk_up_f"][0]).then_inc(small_loaded, 16)
            sp.dma_start(up[0:RANK, GQK:2 * GQK], A["gk_up_b"][0]).then_inc(small_loaded, 16)
            sp.dma_start(up[RANK:RANK + 1, 0:GQK], A["gk_bias_f"]).then_inc(small_loaded, 16)
            sp.dma_start(up[RANK:RANK + 1, GQK:2 * GQK], A["gk_bias_b"]).then_inc(small_loaded, 16)

            def body(it, use, buf, is_ctx):
                sp.wait_ge(silu_done, it + 1)
                sp.wait_ge(qk_done, it * 2 + 2)
                for s in range(2):
                    sp.dma_start(feat_g[it][s], fm[:, 4:10, s * P:(s + 1) * P]).then_inc(feat_stored, 16)
                sp.wait_ge(tok_done, 2 if is_ctx else 2 + it * 6)
                sp.wait_ge(g_done, it * 2 + 2)
                sp.wait_ge(back_done, it * 4 + 4)
                if is_ctx:
                    sp.dma_start(tok_g[0][:, :, 0:T_Z], tm[buf][:, :, 0:T_Z]).then_inc(stored[buf], 16)
                else:
                    sp.dma_start(tok_g[it], tm[buf][:, :, :]).then_inc(stored[buf], 16)

            steps(sp, body)
            sp.wait_ge(feat_stored, 32 * (LAT_GROUPS + 1))
            sp.wait_ge(stored[0], 16 * (LAT_GROUPS // 2 + 1))
            sp.wait_ge(stored[1], 16 * (LAT_GROUPS // 2 + 1))

        @block.scalar
        def _(act):
            def body(it, use, buf, is_ctx):
                act.wait_ge(x_loaded, it * 16 + 16)
                for s in range(2):
                    for h in range(2):
                        if s + h:
                            act.wait_ge(junk_done, it * 4 + 2 * s + h)
                        elif not is_ctx:
                            act.wait_ge(junk_done, it * 4)
                        act.activation(junk[:, :], xg[:, s, h * 512:(h + 1) * 512], ACT.Square,
                                       accum_out=ss[:, s, h:h + 1]).then_inc(junk_done, 1)
                act.wait_ge(junk_done, it * 4 + 4)
                act.sem_inc(ss_done, 1)
                for n in range(5):
                    act.wait_ge(feat_ps, it * 5 + (n + 1))
                    if n < 3:
                        if n == 0 and not is_ctx:
                            act.wait_ge(conv_done, it)
                        act.activation(u_raw[:, 2 * n:2 * n + 2, :], pf[(n) % 2][:, :, :], ACT.Copy).then_inc(u_done, 1)
                    else:
                        if n == 3 and not is_ctx:
                            act.wait_ge(feat_stored, it * 32)
                            act.wait_ge(back_done, it * 4)
                        act.activation(fm[:, 2 * n:2 * n + 2, :], pf[(n) % 2][:, :, :], ACT.Copy,
                                       scale=GK ** -0.5 if n == 3 else 1.0).then_inc(qk_done, 1)
                act.wait_ge(conv_done, it + 1)
                act.activation(fm[:, 0:6, :], fm[:, 0:6, :], ACT.Silu).then_inc(silu_done, 1)
                n = 0
                per = 2 if is_ctx else 6
                base = 0 if is_ctx else 2 + (it - 1) * 6
                for s in range(2):
                    for part in ("v",) if is_ctx else ("z", "g", "v"):
                        act.wait_ge(tok_ps, base + (n + 1))
                        if n == 0 and not is_ctx:
                            act.wait_ge(stored[buf], use * 16 + 16 * buf)
                        o = {"z": T_Z, "g": T_GO, "v": T_V}[part]
                        act.activation(tm[buf][:, s, o:o + 512], pz[n % 2][:, :],
                                       ACT.Copy if part == "v" else ACT.Silu).then_inc(tok_done, 1)
                        n += 1
                for s in range(2):
                    act.wait_ge(g_ps, it * 2 + (s + 1))
                    if not is_ctx:
                        act.wait_ge(g_done, it * 2)
                    act.activation(soft[s][:, 0:512], pz[s][:, :], ACT.Abs).then_inc(abs_done, 1)
                    act.activation(soft[s][:, 512:528], small_sb[:, s, 0:16], ACT.Abs).then_inc(abs_done, 1)
                for s in range(2):
                    act.wait_ge(abs_done, it * 4 + 2 * s + 2)
                    act.activation(soft[s][:, :], soft[s][:, :], ACT.Exp, scale=-1.0).then_inc(exp_done, 1)
                for s in range(2):
                    act.wait_ge(exp_done, it * 2 + (s + 1))
                    act.activation(soft[s][:, :], soft[s][:, :], ACT.Ln, bias=1.0).then_inc(ln_done, 1)
            act.sem_inc(stored[1], 16)
            steps(act, body)

        @block.gpsimd
        def _(pool):
            pool.memset(mhalf[:, :], -0.5).then_inc(const_done, 1)
            pool.memset(gkT[:, :, :], 1.0).then_inc(const_done, 1)
            pool.wait_ge(const_done, 2)

            def body(it, use, buf, is_ctx):
                if not is_ctx:
                    hold(pool, x_free, it, pool_held)
                pool.dma_start(xg[:, :, :], ctx_d if is_ctx else x_d[it - 1]).then_inc(x_loaded, 16)
                pool.wait_ge(ss_done, it + 1)
                if not is_ctx:
                    pool.wait_ge(xn_done, it)
                pool.tensor_tensor(rstd[:, :], ss[:, :, 0], ss[:, :, 1], ALU.add).then_inc(rstd_done, 1)
                hold(pool, rstd_done, it * 3 + 1, pool_held)
                pool.tensor_scalar(rstd[:, :], rstd[:, :], 1.0 / D, EPS, ALU.mult, ALU.add).then_inc(rstd_done, 1)
                pool.wait_ge(rstd_done, it * 3 + 2)
                pool.tensor_tensor(rstd[:, :], rstd[:, :], mhalf[:, :], ALU.pow).then_inc(rstd_done, 1)
            steps(pool, body)

        @block.tensor
        def _(pe):
            pe.wait_ge(wsm_done, 2)
            pe.wait_ge(const_done, 2)
            pe.wait_ge(small_loaded, 16 * 6)

            def body(it, use, buf, is_ctx):
                pe.wait_ge(xn_done, it + 1)
                for q in range(4):
                    if q >= 2:
                        pe.wait_ge(ht_done, it * 4 + (q - 1))
                    elif not is_ctx:
                        pe.wait_ge(back_done, it * 4)
                    for kk in range(2):
                        for s in range(2):
                            mm = pe.transpose(pt[q % 2][:, kk * GRP + s * P:kk * GRP + (s + 1) * P],
                                              xg[:, s, (2 * q + kk) * P:(2 * q + kk + 1) * P], ident[:, :])
                    mm.then_inc(ht_ps, 1)
                pe.wait_ge(ht_done, it * 4 + 4)
                h = hT[buf]
                for n in range(5):
                    if n >= 2 or not is_ctx:
                        m = n - 2
                        if m >= 0:
                            pe.wait_ge(u_done if m < 3 else qk_done, it * 3 + (m + 1) if m < 3 else it * 2 + (m - 2))
                        elif n == 0:
                            pe.wait_ge(qk_done, it * 2)
                    for f in range(2):
                        for k in range(KT):
                            c0 = col[2 * n + f]
                            mm = pe.matmul(pf[n % 2][:, f, :], w[:, k, c0:c0 + P], h[:, k, :],
                                           start=(k == 0), stop=(k == KT - 1))
                    mm.then_inc(feat_ps, 1)
                if not is_ctx:
                    pe.wait_ge(gk_done, it)
                    pe.wait_ge(small_done, it)
                for s in range(2):
                    for k in range(KT):
                        pe.matmul(psm[:, s * 32:s * 32 + 32], h[:, k, s * P:(s + 1) * P], w_small[:, k, :],
                                  start=(k == 0), stop=False)
                    mm = pe.matmul(psm[:, s * 32:s * 32 + 16], C["ones"][0:1, :], dtb[0:1, :], start=False, stop=True)
                mm.then_inc(small_ps, 1)
                n = 0
                base = 0 if is_ctx else 2 + (it - 1) * 6
                for s in range(2):
                    for part in ("v",) if is_ctx else ("z", "g", "v"):
                        if n >= 2:
                            pe.wait_ge(tok_done, base + (n - 1))
                        elif n == 0 and not is_ctx:
                            pe.wait_ge(min_done, it * 4)
                            pe.wait_ge(abs_done, it * 4)
                        o = {"z": O_Z, "g": O_G, "v": O_V}[part]
                        for k in range(KT):
                            mm = pe.matmul(pz[n % 2][:, :], h[:, k, s * P:(s + 1) * P], w[:, k, o:o + 512],
                                           start=(k == 0), stop=(k == KT - 1))
                        mm.then_inc(tok_ps, 1)
                        n += 1
                pe.wait_ge(small_done, it + 1)
                for s in range(2):
                    mm = pe.transpose(psm[0:RANK, 128 + s * P:256 + s * P], small_sb[:, s, 16:32], ident[:, :])
                mm.then_inc(gk_ps, 1)
                pe.wait_ge(gk_done, it + 1)
                pe.wait_ge(tok_done, base + n)
                for s in range(2):
                    pe.matmul(pz[s][:, :], gkT[:, s, :], up[:, :], start=True, stop=True).then_inc(g_ps, 1)
                pe.wait_ge(silu_done, it + 1)
                pe.wait_ge(qk_done, it * 2 + 2)
                for s in range(2):
                    for half in range(2):
                        q = 2 * s + half
                        if q >= 2:
                            pe.wait_ge(back_done, it * 4 + (q - 1))
                        tiles = (0, 1, 2, 3) if half == 0 else (4, 8, 9)
                        for j, f in enumerate(tiles):
                            mm = pe.transpose(pt[q % 2][:, j * P:(j + 1) * P], fm[:, f, s * P:(s + 1) * P], ident[:, :])
                        mm.then_inc(back_ps, 1)
            steps(pe, body)

        @block.vector
        def _(dve):
            dve.wait_ge(w_loaded, 16 * KT)
            for j in range(2):
                dve.tensor_copy(w_small[:, :, 8 * j:8 * j + 8], w[:, :, O_DT:O_DT + 8])
            dve.tensor_copy(w_small[:, :, 16:32], w[:, :, O_GK:O_GK + 16]).then_inc(wsm_done, 2)
            dve.wait_ge(small_loaded, 16 * 6)

            def body(it, use, buf, is_ctx):
                dve.wait_ge(rstd_done, it * 3 + 3)
                for s in range(2):
                    i = dve.tensor_scalar(xg[:, s, :], xg[:, s, :], rstd[:, s:s + 1], None, ALU.mult)
                i.then_inc(xn_done, 1)
                who = 1 if is_ctx else 0
                for q in range(4):
                    dve.wait_ge(ht_ps, it * 4 + (q + 1))
                    for kk in range(2):
                        k = 2 * q + kk
                        i = dve.tensor_scalar(hT[buf][:, k, :], pt[q % 2][:, kk * GRP:(kk + 1) * GRP],
                                              mod[:, KT + k, who:who + 1], mod[:, k, who:who + 1], ALU.mult, ALU.add)
                    i.then_inc(ht_done, 1)
                    if q == 3:
                        dve.sem_inc(x_free, 1)
                wide = GRP if is_ctx else ROWW
                dve.wait_ge(u_done, it * 3 + 3)
                if not is_ctx:
                    dve.wait_ge(feat_stored, it * 32)
                    dve.wait_ge(back_done, it * 4)
                for n, tap in enumerate((2, 0, 1, 3, 4)):
                    if n:
                        dve.wait_ge(conv_step, it * 4 + n)
                    for f in range(6):
                        a = fm[:, f, :].rearrange("p (r t) -> p r t", t=wide)
                        b = u_raw[:, f, :].rearrange("p (r t) -> p r t", t=wide)
                        wt = cols[:, R_CW + 6 * tap + f:R_CW + 6 * tap + f + 1]
                        if tap == 2:
                            i = dve.tensor_scalar(a, b, wt, cols[:, R_CB + f:R_CB + f + 1], ALU.mult, ALU.add)
                            continue
                        sh = tap - 2
                        to, fr = (a[:, :, -sh:], b[:, :, :wide + sh]) if sh < 0 else (a[:, :, :wide - sh], b[:, :, sh:])
                        i = dve.scalar_tensor_tensor(out=to, in0=fr, scalar=wt, in1=to, op0=ALU.mult, op1=ALU.add)
                    i.then_inc(conv_done if n == 4 else conv_step, 1)
                dve.wait_ge(small_ps, it + 1)
                if not is_ctx:
                    dve.wait_ge(abs_done, it * 4)
                    dve.wait_ge(min_done, it * 4)
                dve.tensor_copy(small_sb[:, :, :], psm[:, 0:64].rearrange("p (s c) -> p s c", s=2)).then_inc(small_done, 1)
                dve.wait_ge(gk_ps, it + 1)
                dve.tensor_copy(gkT[0:RANK, :, :], psm[0:RANK, 128:384].rearrange("p (s c) -> p s c", s=2)).then_inc(gk_done, 1)
                t = tm[buf]
                if not is_ctx:
                    dve.wait_ge(stored[buf], use * 16 + (0 if buf == 0 else 16))
                for s in range(2):
                    dve.wait_ge(g_ps, it * 2 + (s + 1))
                    dve.wait_ge(abs_done, it * 4 + (2 * s + 1))
                    dve.tensor_scalar(t[:, s, T_GF:T_GF + 512], pz[s][:, :], 0.0, 1 / 16.0, ALU.min, ALU.mult).then_inc(min_done, 1)
                    dve.tensor_scalar(t[:, s, T_DT:T_DT + 16], small_sb[:, s, 0:16], 0.0, None, ALU.max).then_inc(min_done, 1)
                for s in range(2):
                    for half in range(2):
                        q = 2 * s + half
                        dve.wait_ge(back_ps, it * 4 + (q + 1))
                        if half == 0:
                            dve.tensor_copy(t[:, s, T_X:T_X + 512], pt[q % 2][:, :]).then_inc(back_done, 1)
                        else:
                            dve.tensor_copy(t[:, s, T_B:T_B + 384], pt[q % 2][:, 0:384]).then_inc(back_done, 1)
                for s in range(2):
                    dve.wait_ge(ln_done, it * 2 + (s + 1))
                    dve.wait_ge(min_done, it * 4 + 4)
                    dve.scalar_tensor_tensor(out=t[:, s, T_GF:T_GF + 512], in0=soft[s][:, 0:512], scalar=-1 / 16.0,
                                             in1=t[:, s, T_GF:T_GF + 512], op0=ALU.mult, op1=ALU.add)
                    dve.tensor_tensor(t[:, s, T_DT:T_DT + 16], t[:, s, T_DT:T_DT + 16], soft[s][:, 512:528],
                                      ALU.add).then_inc(g_done, 1)
            steps(dve, body)


def direction(C, d):
    return (C["le"], C["gt"], C["le_bd"], C["gt_bd"]) if d == 0 else (C["ge"], C["lt"], C["ge_bd"], C["lt_bd"])


def state_products(pe, C, d, rec, dta, small):
    _, past, _, past_bd = direction(C, d)
    g0 = T_GF + d * GQK
    pe.matmul(small[:, 0:GQK], past_bd[:, :], rec[:, g0:g0 + GQK], start=True, stop=True)
    pe.matmul(small[:, 256:264], past[:, :], dta, start=True, stop=True)
    for g in range(2):
        pe.matmul(small[64 * g:64 * g + 64, 264:268], C["ones"][:, 0:64], dta[:, 4 * g:4 * g + 4], start=True, stop=True)
    for pair in range(2):
        mm = pe.matmul(small[:, 268 + 2 * pair:270 + 2 * pair], rec[:, g0 + P * pair:g0 + P * (pair + 1)],
                       C["halves"][:, :], start=True, stop=True)
    return mm


class Turn:

    def __init__(self, c, r=None):
        self.it = c if r is None else r * 4 + c
        self.use4 = c // 4 if r is None else r + c // 4
        self.least, self.b4, self.b2 = c, c % 4, c % 2
        self.c, self.r = c, r

    def before(self, n):
        return Turn(self.c - n, self.r)


def scan_states(nc, A, C, tok_rec, d, state_out):
    first, second = (1, 0) if d else (0, 1)
    LAST = TILES if d else CT
    with ExitStack() as ctx:
        sem = Names(nc, ctx, f"sc{d}")

        def sb(name, shape, dt=F32):
            return ctx.enter_context(nc.sbuf_tensor(f"{name}_s{d}", shape, dt))

        def ps(name, shape):
            return ctx.enter_context(nc.psum_tensor(f"{name}_s{d}", shape, F32))

        rec = [sb(f"rec{b}", [P, T_Z]) for b in range(4)]
        st = [sb(f"st{b}", [P, 3, 256]) for b in range(4)]
        ex = [sb(f"ex{b}", [P, 272]) for b in range(4)]
        nega = sb("nega", [P, SH])
        dta, wend = ([sb(f"{n}{b}", [P, SH]) for b in range(2)] for n in ("dta", "wend"))
        xw, kend = [sb(f"xw{b}", [P, SW]) for b in range(2)], [sb(f"kend{b}", [P, GQK]) for b in range(2)]
        small, p_ssd = ([ps(f"{n}{b}", [P, 512]) for b in range(2)] for n in ("small", "p_ssd"))
        p_gla = [[ps(f"p_gla{c}{b}", [P, 2, P]) for c in range(2)] for b in range(2)]
        sp_held = sem("sp_held")
        loaded = [sem(f"rec{b}_loaded") for b in range(4)]
        saved = [sem(f"st{b}_saved") for b in range(4)]
        (a_loaded, a_exp, a_done, zeroed, dta_done, small_ps, ex_done, wend_done, scaled, kend_done,
         states_ps, decayed, mid_done, next_done) = (sem(n) for n in (
             "a_loaded", "a_exp", "a_done", "zeroed", "dta_done", "small_product", "exp_done", "wend_done", "x_scaled",
             "kend_done", "state_products", "decayed", "mid_state", "next_state"))
        block = ctx.enter_context(nc.Block())
        a_d = A["a_log_b" if d else "a_log_f"]

        def rounds(eng, *parts):
            def static(i):
                for n, f in parts:
                    if 0 <= i + n < LAST:
                        f(Turn(i + n))
            for i in range(-3, 2):
                static(i)
            if d:
                with eng.Fori(0, (LAST - 6) // 4) as r:
                    for u in range(4):
                        for n, f in parts:
                            f(Turn(2 + u + n, r))
                for i in range(LAST - 4, LAST):
                    static(i)

        @block.sync
        def _(sp):
            sp.dma_start(nega[:, :], a_d.to_broadcast([P, SH])).then_inc(a_loaded, 16)
            for b in range(4):
                sp.sem_inc(saved[b], 16)

            def load(t):
                if t.least >= 4:
                    hold(sp, next_done, t.it - 3, sp_held)
                at = (TILES + 1) - t.it if t.least >= CT else 1 - t.it if d else t.it
                sp.dma_start(rec[t.b4][:, :], tok_rec[at][:, 0:T_Z]).then_inc(loaded[t.b4], 16)

            def save(t):
                if t.least < CT:
                    return
                hold(sp, mid_done, t.it + 1, sp_held)
                sp.dma_start(state_out[(TILES + 1) - t.it], st[t.b4][:, :, :].rearrange("p a b -> p (a b)")).then_inc(saved[t.b4], 16)
            rounds(sp, (3, load), (0, save))
            if d:
                for b in range(4):
                    sp.wait_ge(saved[b], 16 * (LT // 4 + 1))
            else:
                sp.wait_ge(next_done, CT)
                sp.dma_start(state_out[0], st[CT][:, :, :].rearrange("p a b -> p (a b)")).then_inc(saved[CT], 16)
                sp.wait_ge(saved[CT], 32)

        @block.scalar
        def _(act):
            act.wait_ge(a_loaded, 16)
            act.activation(nega[:, :], nega[:, :], ACT.Exp).then_inc(a_exp, 1)

            def exponentials(t):
                act.wait_ge(small_ps, t.it + 1)
                if t.least >= 4:
                    act.wait_ge(next_done, t.it - 3)
                act.activation(ex[t.b4][:, :], small[t.b2][:, 0:272], ACT.Exp).then_inc(ex_done, 1)
            rounds(act, (2, exponentials))

        @block.tensor
        def _(pe):
            def sums(t):
                pe.wait_ge(dta_done, t.it + 1)
                if t.least >= 2:
                    pe.wait_ge(ex_done, t.it - 1)
                state_products(pe, C, d, rec[t.b4], dta[t.b2][:, :], small[t.b2]).then_inc(small_ps, 1)

            def products(t):
                pe.wait_ge(scaled, t.it + 1)
                pe.wait_ge(kend_done, t.it + 1)
                if t.least >= 2:
                    pe.wait_ge(next_done, t.it - 1)
                state_matmuls(pe, rec[t.b4], xw[t.b2], kend[t.b2], p_ssd[t.b2], p_gla[t.b2]).then_inc(states_ps, 1)
            rounds(pe, (0, products), (2, sums))

        @block.vector
        def _(dve):
            for b in range(4):
                dve.memset(st[b][:, :, :], 0.0).then_inc(zeroed, 1)
            dve.wait_ge(a_exp, 1)
            dve.tensor_scalar(nega[:, :], nega[:, :], -1.0, None, ALU.mult).then_inc(a_done, 1)
            dve.wait_ge(a_done, 1)
            dve.wait_ge(zeroed, 4)

            def dt(t):
                return rec[t.b4][:, T_DT + SH * d:T_DT + SH * (d + 1)]

            def log_decays(t):
                dve.wait_ge(loaded[t.b4], t.use4 * 16 + 16)
                if t.least >= 2:
                    dve.wait_ge(small_ps, t.it - 1)
                dve.tensor_tensor(dta[t.b2][:, :], dt(t), nega[:, :], ALU.mult).then_inc(dta_done, 1)

            def weighted(t):
                dve.wait_ge(ex_done, t.it + 1)
                if t.least >= 2:
                    dve.wait_ge(states_ps, t.it - 1)
                dve.tensor_tensor(wend[t.b2][:, :], ex[t.b4][:, 256:264], dt(t), ALU.mult).then_inc(wend_done, 1)
                dve.tensor_tensor(kend[t.b2][:, :], rec[t.b4][:, T_K:T_K + GQK], ex[t.b4][:, 0:256], ALU.mult).then_inc(kend_done, 1)
                dve.wait_ge(wend_done, t.it + 1)
                dve.tensor_tensor(xw[t.b2][:, :].rearrange("p (h c) -> p h c", h=SH),
                                  rec[t.b4][:, 0:SW].rearrange("p (h c) -> p h c", h=SH),
                                  wend[t.b2][:, :].unsqueeze(2).to_broadcast([P, SH, SP_]), ALU.mult).then_inc(scaled, 1)

            def states(t):
                dve.wait_ge(states_ps, t.it + 1)
                if t.least >= 1:
                    dve.wait_ge(next_done, t.it)
                if t.least >= 2:
                    old = t.before(3)
                    dve.wait_ge(saved[old.b4], (old.use4 + (2 if old.b4 >= 2 else 1)) * 16)
                update_states(dve, t.it, ex[t.b4], p_ssd[t.b2], p_gla[t.b2], st[t.b4], st[(t.b4 + 1) % 4], first, second,
                              decayed, mid_done, next_done)
            rounds(dve, (2, log_decays), (1, weighted), (0, states))


def state_matmuls(pe, rec, xw, kend, p_ssd, p_gla):
    for g in range(2):
        pe.matmul(p_ssd[64 * g:64 * g + 64, 0:256], rec[:, T_B + 64 * g:T_B + 64 * g + 64],
                  xw[:, 256 * g:256 * g + 256], start=True, stop=True)
    for c in range(2):
        for h in range(GH):
            mm = pe.matmul(p_gla[c][64 * (h % 2):64 * (h % 2) + 64, h // 2, :], kend[64 * c:64 * c + 64, 64 * h:64 * h + 64],
                           rec[64 * c:64 * c + 64, T_V + GV * h:T_V + GV * (h + 1)], start=True, stop=True)
    return mm


def update_states(dve, it, ex, p_ssd, p_gla, now, nxt, first, second, decayed, mid_done, next_done):
    for pair in range(2):
        i = dve.scalar_tensor_tensor(out=now[:, 1 + second, P * pair:P * (pair + 1)],
                                     in0=now[:, 1 + first, P * pair:P * (pair + 1)],
                                     scalar=ex[:, 268 + 2 * pair + first:269 + 2 * pair + first],
                                     in1=p_gla[first][:, pair, :], op0=ALU.mult, op1=ALU.add)
    i.then_inc(mid_done, 1)
    h = now[:, 0, :].rearrange("p (h c) -> p h c", h=4)
    n = nxt[:, 0, :].rearrange("p (h c) -> p h c", h=4)
    dve.tensor_tensor(n, h, ex[:, 264:268].unsqueeze(2).to_broadcast([P, 4, SP_]), ALU.mult).then_inc(decayed, 1)
    dve.wait_ge(mid_done, it + 1)
    for pair in range(2):
        dve.scalar_tensor_tensor(out=nxt[:, 1 + first, P * pair:P * (pair + 1)],
                                 in0=now[:, 1 + second, P * pair:P * (pair + 1)],
                                 scalar=ex[:, 268 + 2 * pair + second:269 + 2 * pair + second],
                                 in1=p_gla[second][:, pair, :], op0=ALU.mult, op1=ALU.add)
    dve.wait_ge(decayed, it + 1)
    dve.tensor_tensor(nxt[:, 0, :], nxt[:, 0, :], p_ssd[:, 0:256], ALU.add).then_inc(next_done, 1)


class Step:

    def __init__(self, it, use, buf, later, reused):
        self.it, self.use, self.buf, self.later, self.reused = it, use, buf, later, reused


def pipeline(eng, ahead, front, output, tail):
    def at(n):
        return Step(n, n // 2, n % 2, n >= 1, n >= 2)

    def turn(before, now, after):
        front(now, before)
        output(now, after)
        if after is not None:
            ahead(after)
        if before is not None:
            tail(before)

    ahead(at(0))
    turn(None, at(0), at(1))
    turn(at(0), at(1), at(2))
    with eng.Fori(0, LT // 2 - 2) as r:
        turn(Step(r * 2 + 1, r, 1, True, True), Step(r * 2 + 2, r + 1, 0, True, True), Step(r * 2 + 3, r + 1, 1, True, True))
        turn(Step(r * 2 + 2, r + 1, 0, True, True), Step(r * 2 + 3, r + 1, 1, True, True), Step(r * 2 + 4, r + 2, 0, True, True))
    turn(at(LT - 3), at(LT - 2), at(LT - 1))
    turn(at(LT - 2), at(LT - 1), None)
    front(None, at(LT - 1))
    tail(at(LT - 1))


def mixer(nc, A, C, route, tok_rec, feat_rec, back_state, fwd_state, x_mid, x_hat):
    mod, ident = C["mod"], C["ident"]
    FRONT = ["v", "v", "v", "v", "v", "v", "a", "v", "v", "v", "v", "v", "v", "v"]
    TAIL = ["a", "a", "v", "v", "a", "a", "v"]
    R_SC, R_BC, R_BT, R_AT, R_PI, R_PS, R_PG = 0, 2, 6, 7, 9, 11, 12
    R_MT, R_OP, R_XT, R_RT = 0, 2, 4, 6
    x_t = A["x"].rearrange("b (t p) d -> (b t) p d", p=P)
    xh_t = x_hat.rearrange("(t p) d -> t p d", p=P)
    with ExitStack() as ctx:
        sem = Names(nc, ctx, "mix")

        def sb(name, shape, dt=F32):
            return ctx.enter_context(nc.sbuf_tensor(f"{name}_m", shape, dt))

        def ps(name, shape):
            return ctx.enter_context(nc.psum_tensor(f"{name}_m", shape, F32))

        rec = [sb(f"rec{b}", [P, T_LEN]) for b in range(2)]
        feat = [sb(f"feat{b}", [P, F_TILES, P]) for b in range(2)]
        bst = [sb(f"bst{b}", [P, 3, 256]) for b in range(2)]
        xres = [sb(f"xres{b}", [P, D]) for b in range(2)]
        st = [sb(f"st{b}", [P, 3, 256]) for b in range(2)]
        w_out, w_rt = sb("w_out", [P, KT, D]), sb("w_rt", [P, KT, NE])
        gate_bc = sb("gate_bc", [P, D])
        nega, skip = sb("nega", [P, 2 * SH]), sb("skip", [P, SH])
        inv, mhalf = sb("inv", [P, 8]), sb("mhalf", [P, 8])
        dta, ex, a_sb = sb("dta", [P, 2 * SH]), sb("ex", [P, 288]), sb("a_sb", [P, 2 * SH])
        scm = sb("scm", [P, 2, 2, P])
        seg = [sb(f"seg{b}", [P, 4, P]) for b in range(2)]
        M = [sb(f"M{n}", [P, 4, P]) for n in range(4)]
        xd, xw, xD = sb("xd", [P, 2, SW]), sb("xw", [P, SW]), sb("xD", [P, SW])
        wend, kend = sb("wend", [P, SH]), sb("kend", [P, GQK])
        eb, enb, qd, ki = (sb(n, [P, 4, P]) for n in ("eb", "enb", "qd", "ki"))
        am = [sb(f"am{b}", [P, 4, P]) for b in range(2)]
        yi, y, junk = sb("yi", [P, 2, SW]), sb("y", [P, SW]), sb("junk", [P, D])
        m, mT = sb("m", [P, D]), sb("mT", [P, KT, P])
        x1 = [sb(f"x1{b}", [P, D]) for b in range(2)]
        xh = [sb(f"xh{b}", [P, D]) for b in range(2)]
        h2T = sb("h2T", [P, KT, P])
        ssm, ssx, rsx = sb("ssm", [P, 8]), sb("ssx", [P, 1]), sb("rsx", [P, 1])
        small, py = ps("small", [P, 512]), ps("py", [P, 512])
        po = [ps(f"po{b}", [P, 2, P]) for b in range(2)]
        fr = [ps(f"fr{b}", [P, 512]) for b in range(2)]
        tr = [ps(f"tr{b}", [P, 512]) for b in range(2)]

        rec_loaded, x_loaded = [sem(f"rec{b}_loaded") for b in range(2)], [sem(f"x{b}_loaded") for b in range(2)]
        x1_stored, xh_stored = [sem(f"x1{b}_stored") for b in range(2)], [sem(f"xh{b}_stored") for b in range(2)]
        (setup, a_exp, setup_done, gate_ps, gate_done, setup_pool, dta_done, small_ps, ex_done, a_copied, scm_done, seg_done,
         seg_exp, m_ready, eb_done, qk_done, xd_done, wend_done, xw_done, kend_done, xD_done, am_done, pi_done,
         decayed, mid_done, next_done, y_ps, o_ps, ysum1, ysum_done, y_raw, y_gated, sq_done, r_step, r_done, m_step, mix_done,
         xg_done, xadd_done, sx_done, rx_step, rx_done, xh_done, h2_done, log_done) = (sem(n) for n in (
             "setup", "a_exp", "setup_done", "gate_spread", "gate_done", "setup_pool", "dta_done", "small_product", "exp_done",
             "a_copied", "masked_scores", "seg_done", "seg_exp", "decayed_scores", "eb_done", "qk_decayed", "xd_done", "wend_done",
             "xw_done", "kend_done", "x_skip", "attn_masked", "inter_scaled", "decayed", "mid_state", "next_state", "y_product",
             "o_product", "y_sum1", "y_sum", "y_raw", "y_gated", "squares", "r_step", "r_done", "m_step", "mix_done", "x_gated",
             "x_added", "x_square", "rx_step", "rx_done", "xh_done", "h2T_done", "logits_done"))
        pool_held = sem("pool_held")
        pe_held = sem("pe_held")
        x_buf_free = sem("x_buffer_free")
        f_ps, t_ps = sem("front_product"), sem("tail_product")
        f_v, f_a, t_v, t_a = sem("front_freed_v"), sem("front_freed_a"), sem("tail_freed_v"), sem("tail_freed_a")
        block = ctx.enter_context(nc.Block())

        def count(rounds, n, who, it):
            return it * rounds.count(who) + rounds[:n + 1].count(who)

        def bank_free(pe, rounds, n, s, by_v, by_a):
            last = n - 2 if n >= 2 else max(i for i in range(len(rounds)) if i % 2 == n % 2)
            if n < 2 and not s.later:
                return
            it = s.it if n >= 2 else s.it - 1
            who = rounds[last]
            hold(pe, by_v if who == "v" else by_a, count(rounds, last, who, it), pe_held)

        @block.sync
        def _(sp):
            for k in range(KT):
                sp.dma_start(w_out[:, k, :], A["w_out"][0, k * P:(k + 1) * P, :]).then_inc(setup, 16)
            sp.dma_start(w_rt[:, :, :], A["w_router"].rearrange("(k p) e -> p k e", p=P)).then_inc(setup, 16)
            sp.dma_start(nega[:, 0:SH], A["a_log_f"].to_broadcast([P, SH])).then_inc(setup, 16)
            sp.dma_start(nega[:, SH:], A["a_log_b"].to_broadcast([P, SH])).then_inc(setup, 16)
            sp.dma_start(skip[:, :], A["d_skip"].to_broadcast([P, SH])).then_inc(setup, 16)
            sp.dma_start(st[0][:, :, :].rearrange("p a b -> p (a b)"), fwd_state[0]).then_inc(setup, 16)
            def ahead(s):
                if s.reused:
                    sp.wait_ge(mix_done, s.it - 1)
                sp.dma_start(rec[s.buf][:, :], tok_rec[s.it + CT]).then_inc(rec_loaded[s.buf], 16)
                sp.dma_start(feat[s.buf][:, :, :].rearrange("p a b -> p (a b)"), feat_rec[s.it + CT]).then_inc(rec_loaded[s.buf], 16)
                sp.dma_start(bst[s.buf][:, :, :].rearrange("p a b -> p (a b)"), back_state[s.it + CT]).then_inc(rec_loaded[s.buf], 16)
                if s.reused:
                    sp.wait_ge(xadd_done, s.it - 1)
                sp.dma_start(xres[s.buf][:, :], x_t[s.it]).then_inc(x_loaded[s.buf], 16)

            def none(*tiles):
                pass

            pipeline(sp, ahead, none, none, none)

        @block.gpsimd
        def _(pool):
            pool.sem_inc(x_buf_free, 1)
            pool.memset(mhalf[:, :], -0.5).then_inc(setup_pool, 1)
            pool.memset(inv[:, 0:4], 1.0 / GV).then_inc(setup_pool, 1)
            pool.memset(inv[:, 4:8], 1.0 / SW).then_inc(setup_pool, 1)
            pool.memset(ssm[:, :], 1.0).then_inc(setup_pool, 1)
            pool.wait_ge(setup_pool, 4)
            pool.wait_ge(setup, 16 * (KT + 5))

            def spread(out, x, by):
                return pool.tensor_tensor(out.rearrange("p (h c) -> p h c", h=SH), x.rearrange("p (h c) -> p h c", h=SH),
                                          by.unsqueeze(2).to_broadcast([P, SH, SP_]), ALU.mult)

            def ahead(s):
                r, it = rec[s.buf], s.it
                pool.wait_ge(rec_loaded[s.buf], s.use * 48 + 48)
                if s.later:
                    pool.wait_ge(y_ps, it)
                for d in range(2):
                    spread(xd[:, d, :], r[:, 0:SW], r[:, T_DT + SH * d:T_DT + SH * (d + 1)]).then_inc(xd_done, 1)
                spread(xD[:, :], r[:, 0:SW], skip[:, :]).then_inc(xD_done, 1)
                pool.wait_ge(ex_done, it + 1)
                pool.tensor_tensor(wend[:, :], ex[:, 256:264], r[:, T_DT:T_DT + SH], ALU.mult).then_inc(wend_done, 1)
                pool.tensor_tensor(kend[:, :], r[:, T_K:T_K + GQK], ex[:, 0:256], ALU.mult).then_inc(kend_done, 1)
                pool.wait_ge(wend_done, it + 1)
                spread(xw[:, :], r[:, 0:SW], wend[:, :]).then_inc(xw_done, 1)

            def front(now, s):
                if s is None:
                    return
                it = s.it
                pool.wait_ge(xg_done, it * 2 + 2)
                pool.wait_ge(x_loaded[s.buf], s.use * 16 + 16)
                pool.tensor_tensor(x1[s.buf][:, :], x1[s.buf][:, :], xres[s.buf][:, :], ALU.add).then_inc(xadd_done, 1)
                pool.wait_ge(sx_done, it + 1)
                if s.later:
                    hold(pool, xh_done, it, pool_held)
                pool.tensor_scalar(rsx[:, :], ssx[:, :], 1.0 / D, EPS, ALU.mult, ALU.add).then_inc(rx_step, 1)
                pool.wait_ge(rx_step, it + 1)
                pool.tensor_tensor(rsx[:, :], rsx[:, :], mhalf[:, 0:1], ALU.pow).then_inc(rx_done, 1)
                if s.later:
                    prior_use = s.use if s.buf == 1 else s.use - 1
                    pool.wait_ge(x1_stored[1 - s.buf], prior_use * 16 + 16)
                    pool.wait_ge(xh_stored[1 - s.buf], prior_use * 16 + 16)
                    pool.sem_inc(x_buf_free, 1)
                pool.dma_start(x_mid[it], x1[s.buf][:, :]).then_inc(x1_stored[s.buf], 16)

            def output(s, after):
                it = s.it
                pool.wait_ge(pi_done, it * 2 + 2)
                pool.wait_ge(xD_done, it + 1)
                pool.tensor_tensor(yi[:, 0, :], yi[:, 0, :], yi[:, 1, :], ALU.add).then_inc(ysum1, 1)
                pool.wait_ge(ysum1, it + 1)
                pool.tensor_tensor(yi[:, 0, :], yi[:, 0, :], xD[:, :], ALU.add).then_inc(ysum_done, 1)
                pool.wait_ge(sq_done, it * 5 + 5)
                pool.tensor_tensor(ssm[:, :], ssm[:, :], inv[:, :], ALU.mult).then_inc(r_step, 1)
                hold(pool, r_step, it * 2 + 1, pool_held)
                pool.tensor_scalar(ssm[:, :], ssm[:, :], EPS, None, ALU.add).then_inc(r_step, 1)
                pool.wait_ge(r_step, it * 2 + 2)
                pool.tensor_tensor(ssm[:, :], ssm[:, :], mhalf[:, :], ALU.pow).then_inc(r_done, 1)

            def tail(s):
                hold(pool, xh_done, s.it + 1, pool_held)
                pool.dma_start(xh_t[s.it], xh[s.buf][:, :]).then_inc(xh_stored[s.buf], 16)

            pipeline(pool, ahead, front, output, tail)
            for b in range(2):
                pool.wait_ge(x1_stored[b], 16 * (LT // 2))
                pool.wait_ge(xh_stored[b], 16 * (LT // 2))

        @block.scalar
        def _(act):
            act.wait_ge(setup, 16 * (KT + 5))
            act.activation(nega[:, :], nega[:, :], ACT.Exp).then_inc(a_exp, 1)

            def ahead(s):
                it = s.it
                act.wait_ge(small_ps, it + 1)
                if s.later:
                    act.wait_ge(next_done, it)
                act.activation(ex[:, :], small[:, 0:288], ACT.Exp).then_inc(ex_done, 1)
                act.activation(a_sb[:, :], small[:, 272:288], ACT.Copy).then_inc(a_copied, 1)

            def decays(s, r):
                act.wait_ge(seg_done, s.it * 4 + (r + 1))
                act.activation(seg[r % 2][:, :, :], seg[r % 2][:, :, :], ACT.Exp).then_inc(seg_exp, 1)

            def gains(s, n):
                act.wait_ge(t_ps, s.it * 7 + (n + 1))
                for j in range(4):
                    g = R_SG + j if n == 0 else R_GG
                    i = act.activation(mT[:, 4 * n + j, :], tr[n][:, P * j:P * (j + 1)], ACT.Copy,
                                       scale=C["cols"][:, g:g + 1])
                i.then_inc(t_a, 1)

            def front(now, before):
                for n in range(2):
                    if now is not None:
                        decays(now, n)
                    if before is not None:
                        gains(before, n)
                if now is not None:
                    it = now.it
                    decays(now, 2)
                    decays(now, 3)
                    act.wait_ge(f_ps, it * 14 + (R_BT + 1))
                    if now.later:
                        act.wait_ge(qk_done, it * 2)
                    act.activation(eb[:, :, :], fr[R_BT % 2][:, :].rearrange("p (a b) -> p a b", a=4), ACT.Exp).then_inc(eb_done, 1)
                    act.activation(enb[:, :, :], fr[R_BT % 2][:, :].rearrange("p (a b) -> p a b", a=4), ACT.Exp, scale=-1.0).then_inc(eb_done, 1)
                    act.wait_ge(eb_done, it * 2 + 2)
                    act.sem_inc(f_a, 1)
                if before is not None:
                    s, it = before, before.it
                    act.wait_ge(xadd_done, it + 1)
                    if s.later:
                        act.wait_ge(rx_step, it)
                    act.activation(junk[:, :], x1[s.buf][:, :], ACT.Square, accum_out=ssx[:, :]).then_inc(sx_done, 1)
                    act.wait_ge(rx_done, it + 1)
                    if s.later:
                        act.wait_ge(x_buf_free, it)
                    act.activation(xh[s.buf][:, :], x1[s.buf][:, :], ACT.Copy, scale=rsx[:, :]).then_inc(xh_done, 1)

            def output(s, after):
                it = s.it
                act.wait_ge(o_ps, it * 2 + 2)
                if s.later:
                    act.wait_ge(mix_done, it)
                    act.wait_ge(xh_done, it)
                for h in range(GH):
                    if h or s.later:
                        act.wait_ge(sq_done, it * 5 + h)
                    act.activation(junk[:, 0:GV], po[h % 2][:, h // 2, :], ACT.Square, accum_out=ssm[:, h:h + 1]).then_inc(sq_done, 1)
                act.wait_ge(y_gated, it + 1)
                act.wait_ge(sq_done, it * 5 + 4)
                act.activation(junk[:, 0:SW], y[:, :], ACT.Square, accum_out=ssm[:, 4:5]).then_inc(sq_done, 1)

            def tail(s):
                it = s.it
                if s.later:
                    act.wait_ge(log_done, it)
                for n in range(2):
                    act.wait_ge(t_ps, it * 7 + (R_XT + n + 1))
                    for j in range(4):
                        k = 4 * n + j
                        i = act.activation(h2T[:, k, :], tr[n][:, P * j:P * (j + 1)], ACT.Identity,
                                           scale=mod[:, 4 * KT + k, 0:1], bias=mod[:, 3 * KT + k, 0:1])
                    i.then_inc(t_a, 1)

            pipeline(act, ahead, front, output, tail)

        @block.tensor
        def _(pe):
            for j in range(KT):
                pe.matmul(tr[j // 4][:, P * (j % 4):P * (j % 4 + 1)], mod[:, 2 * KT + j, 0:1].to_broadcast([P, P]), ident[:, :],
                          start=True, stop=True).then_inc(gate_ps, 1)
            pe.wait_ge(gate_done, 2)
            pe.wait_ge(setup, 16 * (KT + 5))

            def ahead(s):
                it, r, f = s.it, rec[s.buf], feat[s.buf]
                pe.wait_ge(rec_loaded[s.buf], s.use * 48 + 48)
                pe.wait_ge(dta_done, it + 1)
                if s.later:
                    pe.wait_ge(a_copied, it)
                state_products(pe, C, 0, r, dta[:, 0:SH], small)
                pe.matmul(small[:, 272:280], C["le"][:, :], dta[:, 0:SH], start=True, stop=True)
                pe.matmul(small[:, 280:288], C["ge"][:, :], dta[:, SH:], start=True, stop=True).then_inc(small_ps, 1)
                for g in range(2):
                    bank_free(pe, FRONT, R_SC + g, s, f_v, f_a)
                    pe.matmul(fr[g][:, 0:P], f[64 * g:64 * g + 64, 0, :], f[64 * g:64 * g + 64, 1, :],
                              start=True, stop=True).then_inc(f_ps, 1)

            def sums(s, n):
                d, g = n // 2, n % 2
                bank_free(pe, FRONT, R_BC + n, s, f_v, f_a)
                for h in range(4):
                    c = SH * d + 4 * g + h
                    mm = pe.matmul(fr[g][:, P * h:P * (h + 1)], dta[:, c:c + 1].to_broadcast([P, P]),
                                   C["ge" if d else "le"][:, :], start=True, stop=True)
                mm.then_inc(f_ps, 1)

            def gate_sums(s):
                r = rec[s.buf]
                bank_free(pe, FRONT, R_BT, s, f_v, f_a)
                for d in range(2):
                    for pair in range(2):
                        c0 = T_GF + GQK * d + P * pair
                        mm = pe.matmul(fr[R_BT % 2][:, P * (2 * d + pair):P * (2 * d + pair + 1)], r[:, c0:c0 + P],
                                       C["ge_bd" if d else "le_bd"][:, :], start=True, stop=True)
                mm.then_inc(f_ps, 1)

            def turned(s):
                pe.wait_ge(mix_done, s.it + 1)
                for n in range(2):
                    bank_free(pe, TAIL, R_MT + n, s, t_v, t_a)
                    for j in range(4):
                        mm = pe.transpose(tr[n][:, P * j:P * (j + 1)], m[:, P * (4 * n + j):P * (4 * n + j + 1)], ident[:, :])
                    mm.then_inc(t_ps, 1)

            def project(s, n):
                if n == 0:
                    pe.wait_ge(t_a, s.it * 4 + 2)
                for k in range(KT):
                    mm = pe.matmul(tr[n][:, :], mT[:, k, :], w_out[:, k, 512 * n:512 * (n + 1)], start=(k == 0), stop=(k == KT - 1))
                mm.then_inc(t_ps, 1)

            def front(now, before):
                if now is not None:
                    sums(now, 0)
                    sums(now, 1)
                if before is not None:
                    turned(before)
                if now is not None:
                    sums(now, 2)
                if before is not None:
                    project(before, 0)
                if now is not None:
                    sums(now, 3)
                    gate_sums(now)
                if before is not None:
                    project(before, 1)

            def output(s, after):
                it, r, f = s.it, rec[s.buf], feat[s.buf]
                pe.wait_ge(qk_done, it * 2 + 2)
                for hh in range(2):
                    bank_free(pe, FRONT, R_AT + hh, s, f_v, f_a)
                    for dp in range(4):
                        mm = pe.matmul(fr[(R_AT + hh) % 2][:, P * dp:P * (dp + 1)], ki[64 * hh:64 * hh + 64, dp, :],
                                       qd[64 * hh:64 * hh + 64, dp, :], start=True, stop=True)
                    mm.then_inc(f_ps, 1)
                if s.later:
                    pe.wait_ge(next_done, it)
                for g in range(2):
                    bank_free(pe, FRONT, R_PI + g, s, f_v, f_a)
                    for d, h_in in enumerate((st[s.buf], bst[s.buf])):
                        mm = pe.matmul(fr[(R_PI + g) % 2][:, 256 * d:256 * d + 256], f[64 * g:64 * g + 64, 1, :],
                                       h_in[64 * g:64 * g + 64, 0, :], start=True, stop=True)
                    mm.then_inc(f_ps, 1)
                pe.wait_ge(xw_done, it + 1)
                bank_free(pe, FRONT, R_PS, s, f_v, f_a)
                for g in range(2):
                    mm = pe.matmul(fr[R_PS % 2][64 * g:64 * g + 64, 0:256], r[:, T_B + 64 * g:T_B + 64 * g + 64],
                                   xw[:, 256 * g:256 * g + 256], start=True, stop=True)
                mm.then_inc(f_ps, 1)
                pe.wait_ge(kend_done, it + 1)
                for c in range(2):
                    bank_free(pe, FRONT, R_PG + c, s, f_v, f_a)
                    for h in range(GH):
                        mm = pe.matmul(fr[(R_PG + c) % 2][64 * (h % 2):64 * (h % 2) + 64, P * (h // 2):P * (h // 2 + 1)],
                                       kend[64 * c:64 * c + 64, 64 * h:64 * h + 64],
                                       r[64 * c:64 * c + 64, T_V + GV * h:T_V + GV * (h + 1)], start=True, stop=True)
                    mm.then_inc(f_ps, 1)
                pe.wait_ge(m_ready, it * 4 + 4)
                pe.wait_ge(xd_done, it * 2 + 2)
                if s.later:
                    pe.wait_ge(y_raw, it)
                for h in range(SH):
                    for d in range(2):
                        mm = pe.matmul(py[:, 64 * h:64 * h + 64], M[2 * d + h // 4][:, h % 4, :], xd[:, d, 64 * h:64 * h + 64],
                                       start=(d == 0), stop=(d == 1))
                mm.then_inc(y_ps, 1)
                pe.wait_ge(am_done, it * 2 + 2)
                pe.wait_ge(mid_done, it + 1)
                if s.later:
                    pe.wait_ge(mix_done, it)
                for hh in range(2):
                    for pair in range(2):
                        h = 2 * pair + hh
                        for d in range(2):
                            pe.matmul(po[hh][:, pair, :], am[hh][:, 2 * d + pair, :], r[:, T_V + GV * h:T_V + GV * (h + 1)],
                                      start=(d == 0), stop=False, skip_group_check=True)
                        for d, s_in in enumerate((st[s.buf], bst[s.buf])):
                            for c in range(2):
                                mm = pe.matmul(po[hh][64 * c:64 * c + 64, pair, :],
                                               qd[64 * hh:64 * hh + 64, 2 * d + pair, 64 * c:64 * c + 64],
                                               s_in[64 * hh:64 * hh + 64, 1 + c, P * pair:P * (pair + 1)],
                                               start=False, stop=(d == 1), skip_group_check=True)
                    mm.then_inc(o_ps, 1)

            def tail(s):
                it = s.it
                pe.wait_ge(xh_done, it + 1)
                for n in range(2):
                    bank_free(pe, TAIL, R_XT + n, s, t_v, t_a)
                    for j in range(4):
                        mm = pe.transpose(tr[n][:, P * j:P * (j + 1)], xh[s.buf][:, P * (4 * n + j):P * (4 * n + j + 1)], ident[:, :])
                    mm.then_inc(t_ps, 1)
                pe.wait_ge(t_a, it * 4 + 4)
                for k in range(KT):
                    mm = pe.matmul(tr[R_RT % 2][:, 0:NE], h2T[:, k, :], w_rt[:, k, :], start=(k == 0), stop=(k == KT - 1))
                mm.then_inc(t_ps, 1)

            pipeline(pe, ahead, front, output, tail)

        @block.vector
        def _(dve):
            dve.wait_ge(a_exp, 1)
            dve.tensor_scalar(nega[:, :], nega[:, :], -1.0, None, ALU.mult).then_inc(setup_done, 1)
            for n in range(2):
                dve.wait_ge(gate_ps, KT)
                dve.tensor_copy(gate_bc[:, 512 * n:512 * n + 512], tr[n][:, :]).then_inc(gate_done, 1)
            dve.wait_ge(setup_done, 1)
            dve.wait_ge(gate_done, 2)
            dve.wait_ge(setup_pool, 4)
            incl = C["incl"]
            incl_bd = C["incl_bd"]

            def log_decays(s):
                dve.wait_ge(rec_loaded[s.buf], s.use * 48 + 48)
                dve.tensor_tensor(dta[:, :], rec[s.buf][:, T_DT:T_DT + 2 * SH], nega[:, :], ALU.mult).then_inc(dta_done, 1)

            def scores(s):
                for g in range(2):
                    dve.wait_ge(f_ps, s.it * 14 + (R_SC + g + 1))
                    dve.tensor_tensor(scm[:, :, g, :], fr[g][:, 0:P].unsqueeze(1).to_broadcast([P, 2, P]), incl[:, :, :],
                                      ALU.mult).then_inc(f_v, 1)

            def segment(s, n):
                it, d, g = s.it, n // 2, n % 2
                dve.wait_ge(f_ps, it * 14 + (R_BC + n + 1))
                if n == 0:
                    dve.wait_ge(a_copied, it + 1)
                if n >= 2:
                    dve.wait_ge(m_ready, it * 4 + (n - 1))
                for h in range(4):
                    c = SH * d + 4 * g + h
                    i = dve.tensor_scalar(seg[n % 2][:, h, :], fr[g][:, P * h:P * (h + 1)], a_sb[:, c:c + 1], 0.0,
                                          ALU.subtract, ALU.min)
                i.then_inc(seg_done, 1)
                dve.wait_ge(seg_done, it * 4 + (n + 1))
                dve.sem_inc(f_v, 1)

            def decay(s, n):
                it, d, g = s.it, n // 2, n % 2
                dve.wait_ge(seg_exp, it * 4 + (n + 1))
                if n == 0:
                    dve.wait_ge(f_v, it * 13 + 2)
                dve.tensor_tensor(M[n][:, :, :], seg[n % 2][:, :, :], scm[:, d, g, :].unsqueeze(1).to_broadcast([P, 4, P]),
                                  ALU.mult).then_inc(m_ready, 1)

            def decayed_qk(s):
                f = feat[s.buf]
                dve.wait_ge(eb_done, s.it * 2 + 2)
                for dst, e, lo in ((qd, eb, 2), (ki, enb, 4)):
                    src = f[:, lo:lo + 2, :].rearrange("p a b -> p (a b)").unsqueeze(1).to_broadcast([P, 2, 2 * P])
                    dve.tensor_tensor(dst[:, :, :].rearrange("p (d a) b -> p d (a b)", d=2), src,
                                      e[:, :, :].rearrange("p (d a) b -> p d (a b)", d=2), ALU.mult).then_inc(qk_done, 1)

            def gated(s, n):
                it = s.it
                if s.later and n == 0:
                    dve.wait_ge(x_buf_free, it)
                dve.wait_ge(t_ps, it * 7 + (R_OP + n + 1))
                dve.tensor_tensor(x1[s.buf][:, 512 * n:512 * n + 512], tr[n][:, :], gate_bc[:, 512 * n:512 * n + 512],
                                  ALU.mult).then_inc(xg_done, 1)
                dve.wait_ge(xg_done, it * 2 + (n + 1))
                dve.sem_inc(t_v, 1)

            def logits(it):
                dve.wait_ge(t_ps, it * 7 + (R_RT + 1))
                dve.tensor_copy(route["logits"][:, bass.ds(it, 1), :], tr[R_RT % 2][:, 0:NE].unsqueeze(1)).then_inc(log_done, 1)
                dve.wait_ge(log_done, it + 1)
                dve.sem_inc(t_v, 1)

            def front(now, before):
                if now is not None:
                    scores(now)
                if before is not None and before.later:
                    logits(before.it - 1)
                if now is not None:
                    segment(now, 0)
                    segment(now, 1)
                    decay(now, 0)
                    segment(now, 2)
                if before is not None:
                    gated(before, 0)
                if now is not None:
                    decay(now, 1)
                    segment(now, 3)
                    decay(now, 2)
                if before is not None:
                    gated(before, 1)
                if now is not None:
                    decay(now, 3)
                    decayed_qk(now)

            def output(s, after):
                it, r = s.it, rec[s.buf]
                for hh in range(2):
                    dve.wait_ge(f_ps, it * 14 + (R_AT + hh + 1))
                    mask = incl_bd[:, :, :].unsqueeze(2).to_broadcast([P, 2, 2, P])
                    dve.tensor_tensor(am[hh][:, :, :].rearrange("p (d a) b -> p d a b", d=2),
                                      fr[(R_AT + hh) % 2][:, :].rearrange("p (d a b) -> p d a b", d=2, a=2), mask,
                                      ALU.mult).then_inc(am_done, 1)
                    dve.wait_ge(am_done, it * 2 + (hh + 1))
                    dve.sem_inc(f_v, 1)
                for g in range(2):
                    dve.wait_ge(f_ps, it * 14 + (R_PI + g + 1))
                    ea = ex[:, 272:288].rearrange("p (d h) -> p d h", d=2)[:, :, 4 * g:4 * g + 4].unsqueeze(3).to_broadcast([P, 2, 4, SP_])
                    dve.tensor_tensor(yi[:, :, 256 * g:256 * g + 256].rearrange("p d (h c) -> p d h c", h=4),
                                      fr[(R_PI + g) % 2][:, :].rearrange("p (d h c) -> p d h c", d=2, h=4), ea,
                                      ALU.mult).then_inc(pi_done, 1)
                    dve.wait_ge(pi_done, it * 2 + (g + 1))
                    dve.sem_inc(f_v, 1)
                now, nxt = st[s.buf], st[1 - s.buf]
                dve.tensor_tensor(nxt[:, 0, :].rearrange("p (h c) -> p h c", h=4), now[:, 0, :].rearrange("p (h c) -> p h c", h=4),
                                  ex[:, 264:268].unsqueeze(2).to_broadcast([P, 4, SP_]), ALU.mult).then_inc(decayed, 1)
                dve.wait_ge(f_ps, it * 14 + (R_PS + 1))
                dve.wait_ge(decayed, it + 1)
                dve.tensor_tensor(nxt[:, 0, :], nxt[:, 0, :], fr[R_PS % 2][:, 0:256], ALU.add).then_inc(f_v, 1)
                for c in range(2):
                    dve.wait_ge(f_ps, it * 14 + (R_PG + c + 1))
                    if c:
                        dve.wait_ge(mid_done, it + 1)
                    to = now[:, 2, :] if c == 0 else nxt[:, 1, :]
                    for pair in range(2):
                        cs = slice(P * pair, P * (pair + 1))
                        i = dve.scalar_tensor_tensor(out=to[:, cs], in0=now[:, 1 + c, cs],
                                                     scalar=ex[:, 268 + 2 * pair + c:269 + 2 * pair + c],
                                                     in1=fr[(R_PG + c) % 2][:, cs], op0=ALU.mult, op1=ALU.add)
                    i.then_inc(next_done if c else mid_done, 1)
                    dve.wait_ge(next_done if c else mid_done, it + 1)
                    dve.sem_inc(f_v, 1)
                dve.wait_ge(y_ps, it + 1)
                dve.wait_ge(ysum_done, it + 1)
                dve.tensor_tensor(y[:, :], py[:, :], yi[:, 0, :], ALU.add).then_inc(y_raw, 1)
                dve.wait_ge(y_raw, it + 1)
                dve.tensor_tensor(y[:, :], y[:, :], r[:, T_Z:T_Z + SW], ALU.mult).then_inc(y_gated, 1)
                if after is not None:
                    log_decays(after)
                dve.wait_ge(r_done, it + 1)
                dve.tensor_scalar(m[:, 0:SW], y[:, :], ssm[:, 4:5], None, ALU.mult)
                for hh in range(2):
                    mo = m[:, SW:D].rearrange("p (a b c) -> p a b c", a=2, b=2)[:, :, hh, :]
                    rs = ssm[:, 0:4].rearrange("p (a b) -> p a b", b=2)[:, :, hh:hh + 1].to_broadcast([P, 2, P])
                    dve.tensor_tensor(mo, po[hh][:, :, :], rs, ALU.mult).then_inc(m_step, 1)
                dve.wait_ge(m_step, it * 2 + 2)
                dve.tensor_tensor(m[:, SW:D], m[:, SW:D], r[:, T_GO:T_GO + GW], ALU.mult).then_inc(mix_done, 1)

            def none(s):
                pass

            def first(s):
                if not s.later:
                    log_decays(s)

            pipeline(dve, first, front, output, none)
            logits(LT - 1)


TAB = MAXB + 4
PL_ORDER, PL_PAR, PL_NEXT, PL_LOAD, PL_PAIRS = 0, TAB, 2 * TAB, 3 * TAB, 4 * TAB
PL_FIRST = PL_PAIRS + 1
PL_LEN = PL_FIRST + 1


def slots(nc, A, C, route, slot_tok):
    logits, plan = route["logits"], route["plan"]
    with ExitStack() as ctx:
        sem = Names(nc, ctx, "slt")

        def sb(name, shape, dt=F32):
            return ctx.enter_context(nc.sbuf_tensor(f"{name}_r", shape, dt))

        def ps(name, shape):
            return ctx.enter_context(nc.psum_tensor(f"{name}_r", shape, F32))

        s, sel, selm, eq = (sb(n, [P, LT, NE]) for n in ("sig", "sel", "selm", "eq"))
        hot = [sb(f"hot{j}", [P, LT, NE]) for j in range(2)]
        both, base = sb("both", [P, LT, NE]), sb("base", [P, LT, NE])
        bias = sb("bias", [P, NE])
        hi, lo = sb("hi", [P, LT * NG, 2]), sb("lo", [P, LT * NG, 2])
        gscore, geq, goff = (sb(n, [P, LT, NG]) for n in ("gscore", "geq", "goff"))
        t1, t2 = sb("t1", [P, LT * NG]), sb("t2", [P, LT * NG])
        down_g, down_e = sb("down_g", [P, NG]), sb("down_e", [P, NE])
        best = sb("best", [P, LT])
        wsum = sb("wsum", [P, LT])
        prior = sb("prior", [P, LT + 1, NE])
        limits = sb("limits", [P, 16])
        over = sb("over", [P, NE, 16])
        nblk, bend, bstart = sb("nblk", [P, NE]), sb("bend", [P, NE]), sb("bstart", [P, NE])
        diag, ncol, lec = sb("diag", [NE, NE]), sb("ncol", [NE, 1]), sb("lec", [NE, NE])
        past, ends = sb("past", [1, TAB, NE]), sb("ends", [1, TAB, NE])
        held = sb("held", [1, NE])
        blk, eb, order, end = (sb(n, [1, TAB]) for n in ("blk", "eb", "order", "end"))
        due, more = sb("due", [1, TAB]), sb("more", [1, TAB])
        last = sb("last", [1, 1])
        bnum = sb("bnum", [1, TAB])
        npf = sb("npf", [1, MAXB // 2])
        slot_f = sb("slot_f", [P, LT, 2])
        zero_i = sb("zero_i", [P, TAB * 16], I32)
        tok_id = sb("tok_id", [P, LT, 16], I32)
        excl, tot, pb = ps("excl", [P, LT, NE]), ps("tot", [P, LT, NE]), ps("pb", [P, 512])
        bias_loaded, made, sig_done, both_done, ranks_ps, lec_done, bend_ps, slot_done, cleared, scattered, chain = (
            sem(n) for n in ("bias_loaded", "made", "sigmoid_done", "both_done", "ranks_product", "lec_done", "bend_product",
                             "slots_done", "table_cleared", "scattered", "chain"))
        block = ctx.enter_context(nc.Block())

        @block.sync
        def _(sp):
            sp.dma_start(bias[:, :], A["router_bias"].rearrange("(a e) -> a e", a=1).to_broadcast([P, NE])).then_inc(bias_loaded, 16)

        @block.scalar
        def _(act):
            act.activation(s[:, :, :], logits[:, :, :], ACT.Sigmoid).then_inc(sig_done, 1)

        @block.tensor
        def _(pe):
            pe.wait_ge(both_done, 1)
            pe.matmul(excl[:, :, :], C["lt"][:, :], both[:, :, :], start=True, stop=True)
            pe.matmul(tot[:, :, :], C["ones"][:, :], both[:, :, :], start=True, stop=True).then_inc(ranks_ps, 1)
            pe.wait_ge(lec_done, 1)
            pe.matmul(pb[:, 0:NE], C["ones"][0:NE, :], lec[:, :], start=True, stop=True).then_inc(bend_ps, 1)

        @block.gpsimd
        def _(pool):
            pool.iota(down_g[:, :], pattern=[[-1, NG]], base=NG, channel_multiplier=0,
                      allow_small_or_imprecise_dtypes=True).then_inc(made, 1)
            pool.iota(down_e[:, :], pattern=[[-1, NE]], base=NE, channel_multiplier=0,
                      allow_small_or_imprecise_dtypes=True).then_inc(made, 1)
            pool.iota(limits[:, :], pattern=[[P, 16]], base=0, channel_multiplier=0,
                      allow_small_or_imprecise_dtypes=True).then_inc(made, 1)
            pool.iota(bnum[:, :], pattern=[[1, TAB]], base=0, channel_multiplier=0,
                      allow_small_or_imprecise_dtypes=True).then_inc(made, 1)
            pool.iota(tok_id[:, :, :], pattern=[[P, LT], [0, 16]], base=0, channel_multiplier=1).then_inc(made, 1)
            pool.memset(zero_i[:, :], 0).then_inc(made, 1)
            pool.wait_ge(made, 6)
            pool.dma_start(slot_tok.rearrange("(b p) c -> p b c", p=P), zero_i[:, :].rearrange("p (b c) -> p b c", c=16)).then_inc(cleared, 16)
            pool.wait_ge(cleared, 16)
            pool.wait_ge(slot_done, 1)
            for t in range(LT):
                for j in range(2):
                    pool.indirect_dma_start(out=slot_tok, out_offset=bass.IndirectOffsetOnAxis(ap=route["slot"][:, t, j:j + 1], axis=0),
                                            in_=tok_id[:, t, :], in_offset=None).then_inc(scattered, 16)
            pool.wait_ge(scattered, 16 * 2 * LT)

        @block.vector
        def _(dve):
            done = [0]

            def then(ins):
                done[0] += 1
                ins.then_inc(chain, 1)
                dve.wait_ge(chain, done[0])

            def over_e(x):
                return x.unsqueeze(2).to_broadcast([P, LT, NE])

            dve.wait_ge(made, 6)
            dve.wait_ge(bias_loaded, 16)
            dve.wait_ge(sig_done, 1)
            then(dve.tensor_tensor(sel[:, :, :], s[:, :, :], bias[:, :].unsqueeze(1).to_broadcast([P, LT, NE]), ALU.add))
            g4 = sel[:, :, :].rearrange("p t (g e) -> p (t g) e", e=EG)
            then(dve.tensor_tensor(hi[:, :, :], g4[:, :, 0:2], g4[:, :, 2:4], ALU.max))
            then(dve.tensor_tensor(lo[:, :, :], g4[:, :, 0:2], g4[:, :, 2:4], ALU.min))
            then(dve.tensor_tensor(t1[:, :], hi[:, :, 0], hi[:, :, 1], ALU.min))
            then(dve.tensor_tensor(t2[:, :], lo[:, :, 0], lo[:, :, 1], ALU.max))
            then(dve.tensor_tensor(t1[:, :], t1[:, :], t2[:, :], ALU.max))
            then(dve.tensor_tensor(t2[:, :], hi[:, :, 0], hi[:, :, 1], ALU.max))
            gs = gscore[:, :, :].rearrange("p t g -> p (t g)")
            then(dve.tensor_tensor(gs, t1[:, :], t2[:, :], ALU.add))
            then(dve.tensor_reduce(best[:, :], gscore[:, :, :], AX, ALU.max))
            bg = best[:, :].unsqueeze(2).to_broadcast([P, LT, NG])
            then(dve.tensor_tensor(geq[:, :, :], gscore[:, :, :], bg, ALU.is_equal))
            then(dve.tensor_tensor(geq[:, :, :], geq[:, :, :], down_g[:, :].unsqueeze(1).to_broadcast([P, LT, NG]), ALU.mult))
            then(dve.tensor_reduce(best[:, :], geq[:, :, :], AX, ALU.max))
            then(dve.tensor_tensor(geq[:, :, :], geq[:, :, :], bg, ALU.is_equal))
            then(dve.tensor_scalar(goff[:, :, :], geq[:, :, :], -1.0, BIG, ALU.add, ALU.mult))
            in_group = geq[:, :, :].rearrange("p t g -> p (t g)").unsqueeze(2).to_broadcast([P, LT * NG, EG])
            off_group = goff[:, :, :].rearrange("p t g -> p (t g)").unsqueeze(2).to_broadcast([P, LT * NG, EG])
            sm4 = selm[:, :, :].rearrange("p t (g e) -> p (t g) e", e=EG)
            then(dve.tensor_tensor(sm4, g4, in_group, ALU.mult))
            then(dve.tensor_tensor(sm4, sm4, off_group, ALU.add))
            for j in range(2):
                then(dve.tensor_reduce(best[:, :], selm[:, :, :], AX, ALU.max))
                then(dve.tensor_tensor(eq[:, :, :], selm[:, :, :], over_e(best[:, :]), ALU.is_equal))
                then(dve.tensor_tensor(eq[:, :, :], eq[:, :, :], down_e[:, :].unsqueeze(1).to_broadcast([P, LT, NE]), ALU.mult))
                then(dve.tensor_reduce(best[:, :], eq[:, :, :], AX, ALU.max))
                then(dve.tensor_tensor(hot[j][:, :, :], eq[:, :, :], over_e(best[:, :]), ALU.is_equal))
                if j == 0:
                    then(dve.scalar_tensor_tensor(out=selm[:, :, :], in0=hot[0][:, :, :], scalar=-2.0 * BIG, in1=selm[:, :, :],
                                                  op0=ALU.mult, op1=ALU.add))
            dve.tensor_tensor(both[:, :, :], hot[0][:, :, :], hot[1][:, :, :], ALU.add).then_inc(both_done, 1)
            for j in range(2):
                then(dve.tensor_tensor(eq[:, :, :], hot[j][:, :, :], s[:, :, :], ALU.mult))
                then(dve.tensor_reduce(route["gate"][:, :, j], eq[:, :, :], AX, ALU.add))
            then(dve.tensor_tensor(wsum[:, :], route["gate"][:, :, 0], route["gate"][:, :, 1], ALU.add))
            then(dve.reciprocal(wsum[:, :], wsum[:, :]))
            then(dve.tensor_tensor(route["gate"][:, :, :], route["gate"][:, :, :], wsum[:, :].unsqueeze(2).to_broadcast([P, LT, 2]), ALU.mult))
            then(dve.memset(prior[:, 0, :], 0.0))
            dve.wait_ge(ranks_ps, 1)
            for t in range(LT):
                then(dve.tensor_tensor(prior[:, t + 1, :], prior[:, t, :], tot[:, t, :], ALU.add))
            then(dve.tensor_tensor(over[:, :, :], prior[:, LT, :].unsqueeze(2).to_broadcast([P, NE, 16]),
                                   limits[:, :].unsqueeze(1).to_broadcast([P, NE, 16]), ALU.is_gt))
            then(dve.tensor_reduce(nblk[:, :], over[:, :, :], AX, ALU.add))
            then(dve.tensor_tensor(diag[:, :], nblk[0:NE, :], C["ident"][0:NE, 0:NE], ALU.mult))
            then(dve.tensor_reduce(ncol[:, :], diag[:, :], AX, ALU.add))
            dve.tensor_scalar(lec[:, :], C["le"][0:NE, 0:NE], ncol[:, :], None, ALU.mult).then_inc(lec_done, 1)
            dve.wait_ge(bend_ps, 1)
            then(dve.tensor_copy(bend[:, :], pb[:, 0:NE]))
            then(dve.tensor_tensor(bstart[:, :], bend[:, :], nblk[:, :], ALU.subtract))
            then(dve.tensor_scalar(bstart[:, :], bstart[:, :], float(P), None, ALU.mult))
            then(dve.tensor_tensor(base[:, :, :], excl[:, :, :], prior[:, 0:LT, :], ALU.add))
            then(dve.tensor_tensor(base[:, :, :], base[:, :, :], bstart[:, :].unsqueeze(1).to_broadcast([P, LT, NE]), ALU.add))
            for j in range(2):
                then(dve.tensor_tensor(eq[:, :, :], hot[j][:, :, :], base[:, :, :], ALU.mult))
                then(dve.tensor_reduce(slot_f[:, :, j], eq[:, :, :], AX, ALU.add))
            then(dve.tensor_copy(route["slot"][:, :, :], slot_f[:, :, :]))
            dve.sem_inc(slot_done, 1)
            def by_block(x):
                return x.unsqueeze(2).to_broadcast([1, TAB, NE])

            def by_expert(x):
                return x.unsqueeze(1).to_broadcast([1, TAB, NE])
            then(dve.tensor_scalar(last[:, :], bend[0:1, NE - 1:NE], -1.0, None, ALU.add))
            then(dve.tensor_tensor(blk[:, :], bnum[:, :], last[:, :].to_broadcast([1, TAB]), ALU.min))
            then(dve.tensor_tensor(past[:, :, :], by_block(blk[:, :]), by_expert(bend[0:1, :]), ALU.is_ge))
            then(dve.tensor_reduce(eb[:, :], past[:, :, :], AX, ALU.add))
            then(dve.tensor_scalar(ends[:, :, :], past[:, :, :], float(8 * MAXB), None, ALU.mult))
            then(dve.tensor_tensor(ends[:, :, :], ends[:, :, :], by_expert(bend[0:1, :]), ALU.add))
            then(dve.tensor_reduce(end[:, :], ends[:, :, :], AX, ALU.min))
            then(dve.tensor_scalar(held[:, :], nblk[0:1, :], 0.0, None, ALU.is_gt))
            then(dve.tensor_tensor(past[:, :, :], past[:, :, :], by_expert(held[:, :]), ALU.mult))
            then(dve.tensor_reduce(order[:, :], past[:, :, :], AX, ALU.add))
            then(dve.tensor_tensor(past[:, :, :], by_block(end[:, :]), by_expert(bend[0:1, :]), ALU.is_ge))
            then(dve.tensor_reduce(more[:, :], past[:, :, :], AX, ALU.add))
            then(dve.tensor_scalar(more[:, :], more[:, :], float(NE - 1), None, ALU.min))
            then(dve.tensor_copy(plan[:, PL_NEXT:PL_NEXT + TAB], more[:, :]))
            then(dve.memset(due[:, 0:1], 1.0))
            then(dve.tensor_tensor(due[:, 1:TAB], eb[:, 1:TAB], eb[:, 0:TAB - 1], ALU.not_equal))
            then(dve.tensor_tensor(more[:, :], end[:, :], bend[0:1, NE - 1:NE].to_broadcast([1, TAB]), ALU.is_lt))
            then(dve.tensor_tensor(due[:, :], due[:, :], more[:, :], ALU.mult))
            then(dve.tensor_copy(plan[:, PL_LOAD:PL_LOAD + TAB], due[:, :]))
            then(dve.tensor_copy(plan[:, PL_ORDER:PL_ORDER + TAB], order[:, :]))
            then(dve.tensor_scalar(plan[:, PL_PAR:PL_PAR + TAB], plan[:, PL_ORDER:PL_ORDER + TAB], 1, None, ALU.bitwise_and))
            then(dve.tensor_copy(plan[:, PL_FIRST:PL_FIRST + 1], eb[:, 0:1]))
            then(dve.tensor_tensor(npf[:, :], bnum[:, 0:MAXB].rearrange("p (a b) -> p a b", b=2)[:, :, 0],
                                   bend[0:1, NE - 1:NE].to_broadcast([1, MAXB // 2]), ALU.is_lt))
            then(dve.tensor_reduce(eb[:, 0:1], npf[:, :], AX, ALU.add))
            then(dve.tensor_copy(plan[:, PL_PAIRS:PL_PAIRS + 1], eb[:, 0:1]))


def experts(nc, A, C, route, slot_tok, x_hat, y_slots):
    mod, ident, plan = C["mod"], C["ident"], route["plan"]
    KF = FF // P
    tok_b = slot_tok.rearrange("(b p) c -> b p c", p=P)
    y_b = y_slots.rearrange("(b p) d -> b p d", p=P)
    with ExitStack() as ctx:
        sem = Names(nc, ctx, "exp")

        def sb(name, shape, dt=F32):
            return ctx.enter_context(nc.sbuf_tensor(f"{name}_e", shape, dt))

        def ps(name, shape):
            return ctx.enter_context(nc.psum_tensor(f"{name}_e", shape, F32))

        wg, wu, wd = sb("wg", [P, 2, KT, FF]), sb("wu", [P, 2, KT, FF]), sb("wd", [P, 2, KF, D])
        toks = sb("toks", [P, TAB, 16], I32)
        idx = [sb(f"idx{b}", [P, 1], I32) for b in range(2)]
        xg = [sb(f"xg{b}", [P, D]) for b in range(2)]
        xT = [sb(f"xT{b}", [P, KT, P]) for b in range(2)]
        hs, h, hT = sb("hs", [P, FF]), sb("h", [P, FF]), sb("hT", [P, KF, P])
        yb = [sb(f"yb{b}", [P, D]) for b in range(2)]
        gate_bc, zero = sb("gate_bc", [P, D]), sb("zero", [P, D])
        pool_held, sync_held = sem("pool_held"), sem("sync_held")
        zero_done, zeros_stored = sem("zero_done"), sem("zeros_stored")
        tx = [ps(f"tx{b}", [P, 512]) for b in range(2)]
        pg, pu, ph = ps("pg", [P, 512]), ps("pu", [P, 512]), ps("ph", [P, 512])
        pd = [ps(f"pd{b}", [P, 512]) for b in range(2)]
        w_loaded = [sem(f"{n}_loaded") for n in ("gates", "ups", "downs")]
        toks_loaded, idx_ready = sem("toks_loaded"), sem("idx_ready")
        gathered = [sem(f"x{b}_gathered") for b in range(2)]
        stored = [sem(f"y{b}_stored") for b in range(2)]
        (gate_ps, gate_done, xt_ps, xt_done, gp_ps, up_ps, silu_done, h_done, ht_ps, ht_done, dn_ps, y_done,
         y_free) = (sem(n) for n in ("gate_spread", "gate_done", "x_transposed", "xT_done", "gate_product", "up_product",
                                     "silu_done", "h_done", "h_transposed", "hT_done", "down_product", "y_done",
                                     "y_buffer_free"))
        block = ctx.enter_context(nc.Block())
        first = plan[0:1, PL_PAIRS:PL_PAIRS + 1]

        def entry(eng, b, table, most):
            return eng.value_load(plan[0:1, bass.ds(b + table, 1)], min_val=0, max_val=most)

        def pairs(eng, body, unused=None):
            n = eng.value_load(first, min_val=1, max_val=MAXB // 2)
            with eng.Fori(0, MAXB // 2) as r:
                with eng.If(r < n):
                    for u in range(2):
                        body(r, u)
                if unused is not None:
                    with eng.Else():
                        for u in range(2):
                            unused(r, u)
            return n

        @block.sync
        def _(sp):
            def load(n, e, place):
                w = (wg, wu, wd)[n]
                sp.dma_start(w[:, place, :, :], A[("w_gate", "w_up", "w_down")[n]][0][e].rearrange("(k p) f -> p k f", p=P)).then_inc(w_loaded[n], 16)

            sp.wait_ge(zero_done, 1)
            sp.wait_ge(toks_loaded, 16)
            first = sp.value_load(plan[0:1, PL_FIRST:PL_FIRST + 1], min_val=0, max_val=NE - 1)
            for n in range(3):
                load(n, first, 0)

            def body(r, u):
                b = r * 2 + u
                sp.sem_inc(zeros_stored, 16)
                with sp.If(entry(sp, b, PL_LOAD, 1) > 0):
                    order, par, e = entry(sp, b, PL_ORDER, NE - 1), entry(sp, b, PL_PAR, 1), entry(sp, b, PL_NEXT, NE - 1)
                    for n, (done, value) in enumerate(((gp_ps, b + 1), (up_ps, b + 1), (y_done, b * 2 + 2))):
                        hold(sp, w_loaded[n], order * 16 + 16, sync_held)
                        hold(sp, done, value, sync_held)
                        load(n, e, bass.ds(1 - par, 1))
            def unused(r, u):
                sp.dma_start(y_b[r * 2 + u], zero[:, :]).then_inc(zeros_stored, 16)
            pairs(sp, body, unused)
            sp.wait_ge(zeros_stored, MAXB * 16)

        @block.gpsimd
        def _(pool):
            def fetch(b, use, u):
                pool.tensor_copy(idx[u][:, :], toks[:, bass.ds(b, 1), 0]).then_inc(idx_ready, 1)
                hold(pool, idx_ready, b + 1, pool_held)
                pool.indirect_dma_start(out=xg[u][:, :], out_offset=None, in_=x_hat,
                                        in_offset=bass.IndirectOffsetOnAxis(ap=idx[u][:, 0:1], axis=0)).then_inc(gathered[u], 16)
            pool.memset(zero[:, :], 0.0).then_inc(zero_done, 1)
            pool.wait_ge(zero_done, 1)
            pool.dma_start(toks[:, :, :], slot_tok.rearrange("(b p) c -> p b c", p=P)).then_inc(toks_loaded, 16)
            pool.wait_ge(toks_loaded, 16)
            fetch(0, 0, 0)
            fetch(1, 0, 1)
            for b in range(2, 4):
                pool.wait_ge(xt_ps, 2 * b - 2)
                pool.wait_ge(gathered[b % 2], 16)
                fetch(b, 1, b % 2)

            def body(r, u):
                b = r * 2 + u
                hold(pool, xt_ps, b * 2 + 6, pool_held)
                hold(pool, gathered[u], r * 16 + 32, pool_held)
                fetch(b + 4, r + 2, u)
                hold(pool, y_done, r * 4 + 2 * (u + 2), pool_held)
                pool.dma_start(y_b[r * 2 + u], yb[u][:, :]).then_inc(stored[u], 16)
                pool.wait_ge(stored[u], r * 16 + 16)
                pool.sem_inc(y_free, 1)

            n = pairs(pool, body)
            for u in range(2):
                pool.wait_ge(gathered[u], n * 16 + 32)
                pool.wait_ge(stored[u], n * 16)

        @block.scalar
        def _(act):
            act.sem_inc(y_free, 2)

            def features(b, u):
                for q in range(2):
                    act.wait_ge(xt_ps, b * 2 + (q + 1))
                    for j in range(4):
                        k = 4 * q + j
                        i = act.activation(xT[u][:, k, :], tx[q][:, P * j:P * (j + 1)], ACT.Identity,
                                           scale=mod[:, 4 * KT + k, 0:1], bias=mod[:, 3 * KT + k, 0:1])
                    i.then_inc(xt_done, 1)
            features(0, 0)
            features(1, 1)

            def body(r, u):
                b = r * 2 + u
                act.wait_ge(gp_ps, b + 2)
                act.wait_ge(h_done, b + 1)
                act.activation(hs[:, :], pg[:, :], ACT.Silu).then_inc(silu_done, 1)
                features(b + 2, u)
            pairs(act, body)

        @block.tensor
        def _(pe):
            for j in range(KT):
                pe.matmul(pd[j // 4][:, P * (j % 4):P * (j % 4 + 1)], mod[:, 5 * KT + j, 0:1].to_broadcast([P, P]), ident[:, :],
                          start=True, stop=True).then_inc(gate_ps, 1)
            pe.wait_ge(gate_done, 2)

            def turn(b, use, u, peeled=False):
                pe.wait_ge(gathered[u], use * 16 + 16)
                for q in range(2):
                    if not peeled:
                        pe.wait_ge(xt_done, b * 2 + (q - 1))
                    for j in range(4):
                        mm = pe.transpose(tx[q][:, P * j:P * (j + 1)], xg[u][:, P * (4 * q + j):P * (4 * q + j + 1)], ident[:, :])
                    mm.then_inc(xt_ps, 1)

            def place(b):
                return entry(pe, b, PL_PAR, 1), entry(pe, b, PL_ORDER, NE - 1)

            def wide(u, at, n, w, acc, ready):
                par, order = at
                pe.wait_ge(w_loaded[n], order * 16 + 16)
                for k in range(KT):
                    mm = pe.matmul(acc[:, :], xT[u][:, k, :], w[:, bass.ds(par, 1), k, :], start=(k == 0), stop=(k == KT - 1))
                mm.then_inc(ready, 1)

            pe.sem_inc(gp_ps, 1)
            pe.sem_inc(up_ps, 1)
            turn(0, 0, 0, True)
            turn(1, 0, 1)
            pe.wait_ge(xt_done, 2)
            wide(0, place(0), 0, wg, pg, gp_ps)

            def body(r, u):
                b = r * 2 + u
                here, after = place(b), place(b + 1)
                wide(u, here, 1, wu, pu, up_ps)
                pe.wait_ge(silu_done, b + 1)
                pe.wait_ge(xt_done, b * 2 + 4)
                wide(1 - u, after, 0, wg, pg, gp_ps)
                pe.wait_ge(h_done, b + 2)
                for j in range(KF):
                    mm = pe.transpose(ph[:, P * j:P * (j + 1)], h[:, P * j:P * (j + 1)], ident[:, :])
                mm.then_inc(ht_ps, 1)
                turn(b + 2, r + 1, u)
                pe.wait_ge(ht_done, b + 1)
                pe.wait_ge(y_done, b * 2 + 2)
                par, order = here
                pe.wait_ge(w_loaded[2], order * 16 + 16)
                for n in range(2):
                    for k in range(KF):
                        mm = pe.matmul(pd[n][:, :], hT[:, k, :], wd[:, bass.ds(par, 1), k, 512 * n:512 * (n + 1)],
                                       start=(k == 0), stop=(k == KF - 1))
                    mm.then_inc(dn_ps, 1)
            pairs(pe, body)

        @block.vector
        def _(dve):
            for n in range(2):
                dve.wait_ge(gate_ps, KT)
                dve.tensor_copy(gate_bc[:, 512 * n:512 * n + 512], pd[n][:, :]).then_inc(gate_done, 1)
            dve.wait_ge(gate_done, 2)
            dve.sem_inc(y_done, 2)
            dve.sem_inc(h_done, 1)

            def body(r, u):
                b = r * 2 + u
                dve.wait_ge(up_ps, b + 2)
                dve.wait_ge(silu_done, b + 1)
                dve.tensor_tensor(h[:, :], pu[:, :], hs[:, :], ALU.mult).then_inc(h_done, 1)
                dve.wait_ge(ht_ps, b + 1)
                dve.tensor_copy(hT[:, :, :], ph[:, :].rearrange("p (k c) -> p k c", k=KF)).then_inc(ht_done, 1)
                dve.wait_ge(y_free, b + 1)
                for n in range(2):
                    dve.wait_ge(dn_ps, b * 2 + (n + 1))
                    dve.tensor_tensor(yb[u][:, 512 * n:512 * n + 512], pd[n][:, :], gate_bc[:, 512 * n:512 * n + 512],
                                      ALU.mult).then_inc(y_done, 1)
            pairs(dve, body)


def combine(nc, A, C, route, y_slots, x_mid, out):
    out_t = out.rearrange("b (t p) d -> (b t) p d", p=P)
    with ExitStack() as ctx:
        sem = Names(nc, ctx, "cmb")

        def sb(name, shape, dt=F32):
            return ctx.enter_context(nc.sbuf_tensor(f"{name}_c", shape, dt))

        idx = [sb(f"idx{b}", [P, 2], I32) for b in range(2)]
        gates = [sb(f"gates{b}", [P, 2]) for b in range(2)]
        yr = [[sb(f"y{b}{j}", [P, D]) for j in range(2)] for b in range(2)]
        xr = [sb(f"x{b}", [P, D]) for b in range(2)]
        o = [sb(f"o{b}", [P, D]) for b in range(2)]
        junk, fg = sb("junk", [P, D]), sb("fg", [P, D])
        ss = [sb(f"ss{b}", [P, 1]) for b in range(2)]
        mhalf = sb("mhalf", [P, 1])
        sp_held = sem("sp_held")
        pool_held = sem("pool_held")
        x_loaded, gathered, stored = ([sem(f"{n}{b}") for b in range(2)] for n in ("x_loaded", "gathered", "stored"))
        (fg_loaded, half_done, idx_done, added, sum_done, ss_done, r_step, r_done, o_done, o_free) = (sem(n) for n in (
            "fg_loaded", "half_done", "idx_done", "added", "sum_done", "ss_done", "r_step", "r_done", "o_done", "o_free"))
        block = ctx.enter_context(nc.Block())

        def tiles(eng, body):
            with eng.Fori(0, LT // 2 - 1) as r:
                for u in range(2):
                    body(r, u, True)
            for u in range(2):
                body(LT // 2 - 1, u, False)

        @block.sync
        def _(sp):
            sp.dma_start(fg[:, :], A["final_norm_g"].rearrange("(a d) -> a d", a=1).to_broadcast([P, D])).then_inc(fg_loaded, 16)
            sp.sem_inc(o_free, 2)
            for u in range(2):
                sp.dma_start(xr[u][:, :], x_mid[u]).then_inc(x_loaded[u], 16)

            def body(r, u, more):
                it = r * 2 + u
                hold(sp, o_done, it + 1, sp_held)
                if more:
                    sp.dma_start(xr[u][:, :], x_mid[it + 2]).then_inc(x_loaded[u], 16)
                sp.dma_start(out_t[it], o[u][:, :]).then_inc(stored[u], 16)
                sp.wait_ge(stored[u], r * 16 + 16)
                sp.sem_inc(o_free, 1)
            tiles(sp, body)

        @block.gpsimd
        def _(pool):
            pool.memset(mhalf[:, :], -0.5).then_inc(half_done, 1)
            pool.wait_ge(half_done, 1)

            def gather(it, u):
                hold(pool, idx_done, it + 1, pool_held)
                for j in range(2):
                    pool.indirect_dma_start(out=yr[u][j][:, :], out_offset=None, in_=y_slots,
                                            in_offset=bass.IndirectOffsetOnAxis(ap=idx[u][:, j:j + 1], axis=0)).then_inc(gathered[u], 16)

            for u in range(2):
                gather(u, u)

            def body(r, u, more):
                it = r * 2 + u
                hold(pool, ss_done, it + 1, pool_held)
                pool.tensor_scalar(ss[u][:, :], ss[u][:, :], 1.0 / D, EPS, ALU.mult, ALU.add).then_inc(r_step, 1)
                pool.wait_ge(r_step, it + 1)
                pool.tensor_tensor(ss[u][:, :], ss[u][:, :], mhalf[:, :], ALU.pow).then_inc(r_done, 1)
                if more:
                    gather(it + 2, u)
            tiles(pool, body)

        @block.scalar
        def _(act):
            def body(r, u, more):
                it = r * 2 + u
                act.wait_ge(sum_done, it + 1)
                act.activation(junk[:, :], xr[u][:, :], ACT.Square, accum_out=ss[u][:, :]).then_inc(ss_done, 1)
                act.wait_ge(ss_done, it + 1)
            tiles(act, body)

        @block.vector
        def _(dve):
            def indices(it, u):
                dve.tensor_copy(idx[u][:, :], route["slot"][:, bass.ds(it, 1), :].rearrange("p a b -> p (a b)"))
                dve.tensor_copy(gates[u][:, :], route["gate"][:, bass.ds(it, 1), :].rearrange("p a b -> p (a b)")).then_inc(idx_done, 1)

            for u in range(2):
                indices(u, u)
            dve.wait_ge(fg_loaded, 16)

            def body(r, u, more):
                it = r * 2 + u
                dve.wait_ge(idx_done, it + 1)
                dve.wait_ge(x_loaded[u], r * 16 + 16)
                dve.wait_ge(gathered[u], r * 32 + 32)
                dve.scalar_tensor_tensor(out=xr[u][:, :], in0=yr[u][0][:, :], scalar=gates[u][:, 0:1], in1=xr[u][:, :],
                                         op0=ALU.mult, op1=ALU.add).then_inc(added, 1)
                dve.wait_ge(added, it + 1)
                dve.scalar_tensor_tensor(out=xr[u][:, :], in0=yr[u][1][:, :], scalar=gates[u][:, 1:2], in1=xr[u][:, :],
                                         op0=ALU.mult, op1=ALU.add).then_inc(sum_done, 1)
                dve.wait_ge(sum_done, it + 1)
                if more:
                    indices(it + 2, u)
                dve.wait_ge(r_done, it + 1)
                dve.wait_ge(o_free, it + 1)
                dve.scalar_tensor_tensor(out=o[u][:, :], in0=xr[u][:, :], scalar=ss[u][:, :], in1=fg[:, :],
                                         op0=ALU.mult, op1=ALU.mult).then_inc(o_done, 1)
            tiles(dve, body)


_INS = ['x', 'c', 'ctx', 'c_ctx', 'w_mod', 'b_mod', 'norm1_g', 'norm2_g', 'w_in', 'conv_w', 'conv_b', 'dt_bias_f', 'dt_bias_b',
        'a_log_f', 'a_log_b', 'd_skip', 'ssd_norm_g', 'gk_up_f', 'gk_bias_f', 'gk_up_b', 'gk_bias_b', 'gla_norm_g', 'w_out',
        'w_router', 'router_bias', 'w_gate', 'w_up', 'w_down', 'final_norm_g']
_OUTS = [((1, SEQ, D), 'float32')]


def kernel(**inputs):
    import numpy as _np
    import concourse.bacc as _bacc
    from concourse import mybir as _mybir
    from concourse.bass_utils import run_bass_kernel_spmd as _run

    nc = _bacc.Bacc("TRN2", target_bir_lowering=False, num_devices=1)
    arrays, args = {}, {}
    for name in _INS:
        a = _np.ascontiguousarray(inputs[name])
        arrays[f"in_{name}_dram"] = a
        args[name] = nc.dram_tensor(f"in_{name}_dram", a.shape, _mybir.dt.from_np(a.dtype), kind="ExternalInput").ap()
    shape, dtype = _OUTS[0]
    out = nc.dram_tensor("out_0_dram", shape, _mybir.dt.from_np(_np.dtype(dtype)), kind="ExternalOutput").ap()
    build(nc, args, out)
    r = _run(nc, [arrays], core_ids=[0])
    return r.results[0]["out_0_dram"]
```

```python
from contextlib import ExitStack

import concourse.bass as bass
from concourse import mybir

ALU = mybir.AluOpType
ACT = mybir.ActivationFunctionType
F32 = mybir.dt.float32
I32 = mybir.dt.int32
AX = mybir.AxisListType.X

P = 128
D = 1024
KT = D // P
SEQ = 2048
CTX = 256
GRP = 256
LAT_GROUPS = SEQ // GRP
TILES = (SEQ + CTX) // P
CT = CTX // P
LT = SEQ // P
SH, SP_, SN = 8, 64, 64
SW = SH * SP_
XBC = SW + 4 * SN
GH, GK, GV = 4, 64, 128
GQK = GH * GK
GW = GH * GV
RANK = 16
TAPS = 5
ROWW = 64
O_Z, O_XBC, O_DT = 0, SW, SW + XBC
O_Q = O_DT + SH
O_K = O_Q + GQK
O_V = O_K + GQK
O_G = O_V + GW
O_GK = O_G + GW
IN_DIM = O_GK + RANK
NE, NG, EG = 32, 8, 4
FF = 512
EPS = 1e-6
MAXB = 64
BIG = 1e30

R_C, R_CC = 0, KT
R_N1, R_N2 = 2 * KT, 3 * KT
R_BM = 4 * KT
R_CW = R_BM + 6 * KT
R_CB = R_CW + TAPS * (XBC // P)
R_SG = R_CB + XBC // P
R_GG = R_SG + SW // P
N_ROWS = R_GG + 1

T_X, T_B, T_K = 0, SW, SW + 2 * SN
T_V = T_K + GQK
T_DT = T_V + GW
T_GF = T_DT + 2 * SH
T_Z = T_GF + 2 * GQK
T_GO = T_Z + SW
T_LEN = T_GO + GW
F_TILES = 6


def hold(eng, sem, value, held):
    eng.wait_ge(sem, value)
    eng.sem_inc(held, 1)


class Names:

    def __init__(self, nc, ctx, prefix):
        self.nc, self.prefix, self.made = nc, prefix, []
        ctx.callback(self.clear)

    def __call__(self, name):
        self.made.append(self.nc.alloc_semaphore(f"{self.prefix}_{name}"))
        return self.made[-1]

    def clear(self):
        self.nc.clear_and_free_semaphores(self.made)
        self.nc.all_engine_barrier()


def build(nc, A, out, debug=()):
    def scratch(name, shape, dt=F32):
        kind = "ExternalOutput" if name in debug else "Internal"
        return nc.dram_tensor(name, shape, dt, kind=kind).ap()

    tok_rec = scratch("tok_rec", (TILES, P, T_LEN))
    feat_rec = scratch("feat_rec", (TILES, P, F_TILES * P))
    back_state = scratch("back_state", (TILES, P, 3 * 256))
    fwd_state = scratch("fwd_state", (1, P, 3 * 256))
    x_mid = scratch("x_mid", (LT, P, D))
    h_rows = scratch("h_rows", (SEQ, D))
    slot_tok = scratch("slot_tok", (TAB * P, 16), I32)
    y_slots = scratch("y_slots", (MAXB * P, D))

    with ExitStack() as top:
        def keep(name, shape, dt=F32):
            return top.enter_context(nc.sbuf_tensor(name, shape, dt))

        C = {n: keep(n, [P, P]) for n in ("ident", "ones", "gt", "lt", "gt_bd", "lt_bd")}
        C["incl"], C["incl_bd"] = keep("incl", [P, 2, P]), keep("incl_bd", [P, 2, P])
        for d, n in enumerate(("le", "ge")):
            C[n], C[n + "_bd"] = C["incl"][:, d, :], C["incl_bd"][:, d, :]
        C["halves"] = keep("halves", [P, 2])
        mod = keep("mod", [P, 6 * KT, 2])
        C["mod"] = mod
        C["cols"] = keep("cols", [P, N_ROWS])
        route = {
            "logits": keep("logits", [P, LT, NE]), "gate": keep("gate", [P, LT, 2]),
            "slot": keep("slot", [P, LT, 2], I32), "plan": keep("plan", [1, PL_LEN], I32),
        }
        constants(nc, C)
        with ExitStack() as ctx:
            w = ctx.enter_context(nc.sbuf_tensor("w_in_sb", [P, KT, IN_DIM], F32))
            w_loaded = Names(nc, ctx, "inp")("w_in_loaded")
            modulation(nc, A, C, w, w_loaded)
            projection(nc, A, C, w, w_loaded, tok_rec, feat_rec)
        if "stop1" in debug:
            return
        scan_states(nc, A, C, tok_rec, 1, back_state)
        scan_states(nc, A, C, tok_rec, 0, fwd_state)
        if "stop2" in debug:
            return
        mixer(nc, A, C, route, tok_rec, feat_rec, back_state, fwd_state, x_mid, h_rows)
        if "stop3" in debug:
            return
        with ExitStack() as ctx:
            weights = [ctx.enter_context(nc.sbuf_tensor(n, [P, 2, KT * FF], F32)) for n in ("w_gates", "w_ups", "w_downs")]
            names = Names(nc, ctx, "wts")
            loaded = [names(f"{n}_loaded") for n in ("gates", "ups", "downs")]
            slots(nc, A, C, route, slot_tok, weights, loaded)
            experts(nc, A, C, route, slot_tok, weights, loaded, h_rows, y_slots)
        combine(nc, A, C, route, y_slots, x_mid, out)


def constants(nc, C):
    with ExitStack() as ctx:
        sem = Names(nc, ctx, "cst")
        block = ctx.enter_context(nc.Block())
        made, cut = sem("made"), sem("cut")
        H = P // 2

        @block.gpsimd
        def _(pool):
            n = 0
            for name in ("ident", "le_bd", "ge_bd", "gt_bd", "lt_bd"):
                pool.memset(C[name][:, :], 1.0 if name != "ident" else 0.0).then_inc(made, 1)
                n += 1
            for name in ("ones", "le", "ge", "gt", "lt", "halves"):
                pool.memset(C[name][:, :], 1.0).then_inc(made, 1)
                n += 1
            pool.wait_ge(made, n)
            def select(t, step, cm, base, op, fill=0.0, w=P):
                pool.affine_select(out=t, in_=t, compare_op=op, fill=fill, base=base,
                                   pattern=[[step, w]], channel_multiplier=cm).then_inc(cut, 1)
            select(C["ident"][:, :], -1, 1, 0, ALU.not_equal, 1.0)
            signs = {"le": (1, -1, ALU.is_ge), "ge": (-1, 1, ALU.is_ge),
                     "gt": (-1, 1, ALU.is_gt), "lt": (1, -1, ALU.is_gt)}
            m = 1
            for name, (step, cm, op) in signs.items():
                select(C[name][:, :], step, cm, 0, op)
                select(C[name + "_bd"][:, :], step, cm, 0, op)
                m += 2
            pool.wait_ge(cut, m)
            for name in signs:
                pool.memset(C[name + "_bd"][0:H, H:P], 0.0).then_inc(cut, 1)
                pool.memset(C[name + "_bd"][H:P, 0:H], 0.0).then_inc(cut, 1)
            pool.memset(C["halves"][0:H, 1:2], 0.0).then_inc(cut, 1)
            pool.memset(C["halves"][H:P, 0:1], 0.0).then_inc(cut, 1)
            pool.wait_ge(cut, m + 10)


def modulation(nc, A, C, w_in_sb, w_in_loaded):
    mod = C["mod"]
    W = 512
    STEPS = 6 * D // W
    w_d = A["w_mod"].rearrange("l (k p) (n c) -> l n p k c", p=P, c=W)[0]
    with ExitStack() as ctx:
        sem = Names(nc, ctx, "mod")
        slab = [ctx.enter_context(nc.sbuf_tensor(f"w_mod{b}", [P, KT, W], F32)) for b in range(3)]
        rows = ctx.enter_context(nc.sbuf_tensor("rows", [N_ROWS, P], F32))
        cond = ctx.enter_context(nc.sbuf_tensor("cond_silu", [P, KT, 2], F32))
        line = [ctx.enter_context(nc.sbuf_tensor(f"line{b}", [2, W], F32)) for b in range(3)]
        rows_t = ctx.enter_context(nc.psum_tensor("rows_t", [P, N_ROWS], F32))
        cols = C["cols"]
        bias = cols[:, R_BM:R_BM + 6 * KT]
        acc = [ctx.enter_context(nc.psum_tensor(f"mod_acc{b}", [2, W], F32)) for b in range(3)]
        turn = ctx.enter_context(nc.psum_tensor("mod_turn", [P, 6 * KT, 2], F32))
        loaded = [sem(f"slab{b}_loaded") for b in range(3)]
        small, turned, copied, silu_done, slab_used, line_done, lines_turned, added, scaled = (
            sem(n) for n in ("small_loaded", "rows_transposed", "cols_copied", "silu_done", "slab_used", "line_done",
                             "lines_turned", "added", "scaled"))
        block = ctx.enter_context(nc.Block())

        @block.sync
        def _(sp):
            for at, n, src in ((R_C, KT, A["c"].rearrange("b (k p) -> (b k) p", p=P)),
                               (R_CC, KT, A["c_ctx"].rearrange("(k p) -> k p", p=P)),
                               (R_N1, KT, A["norm1_g"].rearrange("l (k p) -> (l k) p", p=P)),
                               (R_N2, KT, A["norm2_g"].rearrange("l (k p) -> (l k) p", p=P)),
                               (R_BM, 6 * KT, A["b_mod"].rearrange("l (k p) -> (l k) p", p=P)),
                               (R_CW, TAPS * 6, A["conv_w"].rearrange("l t (k p) -> (l t k) p", p=P)),
                               (R_CB, 6, A["conv_b"].rearrange("l (k p) -> (l k) p", p=P)),
                               (R_SG, 4, A["ssd_norm_g"].rearrange("l (k p) -> (l k) p", p=P)),
                               (R_GG, 1, A["gla_norm_g"])):
                sp.dma_start(rows[at:at + n, :], src).then_inc(small, 16)
            sp.sem_inc(slab_used, 3)
            with sp.Fori(0, STEPS // 3) as r:
                for u in range(3):
                    sp.wait_ge(slab_used, r * 3 + (u + 1))
                    sp.dma_start(slab[u][:, :, :], w_d[r * 3 + u]).then_inc(loaded[u], 16)
            for k in range(KT):
                sp.dma_start(w_in_sb[:, k, :], A["w_in"][0][k * P:(k + 1) * P, :]).then_inc(w_in_loaded, 16)

        @block.scalar
        def _(act):
            act.wait_ge(copied, 1)
            for j in range(2):
                act.activation(cond[:, :, j], cols[:, KT * j:KT * (j + 1)], ACT.Silu).then_inc(silu_done, 1)

        @block.tensor
        def _(pe):
            pe.wait_ge(small, 16 * 9)
            pe.transpose(rows_t[:, :], rows[:, :], C["ident"][0:N_ROWS, 0:N_ROWS]).then_inc(turned, 1)
            pe.wait_ge(silu_done, 2)
            with pe.Fori(0, STEPS // 3) as r:
                for u in range(3):
                    pe.wait_ge(loaded[u], r * 16 + 16)
                    pe.wait_ge(line_done, r * 3 + (u + 1))
                    for k in range(KT):
                        mm = pe.matmul(acc[u][:, :], cond[:, k, :], slab[u][:, k, :], start=(k == 0), stop=(k == KT - 1))
                    mm.then_inc(slab_used, 1)
                for u in range(3):
                    pe.wait_ge(line_done, r * 3 + (u + 4))
                    for m in range(W // P):
                        mm = pe.matmul(turn[:, bass.ds(r * 12 + (4 * u + m), 1), :], line[u][:, m * P:(m + 1) * P], C["ident"][0:2, 0:2],
                                       start=True, stop=True)
                    mm.then_inc(lines_turned, 1)

        @block.vector
        def _(dve):
            dve.wait_ge(turned, 1)
            dve.tensor_copy(cols[:, :], rows_t[:, :]).then_inc(copied, 1)
            dve.wait_ge(copied, 1)
            dve.sem_inc(line_done, 3)
            dve.sem_inc(lines_turned, 3)
            with dve.Fori(0, STEPS // 3) as r:
                for u in range(3):
                    dve.wait_ge(slab_used, r * 3 + (u + 4))
                    dve.wait_ge(lines_turned, r * 3 + (u + 1))
                    dve.tensor_copy(line[u][:, :], acc[u][:, :]).then_inc(line_done, 1)
            dve.wait_ge(lines_turned, 3 + STEPS)
            dve.tensor_tensor(mod[:, :, :], turn[:, :, :], bias.unsqueeze(2).to_broadcast([P, 6 * KT, 2]),
                              ALU.add).then_inc(added, 1)
            dve.wait_ge(added, 1)
            for n, part in enumerate((1, 4)):
                s = mod[:, part * KT:(part + 1) * KT, :]
                dve.scalar_tensor_tensor(out=s, in0=s, scalar=1.0, in1=cols[:, R_N1 + KT * n:R_N1 + KT * (n + 1)].unsqueeze(2).to_broadcast([P, KT, 2]),
                                         op0=ALU.add, op1=ALU.mult).then_inc(scaled, 1)
            dve.wait_ge(scaled, 2)


def projection(nc, A, C, w, w_loaded, tok_rec, feat_rec):
    mod, ident = C["mod"], C["ident"]
    x_d = A["x"].rearrange("b (g s p) d -> (b g) p s d", s=2, p=P)
    ctx_d = A["ctx"].rearrange("b (s p) d -> b p s d", p=P)[0]
    tok_g = tok_rec.rearrange("(g s) p f -> g p s f", s=2)
    feat_g = feat_rec.rearrange("(g s) p (n c) -> g s p n c", s=2, c=P)
    NF = 10
    col = [O_XBC + i * P for i in range(6)] + [O_Q, O_Q + P, O_K, O_K + P]
    with ExitStack() as ctx:
        sem = Names(nc, ctx, "prj")

        def sb(name, shape, dt=F32):
            return ctx.enter_context(nc.sbuf_tensor(name, shape, dt))

        def ps(name, shape):
            return ctx.enter_context(nc.psum_tensor(name, shape, F32))

        w_small = sb("w_small", [P, KT, 32])
        xg = sb("xg", [P, 2, D])
        junk = ps("sq_junk", [P, 512])
        hT = [sb(f"hT{b}", [P, KT, GRP]) for b in range(2)]
        u_raw = sb("u_raw", [P, 6, GRP])
        fm = sb("fm", [P, NF, GRP])
        tm = [sb(f"tm{b}", [P, 2, T_LEN]) for b in range(2)]
        soft = [sb(f"soft{b}", [P, 528]) for b in range(2)]
        small_sb = sb("small_sb", [P, 2, 32])
        gkT = sb("gkT", [RANK + 1, 2, P])
        up = sb("gk_up", [RANK + 1, 2 * GQK])
        dtb = sb("dt_bias", [1, 2 * SH])
        cols = C["cols"]
        ss = sb("ss", [P, 2, 2])
        rstd = sb("rstd", [P, 2])
        mhalf = sb("mhalf", [P, 2])
        pt = [ps(f"pt{b}", [P, 512]) for b in range(2)]
        pf = [ps(f"pf{b}", [P, 2, GRP]) for b in range(2)]
        pz = [ps(f"pz{b}", [P, 512]) for b in range(2)]
        psm = ps("psm", [P, 512])

        pool_held = sem("pool_held")
        small_loaded, x_loaded = sem("small_loaded"), sem("x_loaded")
        x_free, ss_done, rstd_done, xn_done = (sem(n) for n in ("x_free", "ss_done", "rstd_done", "xn_done"))
        ht_ps, ht_done = sem("ht_transposed"), sem("ht_done")
        feat_ps, u_done, qk_done, conv_done, silu_done = (
            sem(n) for n in ("feat_product", "u_done", "qk_done", "conv_done", "silu_done"))
        tok_ps, tok_done = sem("tok_product"), sem("tok_done")
        small_ps, small_done, gk_ps, gk_done, g_ps, abs_done, exp_done, ln_done, min_done, g_done = (
            sem(n) for n in ("small_product", "small_copied", "gk_transposed", "gk_copied", "g_product",
                             "abs_done", "exp_done", "ln_done", "min_done", "g_done"))
        back_ps, back_done = sem("back_transposed"), sem("back_copied")
        stored, feat_stored = [sem("tm0_stored"), sem("tm1_stored")], sem("fm_stored")
        const_done, wsm_done, junk_done = sem("const_done"), sem("w_small_done"), sem("junk_done")
        conv_step, hT_free = sem("conv_step"), sem("hT_free")
        block = ctx.enter_context(nc.Block())

        def steps(eng, head, body):
            def static(it):
                return it, it // 2, it % 2, it == 0
            head(*static(0))
            body(*static(0), static(1))
            with eng.Fori(0, LAT_GROUPS // 2 - 1) as r:
                first, second = (r * 2 + 1, r, 1, False), (r * 2 + 2, r + 1, 0, False)
                body(*first, second)
                body(*second, (r * 2 + 3, r + 1, 1, False))
            body(*static(LAT_GROUPS - 1), static(LAT_GROUPS))
            body(*static(LAT_GROUPS), None)

        @block.sync
        def _(sp):
            sp.dma_start(dtb[:, 0:SH], A["dt_bias_f"]).then_inc(small_loaded, 16)
            sp.dma_start(dtb[:, SH:2 * SH], A["dt_bias_b"]).then_inc(small_loaded, 16)
            sp.dma_start(up[0:RANK, 0:GQK], A["gk_up_f"][0]).then_inc(small_loaded, 16)
            sp.dma_start(up[0:RANK, GQK:2 * GQK], A["gk_up_b"][0]).then_inc(small_loaded, 16)
            sp.dma_start(up[RANK:RANK + 1, 0:GQK], A["gk_bias_f"]).then_inc(small_loaded, 16)
            sp.dma_start(up[RANK:RANK + 1, GQK:2 * GQK], A["gk_bias_b"]).then_inc(small_loaded, 16)

            def body(it, use, buf, is_ctx, after):
                sp.wait_ge(silu_done, it + 1)
                sp.wait_ge(qk_done, it * 2 + 2)
                for s in range(2):
                    sp.dma_start(feat_g[it][s], fm[:, 4:10, s * P:(s + 1) * P]).then_inc(feat_stored, 16)
                sp.wait_ge(tok_done, 2 if is_ctx else 2 + it * 6)
                sp.wait_ge(g_done, it * 2 + 2)
                sp.wait_ge(back_done, it * 4 + 4)
                if is_ctx:
                    sp.dma_start(tok_g[0][:, :, 0:T_Z], tm[buf][:, :, 0:T_Z]).then_inc(stored[buf], 16)
                else:
                    sp.dma_start(tok_g[it], tm[buf][:, :, :]).then_inc(stored[buf], 16)

            steps(sp, lambda *step: None, body)
            sp.wait_ge(feat_stored, 32 * (LAT_GROUPS + 1))
            sp.wait_ge(stored[0], 16 * (LAT_GROUPS // 2 + 1))
            sp.wait_ge(stored[1], 16 * (LAT_GROUPS // 2 + 1))

        @block.scalar
        def _(act):
            def head(it, use, buf, is_ctx):
                act.wait_ge(x_loaded, it * 16 + 16)
                for s in range(2):
                    for h in range(2):
                        if s + h:
                            act.wait_ge(junk_done, it * 4 + 2 * s + h)
                        elif not is_ctx:
                            act.wait_ge(junk_done, it * 4)
                        act.activation(junk[:, :], xg[:, s, h * 512:(h + 1) * 512], ACT.Square,
                                       accum_out=ss[:, s, h:h + 1]).then_inc(junk_done, 1)
                act.wait_ge(junk_done, it * 4 + 4)
                act.sem_inc(ss_done, 1)

            def body(it, use, buf, is_ctx, after):
                for n in range(5):
                    act.wait_ge(feat_ps, it * 5 + (n + 1))
                    if n < 3:
                        if n == 0 and not is_ctx:
                            act.wait_ge(conv_done, it)
                        act.activation(u_raw[:, 2 * n:2 * n + 2, :], pf[(n) % 2][:, :, :], ACT.Copy).then_inc(u_done, 1)
                    else:
                        if n == 3 and not is_ctx:
                            act.wait_ge(feat_stored, it * 32)
                            act.wait_ge(back_done, it * 4)
                        act.activation(fm[:, 2 * n:2 * n + 2, :], pf[(n) % 2][:, :, :], ACT.Copy,
                                       scale=GK ** -0.5 if n == 3 else 1.0).then_inc(qk_done, 1)
                act.wait_ge(conv_done, it + 1)
                act.activation(fm[:, 0:6, :], fm[:, 0:6, :], ACT.Silu).then_inc(silu_done, 1)
                if after is not None:
                    head(*after)
                n = 0
                per = 2 if is_ctx else 6
                base = 0 if is_ctx else 2 + (it - 1) * 6
                for s in range(2):
                    for part in ("v",) if is_ctx else ("z", "g", "v"):
                        act.wait_ge(tok_ps, base + (n + 1))
                        if n == 0 and not is_ctx:
                            act.wait_ge(stored[buf], use * 16 + 16 * buf)
                        o = {"z": T_Z, "g": T_GO, "v": T_V}[part]
                        act.activation(tm[buf][:, s, o:o + 512], pz[n % 2][:, :],
                                       ACT.Copy if part == "v" else ACT.Silu).then_inc(tok_done, 1)
                        n += 1
                for s in range(2):
                    act.wait_ge(g_ps, it * 2 + (s + 1))
                    if not is_ctx:
                        act.wait_ge(g_done, it * 2)
                    act.activation(soft[s][:, 0:512], pz[s][:, :], ACT.Abs).then_inc(abs_done, 1)
                    act.activation(soft[s][:, 512:528], small_sb[:, s, 0:16], ACT.Abs).then_inc(abs_done, 1)
                for s in range(2):
                    act.wait_ge(abs_done, it * 4 + 2 * s + 2)
                    act.activation(soft[s][:, :], soft[s][:, :], ACT.Exp, scale=-1.0).then_inc(exp_done, 1)
                for s in range(2):
                    act.wait_ge(exp_done, it * 2 + (s + 1))
                    act.activation(soft[s][:, :], soft[s][:, :], ACT.Ln, bias=1.0).then_inc(ln_done, 1)
            act.sem_inc(stored[1], 16)
            steps(act, head, body)

        @block.gpsimd
        def _(pool):
            pool.memset(mhalf[:, :], -0.5).then_inc(const_done, 1)
            pool.memset(gkT[:, :, :], 1.0).then_inc(const_done, 1)
            pool.wait_ge(const_done, 2)

            def head(it, use, buf, is_ctx):
                if not is_ctx:
                    hold(pool, x_free, it, pool_held)
                pool.dma_start(xg[:, :, :], ctx_d if is_ctx else x_d[it - 1]).then_inc(x_loaded, 16)
                pool.wait_ge(ss_done, it + 1)
                if not is_ctx:
                    pool.wait_ge(xn_done, it)
                pool.tensor_tensor(rstd[:, :], ss[:, :, 0], ss[:, :, 1], ALU.add).then_inc(rstd_done, 1)
                hold(pool, rstd_done, it * 3 + 1, pool_held)
                pool.tensor_scalar(rstd[:, :], rstd[:, :], 1.0 / D, EPS, ALU.mult, ALU.add).then_inc(rstd_done, 1)
                pool.wait_ge(rstd_done, it * 3 + 2)
                pool.tensor_tensor(rstd[:, :], rstd[:, :], mhalf[:, :], ALU.pow).then_inc(rstd_done, 1)

            def body(it, use, buf, is_ctx, after):
                if after is not None:
                    head(*after)
            steps(pool, head, body)

        @block.tensor
        def _(pe):
            pe.wait_ge(wsm_done, 2)
            pe.wait_ge(const_done, 2)
            pe.wait_ge(small_loaded, 16 * 6)

            def turned(it, use, buf, is_ctx, rounds):
                pe.wait_ge(xn_done, it + 1)
                for q in rounds:
                    if q >= 2:
                        pe.wait_ge(ht_done, it * 4 + (q - 1))
                    elif type(it) is not int or it >= 2:
                        pe.wait_ge(back_done, it * 4 - 4)
                    for kk in range(2):
                        for s in range(2):
                            mm = pe.transpose(pt[q % 2][:, kk * GRP + s * P:kk * GRP + (s + 1) * P],
                                              xg[:, s, (2 * q + kk) * P:(2 * q + kk + 1) * P], ident[:, :])
                    mm.then_inc(ht_ps, 1)

            def head(*step):
                turned(*step, range(4))

            def body(it, use, buf, is_ctx, after):
                pe.wait_ge(ht_done, it * 4 + 4)
                h = hT[buf]
                for n in range(5):
                    if n >= 2 or not is_ctx:
                        m = n - 2
                        if m >= 0:
                            pe.wait_ge(u_done if m < 3 else qk_done, it * 3 + (m + 1) if m < 3 else it * 2 + (m - 2))
                        elif n == 0:
                            pe.wait_ge(qk_done, it * 2)
                    for f in range(2):
                        for k in range(KT):
                            c0 = col[2 * n + f]
                            mm = pe.matmul(pf[n % 2][:, f, :], w[:, k, c0:c0 + P], h[:, k, :],
                                           start=(k == 0), stop=(k == KT - 1))
                    mm.then_inc(feat_ps, 1)
                if not is_ctx:
                    pe.wait_ge(gk_done, it)
                    pe.wait_ge(small_done, it)
                for s in range(2):
                    for k in range(KT):
                        pe.matmul(psm[:, s * 32:s * 32 + 32], h[:, k, s * P:(s + 1) * P], w_small[:, k, :],
                                  start=(k == 0), stop=False)
                    mm = pe.matmul(psm[:, s * 32:s * 32 + 16], C["ones"][0:1, :], dtb[0:1, :], start=False, stop=True)
                mm.then_inc(small_ps, 1)
                n = 0
                base = 0 if is_ctx else 2 + (it - 1) * 6
                for s in range(2):
                    for part in ("v",) if is_ctx else ("z", "g", "v"):
                        if n >= 2:
                            pe.wait_ge(tok_done, base + (n - 1))
                        elif n == 0 and not is_ctx:
                            pe.wait_ge(min_done, it * 4)
                            pe.wait_ge(abs_done, it * 4)
                        o = {"z": O_Z, "g": O_G, "v": O_V}[part]
                        for k in range(KT):
                            mm = pe.matmul(pz[n % 2][:, :], h[:, k, s * P:(s + 1) * P], w[:, k, o:o + 512],
                                           start=(k == 0), stop=(k == KT - 1))
                        mm.then_inc(tok_ps, 1)
                        n += 1
                        split = (1, 2) if is_ctx else (3, 4)
                        if after is not None and n in split:
                            turned(*after, range(2) if n == split[0] else range(2, 4))
                pe.wait_ge(small_done, it + 1)
                for s in range(2):
                    mm = pe.transpose(psm[0:RANK, 128 + s * P:256 + s * P], small_sb[:, s, 16:32], ident[:, :])
                mm.then_inc(gk_ps, 1)
                pe.wait_ge(gk_done, it + 1)
                pe.wait_ge(tok_done, base + n)
                for s in range(2):
                    pe.matmul(pz[s][:, :], gkT[:, s, :], up[:, :], start=True, stop=True).then_inc(g_ps, 1)
                pe.wait_ge(silu_done, it + 1)
                pe.wait_ge(qk_done, it * 2 + 2)
                for s in range(2):
                    for half in range(2):
                        q = 2 * s + half
                        if q >= 2:
                            pe.wait_ge(back_done, it * 4 + (q - 1))
                        elif after is not None:
                            pe.wait_ge(ht_done, it * 4 + 8)
                        else:
                            pe.wait_ge(ht_done, it * 4 + 4)
                        tiles = (0, 1, 2, 3) if half == 0 else (4, 8, 9)
                        for j, f in enumerate(tiles):
                            mm = pe.transpose(pt[q % 2][:, j * P:(j + 1) * P], fm[:, f, s * P:(s + 1) * P], ident[:, :])
                        mm.then_inc(back_ps, 1)
            steps(pe, head, body)

        @block.vector
        def _(dve):
            dve.wait_ge(w_loaded, 16 * KT)
            for j in range(2):
                dve.tensor_copy(w_small[:, :, 8 * j:8 * j + 8], w[:, :, O_DT:O_DT + 8])
            dve.tensor_copy(w_small[:, :, 16:32], w[:, :, O_GK:O_GK + 16]).then_inc(wsm_done, 2)
            dve.wait_ge(small_loaded, 16 * 6)

            def head(it, use, buf, is_ctx):
                dve.wait_ge(rstd_done, it * 3 + 3)
                for s in range(2):
                    i = dve.tensor_scalar(xg[:, s, :], xg[:, s, :], rstd[:, s:s + 1], None, ALU.mult)
                i.then_inc(xn_done, 1)
                who = 1 if is_ctx else 0
                for q in range(4):
                    dve.wait_ge(ht_ps, it * 4 + (q + 1))
                    for kk in range(2):
                        k = 2 * q + kk
                        i = dve.tensor_scalar(hT[buf][:, k, :], pt[q % 2][:, kk * GRP:(kk + 1) * GRP],
                                              mod[:, KT + k, who:who + 1], mod[:, k, who:who + 1], ALU.mult, ALU.add)
                    i.then_inc(ht_done, 1)
                    if q == 3:
                        dve.sem_inc(x_free, 1)

            def body(it, use, buf, is_ctx, after):
                wide = GRP if is_ctx else ROWW
                dve.wait_ge(u_done, it * 3 + 3)
                if not is_ctx:
                    dve.wait_ge(feat_stored, it * 32)
                    dve.wait_ge(back_done, it * 4)
                for n, tap in enumerate((2, 0, 1, 3, 4)):
                    if n:
                        dve.wait_ge(conv_step, it * 4 + n)
                    for f in range(6):
                        a = fm[:, f, :].rearrange("p (r t) -> p r t", t=wide)
                        b = u_raw[:, f, :].rearrange("p (r t) -> p r t", t=wide)
                        wt = cols[:, R_CW + 6 * tap + f:R_CW + 6 * tap + f + 1]
                        if tap == 2:
                            i = dve.tensor_scalar(a, b, wt, cols[:, R_CB + f:R_CB + f + 1], ALU.mult, ALU.add)
                            continue
                        sh = tap - 2
                        to, fr = (a[:, :, -sh:], b[:, :, :wide + sh]) if sh < 0 else (a[:, :, :wide - sh], b[:, :, sh:])
                        i = dve.scalar_tensor_tensor(out=to, in0=fr, scalar=wt, in1=to, op0=ALU.mult, op1=ALU.add)
                    i.then_inc(conv_done if n == 4 else conv_step, 1)
                dve.wait_ge(small_ps, it + 1)
                if not is_ctx:
                    dve.wait_ge(abs_done, it * 4)
                    dve.wait_ge(min_done, it * 4)
                dve.tensor_copy(small_sb[:, :, :], psm[:, 0:64].rearrange("p (s c) -> p s c", s=2)).then_inc(small_done, 1)
                if after is not None:
                    head(*after)
                dve.wait_ge(gk_ps, it + 1)
                dve.tensor_copy(gkT[0:RANK, :, :], psm[0:RANK, 128:384].rearrange("p (s c) -> p s c", s=2)).then_inc(gk_done, 1)
                t = tm[buf]
                if not is_ctx:
                    dve.wait_ge(stored[buf], use * 16 + (0 if buf == 0 else 16))
                for s in range(2):
                    dve.wait_ge(g_ps, it * 2 + (s + 1))
                    dve.wait_ge(abs_done, it * 4 + (2 * s + 1))
                    dve.tensor_scalar(t[:, s, T_GF:T_GF + 512], pz[s][:, :], 0.0, 1 / 16.0, ALU.min, ALU.mult).then_inc(min_done, 1)
                    dve.tensor_scalar(t[:, s, T_DT:T_DT + 16], small_sb[:, s, 0:16], 0.0, None, ALU.max).then_inc(min_done, 1)
                for s in range(2):
                    for half in range(2):
                        q = 2 * s + half
                        dve.wait_ge(back_ps, it * 4 + (q + 1))
                        if half == 0:
                            dve.tensor_copy(t[:, s, T_X:T_X + 512], pt[q % 2][:, :]).then_inc(back_done, 1)
                        else:
                            dve.tensor_copy(t[:, s, T_B:T_B + 384], pt[q % 2][:, 0:384]).then_inc(back_done, 1)
                for s in range(2):
                    dve.wait_ge(ln_done, it * 2 + (s + 1))
                    dve.wait_ge(min_done, it * 4 + 4)
                    dve.scalar_tensor_tensor(out=t[:, s, T_GF:T_GF + 512], in0=soft[s][:, 0:512], scalar=-1 / 16.0,
                                             in1=t[:, s, T_GF:T_GF + 512], op0=ALU.mult, op1=ALU.add)
                    dve.tensor_tensor(t[:, s, T_DT:T_DT + 16], t[:, s, T_DT:T_DT + 16], soft[s][:, 512:528],
                                      ALU.add).then_inc(g_done, 1)
            steps(dve, head, body)


def direction(C, d):
    return (C["le"], C["gt"], C["le_bd"], C["gt_bd"]) if d == 0 else (C["ge"], C["lt"], C["ge_bd"], C["lt_bd"])


def state_products(pe, C, d, rec, dta, small):
    _, past, _, past_bd = direction(C, d)
    g0 = T_GF + d * GQK
    pe.matmul(small[:, 0:GQK], past_bd[:, :], rec[:, g0:g0 + GQK], start=True, stop=True)
    pe.matmul(small[:, 256:264], past[:, :], dta, start=True, stop=True)
    for g in range(2):
        pe.matmul(small[64 * g:64 * g + 64, 264:268], C["ones"][:, 0:64], dta[:, 4 * g:4 * g + 4], start=True, stop=True)
    for pair in range(2):
        mm = pe.matmul(small[:, 268 + 2 * pair:270 + 2 * pair], rec[:, g0 + P * pair:g0 + P * (pair + 1)],
                       C["halves"][:, :], start=True, stop=True)
    return mm


class Turn:

    def __init__(self, c, r=None):
        self.it = c if r is None else r * 4 + c
        self.use4 = c // 4 if r is None else r + c // 4
        self.least, self.b4, self.b2 = c, c % 4, c % 2
        self.c, self.r = c, r

    def before(self, n):
        return Turn(self.c - n, self.r)


def scan_states(nc, A, C, tok_rec, d, state_out):
    first, second = (1, 0) if d else (0, 1)
    LAST = TILES if d else CT
    with ExitStack() as ctx:
        sem = Names(nc, ctx, f"sc{d}")

        def sb(name, shape, dt=F32):
            return ctx.enter_context(nc.sbuf_tensor(f"{name}_s{d}", shape, dt))

        def ps(name, shape):
            return ctx.enter_context(nc.psum_tensor(f"{name}_s{d}", shape, F32))

        rec = [sb(f"rec{b}", [P, T_Z]) for b in range(4)]
        st = [sb(f"st{b}", [P, 3, 256]) for b in range(4)]
        ex = [sb(f"ex{b}", [P, 272]) for b in range(4)]
        nega = sb("nega", [P, SH])
        dta, wend = ([sb(f"{n}{b}", [P, SH]) for b in range(2)] for n in ("dta", "wend"))
        xw, kend = [sb(f"xw{b}", [P, SW]) for b in range(2)], [sb(f"kend{b}", [P, GQK]) for b in range(2)]
        small, p_ssd = ([ps(f"{n}{b}", [P, 512]) for b in range(2)] for n in ("small", "p_ssd"))
        p_gla = [[ps(f"p_gla{c}{b}", [P, 2, P]) for c in range(2)] for b in range(2)]
        sp_held = sem("sp_held")
        loaded = [sem(f"rec{b}_loaded") for b in range(4)]
        saved = [sem(f"st{b}_saved") for b in range(4)]
        (a_loaded, a_exp, a_done, zeroed, dta_done, small_ps, ex_done, wend_done, scaled, kend_done,
         states_ps, decayed, mid_done, next_done) = (sem(n) for n in (
             "a_loaded", "a_exp", "a_done", "zeroed", "dta_done", "small_product", "exp_done", "wend_done", "x_scaled",
             "kend_done", "state_products", "decayed", "mid_state", "next_state"))
        block = ctx.enter_context(nc.Block())
        a_d = A["a_log_b" if d else "a_log_f"]

        def rounds(eng, *parts):
            def static(i):
                for n, f in parts:
                    if 0 <= i + n < LAST:
                        f(Turn(i + n))
            for i in range(-3, 2):
                static(i)
            if d:
                with eng.Fori(0, (LAST - 6) // 4) as r:
                    for u in range(4):
                        for n, f in parts:
                            f(Turn(2 + u + n, r))
                for i in range(LAST - 4, LAST):
                    static(i)

        @block.sync
        def _(sp):
            sp.dma_start(nega[:, :], a_d.to_broadcast([P, SH])).then_inc(a_loaded, 16)
            for b in range(4):
                sp.sem_inc(saved[b], 16)

            def load(t):
                if t.least >= 4:
                    hold(sp, next_done, t.it - 3, sp_held)
                at = (TILES + 1) - t.it if t.least >= CT else 1 - t.it if d else t.it
                sp.dma_start(rec[t.b4][:, :], tok_rec[at][:, 0:T_Z]).then_inc(loaded[t.b4], 16)

            def save(t):
                if t.least < CT:
                    return
                hold(sp, mid_done, t.it + 1, sp_held)
                sp.dma_start(state_out[(TILES + 1) - t.it], st[t.b4][:, :, :].rearrange("p a b -> p (a b)")).then_inc(saved[t.b4], 16)
            rounds(sp, (3, load), (0, save))
            if d:
                for b in range(4):
                    sp.wait_ge(saved[b], 16 * (LT // 4 + 1))
            else:
                sp.wait_ge(next_done, CT)
                sp.dma_start(state_out[0], st[CT][:, :, :].rearrange("p a b -> p (a b)")).then_inc(saved[CT], 16)
                sp.wait_ge(saved[CT], 32)

        @block.scalar
        def _(act):
            act.wait_ge(a_loaded, 16)
            act.activation(nega[:, :], nega[:, :], ACT.Exp).then_inc(a_exp, 1)

            def exponentials(t):
                act.wait_ge(small_ps, t.it + 1)
                if t.least >= 4:
                    act.wait_ge(next_done, t.it - 3)
                act.activation(ex[t.b4][:, :], small[t.b2][:, 0:272], ACT.Exp).then_inc(ex_done, 1)
            rounds(act, (2, exponentials))

        @block.tensor
        def _(pe):
            def sums(t):
                pe.wait_ge(dta_done, t.it + 1)
                if t.least >= 2:
                    pe.wait_ge(ex_done, t.it - 1)
                state_products(pe, C, d, rec[t.b4], dta[t.b2][:, :], small[t.b2]).then_inc(small_ps, 1)

            def products(t):
                pe.wait_ge(scaled, t.it + 1)
                pe.wait_ge(kend_done, t.it + 1)
                if t.least >= 2:
                    pe.wait_ge(next_done, t.it - 1)
                state_matmuls(pe, rec[t.b4], xw[t.b2], kend[t.b2], p_ssd[t.b2], p_gla[t.b2]).then_inc(states_ps, 1)
            rounds(pe, (0, products), (2, sums))

        @block.vector
        def _(dve):
            for b in range(4):
                dve.memset(st[b][:, :, :], 0.0).then_inc(zeroed, 1)
            dve.wait_ge(a_exp, 1)
            dve.tensor_scalar(nega[:, :], nega[:, :], -1.0, None, ALU.mult).then_inc(a_done, 1)
            dve.wait_ge(a_done, 1)
            dve.wait_ge(zeroed, 4)

            def dt(t):
                return rec[t.b4][:, T_DT + SH * d:T_DT + SH * (d + 1)]

            def log_decays(t):
                dve.wait_ge(loaded[t.b4], t.use4 * 16 + 16)
                if t.least >= 2:
                    dve.wait_ge(small_ps, t.it - 1)
                dve.tensor_tensor(dta[t.b2][:, :], dt(t), nega[:, :], ALU.mult).then_inc(dta_done, 1)

            def weighted(t):
                dve.wait_ge(ex_done, t.it + 1)
                if t.least >= 2:
                    dve.wait_ge(states_ps, t.it - 1)
                dve.tensor_tensor(wend[t.b2][:, :], ex[t.b4][:, 256:264], dt(t), ALU.mult).then_inc(wend_done, 1)
                dve.tensor_tensor(kend[t.b2][:, :], rec[t.b4][:, T_K:T_K + GQK], ex[t.b4][:, 0:256], ALU.mult).then_inc(kend_done, 1)
                dve.wait_ge(wend_done, t.it + 1)
                dve.tensor_tensor(xw[t.b2][:, :].rearrange("p (h c) -> p h c", h=SH),
                                  rec[t.b4][:, 0:SW].rearrange("p (h c) -> p h c", h=SH),
                                  wend[t.b2][:, :].unsqueeze(2).to_broadcast([P, SH, SP_]), ALU.mult).then_inc(scaled, 1)

            def states(t):
                dve.wait_ge(states_ps, t.it + 1)
                if t.least >= 1:
                    dve.wait_ge(next_done, t.it)
                if t.least >= 2:
                    old = t.before(3)
                    dve.wait_ge(saved[old.b4], (old.use4 + (2 if old.b4 >= 2 else 1)) * 16)
                update_states(dve, t.it, ex[t.b4], p_ssd[t.b2], p_gla[t.b2], st[t.b4], st[(t.b4 + 1) % 4], first, second,
                              decayed, mid_done, next_done)
            rounds(dve, (2, log_decays), (1, weighted), (0, states))


def state_matmuls(pe, rec, xw, kend, p_ssd, p_gla):
    for g in range(2):
        pe.matmul(p_ssd[64 * g:64 * g + 64, 0:256], rec[:, T_B + 64 * g:T_B + 64 * g + 64],
                  xw[:, 256 * g:256 * g + 256], start=True, stop=True)
    for c in range(2):
        for h in range(GH):
            mm = pe.matmul(p_gla[c][64 * (h % 2):64 * (h % 2) + 64, h // 2, :], kend[64 * c:64 * c + 64, 64 * h:64 * h + 64],
                           rec[64 * c:64 * c + 64, T_V + GV * h:T_V + GV * (h + 1)], start=True, stop=True)
    return mm


def update_states(dve, it, ex, p_ssd, p_gla, now, nxt, first, second, decayed, mid_done, next_done):
    for pair in range(2):
        i = dve.scalar_tensor_tensor(out=now[:, 1 + second, P * pair:P * (pair + 1)],
                                     in0=now[:, 1 + first, P * pair:P * (pair + 1)],
                                     scalar=ex[:, 268 + 2 * pair + first:269 + 2 * pair + first],
                                     in1=p_gla[first][:, pair, :], op0=ALU.mult, op1=ALU.add)
    i.then_inc(mid_done, 1)
    h = now[:, 0, :].rearrange("p (h c) -> p h c", h=4)
    n = nxt[:, 0, :].rearrange("p (h c) -> p h c", h=4)
    dve.tensor_tensor(n, h, ex[:, 264:268].unsqueeze(2).to_broadcast([P, 4, SP_]), ALU.mult).then_inc(decayed, 1)
    dve.wait_ge(mid_done, it + 1)
    for pair in range(2):
        dve.scalar_tensor_tensor(out=nxt[:, 1 + first, P * pair:P * (pair + 1)],
                                 in0=now[:, 1 + second, P * pair:P * (pair + 1)],
                                 scalar=ex[:, 268 + 2 * pair + second:269 + 2 * pair + second],
                                 in1=p_gla[second][:, pair, :], op0=ALU.mult, op1=ALU.add)
    dve.wait_ge(decayed, it + 1)
    dve.tensor_tensor(nxt[:, 0, :], nxt[:, 0, :], p_ssd[:, 0:256], ALU.add).then_inc(next_done, 1)


class Step:

    def __init__(self, it, use, buf, later, reused):
        self.it, self.use, self.buf, self.later, self.reused = it, use, buf, later, reused


def pipeline(eng, ahead, front, output, tail):
    def at(n):
        return Step(n, n // 2, n % 2, n >= 1, n >= 2) if 0 <= n < LT else None

    def turn(done, before, now, after):
        front(now, before, done)
        output(now, before, after)
        if after is not None:
            ahead(after)

    ahead(at(0))
    for n in range(2):
        turn(at(n - 2), at(n - 1), at(n), at(n + 1))
    with eng.Fori(0, LT // 2 - 2) as r:
        steps = [Step(r * 2 + n, r + n // 2, n % 2, True, True) for n in range(5)]
        turn(*steps[0:4])
        turn(*steps[1:5])
    for n in (LT - 2, LT - 1):
        turn(at(n - 2), at(n - 1), at(n), at(n + 1))
    front(None, at(LT - 1), at(LT - 2))
    output(None, at(LT - 1), None)
    tail(at(LT - 1))


def mixer(nc, A, C, route, tok_rec, feat_rec, back_state, fwd_state, x_mid, h_rows):
    mod, ident = C["mod"], C["ident"]
    FRONT = ["v", "v", "v", "v", "v", "v", "a", "v", "v", "v", "v", "v", "v", "v"]
    TAIL = ["a", "v", "v", "v", "a", "v", "v"]
    R_SC, R_BC, R_BT, R_AT, R_PI, R_PS, R_PG = 0, 2, 6, 7, 9, 11, 12
    R_MT, R_OP, R_XT, R_RT = 0, 2, 4, 6
    x_t = A["x"].rearrange("b (t p) d -> (b t) p d", p=P)
    h_t = h_rows.rearrange("(t p) d -> t p d", p=P)
    with ExitStack() as ctx:
        sem = Names(nc, ctx, "mix")

        def sb(name, shape, dt=F32):
            return ctx.enter_context(nc.sbuf_tensor(f"{name}_m", shape, dt))

        def ps(name, shape):
            return ctx.enter_context(nc.psum_tensor(f"{name}_m", shape, F32))

        rec = [sb(f"rec{b}", [P, T_LEN]) for b in range(2)]
        feat = [sb(f"feat{b}", [P, F_TILES, P]) for b in range(2)]
        bst = [sb(f"bst{b}", [P, 3, 256]) for b in range(2)]
        xres = [sb(f"xres{b}", [P, D]) for b in range(2)]
        st = [sb(f"st{b}", [P, 3, 256]) for b in range(2)]
        w_out, w_rt = sb("w_out", [P, KT, D]), sb("w_rt", [P, KT, NE])
        gate_bc, scale_bc, shift_bc = (sb(n, [P, D]) for n in ("gate_bc", "scale_bc", "shift_bc"))
        nega, skip = sb("nega", [P, 2 * SH]), sb("skip", [P, SH])
        inv, mhalf = sb("inv", [P, 8]), sb("mhalf", [P, 8])
        dta, ex, a_sb = sb("dta", [P, 2 * SH]), sb("ex", [P, 288]), sb("a_sb", [P, 2 * SH])
        scm = sb("scm", [P, 2, 2, P])
        seg = [sb(f"seg{b}", [P, 4, P]) for b in range(2)]
        M = [sb(f"M{n}", [P, 4, P]) for n in range(4)]
        xd, xw, xD = sb("xd", [P, 2, SW]), sb("xw", [P, SW]), sb("xD", [P, SW])
        wend, kend = sb("wend", [P, SH]), sb("kend", [P, GQK])
        eb, enb, qd, ki = (sb(n, [P, 4, P]) for n in ("eb", "enb", "qd", "ki"))
        am = [sb(f"am{b}", [P, 4, P]) for b in range(2)]
        yi, y, junk = sb("yi", [P, 2, SW]), sb("y", [P, SW]), sb("junk", [P, D])
        m, mT = sb("m", [P, D]), sb("mT", [P, KT, P])
        x1 = [sb(f"x1{b}", [P, D]) for b in range(2)]
        xh = [sb(f"xh{b}", [P, D]) for b in range(2)]
        h_row = sb("h_row", [P, D])
        h2T = sb("h2T", [P, KT, P])
        ssm, ssx, rsx = sb("ssm", [P, 8]), sb("ssx", [P, 1]), sb("rsx", [P, 1])
        small, py = ps("small", [P, 512]), ps("py", [P, 512])
        po = [ps(f"po{b}", [P, 2, P]) for b in range(2)]
        fr = [ps(f"fr{b}", [P, 512]) for b in range(2)]
        tr = [ps(f"tr{b}", [P, 512]) for b in range(2)]

        rec_loaded, x_loaded = [sem(f"rec{b}_loaded") for b in range(2)], [sem(f"x{b}_loaded") for b in range(2)]
        x1_stored = [sem(f"x1{b}_stored") for b in range(2)]
        row_scaled, row_done, row_stored = sem("row_scaled"), sem("row_done"), sem("row_stored")
        (setup, a_exp, setup_done, gate_ps, gate_done, setup_pool, dta_done, small_ps, ex_done, a_copied, scm_done, seg_done,
         seg_exp, m_ready, eb_done, qk_done, xd_done, wend_done, xw_done, kend_done, xD_done, am_done, pi_done,
         decayed, mid_done, next_done, y_ps, o_ps, ysum1, ysum_done, y_raw, y_gated, sq_done, r_step, r_done, m_step, mix_done,
         xg_done, xadd_done, sx_done, rx_step, rx_done, xh_done, h2_done, log_done) = (sem(n) for n in (
             "setup", "a_exp", "setup_done", "gate_spread", "gate_done", "setup_pool", "dta_done", "small_product", "exp_done",
             "a_copied", "masked_scores", "seg_done", "seg_exp", "decayed_scores", "eb_done", "qk_decayed", "xd_done", "wend_done",
             "xw_done", "kend_done", "x_skip", "attn_masked", "inter_scaled", "decayed", "mid_state", "next_state", "y_product",
             "o_product", "y_sum1", "y_sum", "y_raw", "y_gated", "squares", "r_step", "r_done", "m_step", "mix_done", "x_gated",
             "x_added", "x_square", "rx_step", "rx_done", "xh_done", "h2T_done", "logits_done"))
        pool_held = sem("pool_held")
        pe_held = sem("pe_held")
        x_buf_free = sem("x_buffer_free")
        f_ps, t_ps = sem("front_product"), sem("tail_product")
        f_v, f_a, t_v, t_a = sem("front_freed_v"), sem("front_freed_a"), sem("tail_freed_v"), sem("tail_freed_a")
        block = ctx.enter_context(nc.Block())

        def count(rounds, n, who, it):
            return it * rounds.count(who) + rounds[:n + 1].count(who)

        def bank_free(pe, rounds, n, s, by_v, by_a):
            last = n - 2 if n >= 2 else max(i for i in range(len(rounds)) if i % 2 == n % 2)
            if n < 2 and not s.later:
                return
            it = s.it if n >= 2 else s.it - 1
            who = rounds[last]
            hold(pe, by_v if who == "v" else by_a, count(rounds, last, who, it), pe_held)

        @block.sync
        def _(sp):
            for k in range(KT):
                sp.dma_start(w_out[:, k, :], A["w_out"][0, k * P:(k + 1) * P, :]).then_inc(setup, 16)
            sp.dma_start(w_rt[:, :, :], A["w_router"].rearrange("(k p) e -> p k e", p=P)).then_inc(setup, 16)
            sp.dma_start(nega[:, 0:SH], A["a_log_f"].to_broadcast([P, SH])).then_inc(setup, 16)
            sp.dma_start(nega[:, SH:], A["a_log_b"].to_broadcast([P, SH])).then_inc(setup, 16)
            sp.dma_start(skip[:, :], A["d_skip"].to_broadcast([P, SH])).then_inc(setup, 16)
            sp.dma_start(st[0][:, :, :].rearrange("p a b -> p (a b)"), fwd_state[0]).then_inc(setup, 16)
            def ahead(s):
                if s.reused:
                    sp.wait_ge(mix_done, s.it - 1)
                sp.dma_start(rec[s.buf][:, :], tok_rec[s.it + CT]).then_inc(rec_loaded[s.buf], 16)
                sp.dma_start(feat[s.buf][:, :, :].rearrange("p a b -> p (a b)"), feat_rec[s.it + CT]).then_inc(rec_loaded[s.buf], 16)
                sp.dma_start(bst[s.buf][:, :, :].rearrange("p a b -> p (a b)"), back_state[s.it + CT]).then_inc(rec_loaded[s.buf], 16)
                if s.reused:
                    sp.wait_ge(xadd_done, s.it - 1)
                sp.dma_start(xres[s.buf][:, :], x_t[s.it]).then_inc(x_loaded[s.buf], 16)

            def none(*tiles):
                pass

            pipeline(sp, ahead, none, none, none)

        @block.gpsimd
        def _(pool):
            pool.sem_inc(x_buf_free, 1)
            pool.memset(mhalf[:, :], -0.5).then_inc(setup_pool, 1)
            pool.memset(inv[:, 0:4], 1.0 / GV).then_inc(setup_pool, 1)
            pool.memset(inv[:, 4:8], 1.0 / SW).then_inc(setup_pool, 1)
            pool.memset(ssm[:, :], 1.0).then_inc(setup_pool, 1)
            pool.wait_ge(setup_pool, 4)
            pool.wait_ge(setup, 16 * (KT + 5))
            pool.wait_ge(gate_done, 6)

            def spread(out, x, by):
                return pool.tensor_tensor(out.rearrange("p (h c) -> p h c", h=SH), x.rearrange("p (h c) -> p h c", h=SH),
                                          by.unsqueeze(2).to_broadcast([P, SH, SP_]), ALU.mult)

            def ahead(s):
                r, it = rec[s.buf], s.it
                pool.wait_ge(rec_loaded[s.buf], s.use * 48 + 48)
                if s.later:
                    pool.wait_ge(y_ps, it)
                for d in range(2):
                    spread(xd[:, d, :], r[:, 0:SW], r[:, T_DT + SH * d:T_DT + SH * (d + 1)]).then_inc(xd_done, 1)
                spread(xD[:, :], r[:, 0:SW], skip[:, :]).then_inc(xD_done, 1)
                pool.wait_ge(ex_done, it + 1)
                pool.tensor_tensor(wend[:, :], ex[:, 256:264], r[:, T_DT:T_DT + SH], ALU.mult).then_inc(wend_done, 1)
                pool.tensor_tensor(kend[:, :], r[:, T_K:T_K + GQK], ex[:, 0:256], ALU.mult).then_inc(kend_done, 1)
                pool.wait_ge(wend_done, it + 1)
                spread(xw[:, :], r[:, 0:SW], wend[:, :]).then_inc(xw_done, 1)

            def stream(s):
                it = s.it
                pool.wait_ge(xg_done, it * 2 + 2)
                pool.wait_ge(x_loaded[s.buf], s.use * 16 + 16)
                pool.tensor_tensor(x1[s.buf][:, :], x1[s.buf][:, :], xres[s.buf][:, :], ALU.add).then_inc(xadd_done, 1)

            def stream_norm(s):
                it = s.it
                pool.wait_ge(sx_done, it + 1)
                if s.later:
                    hold(pool, xh_done, it, pool_held)
                pool.tensor_scalar(rsx[:, :], ssx[:, :], 1.0 / D, EPS, ALU.mult, ALU.add).then_inc(rx_step, 1)
                pool.wait_ge(rx_step, it + 1)
                pool.tensor_tensor(rsx[:, :], rsx[:, :], mhalf[:, 0:1], ALU.pow).then_inc(rx_done, 1)
                if s.later:
                    prior_use = s.use if s.buf == 1 else s.use - 1
                    pool.wait_ge(x1_stored[1 - s.buf], prior_use * 16 + 16)
                    pool.wait_ge(row_scaled, it)
                    pool.sem_inc(x_buf_free, 1)
                pool.dma_start(x_mid[it], x1[s.buf][:, :]).then_inc(x1_stored[s.buf], 16)

            def front(now, before, done):
                if done is not None:
                    tail(done)

            def output(now, before, after):
                if now is not None:
                    it = now.it
                    pool.wait_ge(pi_done, it * 2 + 2)
                    pool.wait_ge(xD_done, it + 1)
                    pool.tensor_tensor(yi[:, 0, :], yi[:, 0, :], yi[:, 1, :], ALU.add).then_inc(ysum1, 1)
                    pool.wait_ge(ysum1, it + 1)
                    pool.tensor_tensor(yi[:, 0, :], yi[:, 0, :], xD[:, :], ALU.add).then_inc(ysum_done, 1)
                if before is not None:
                    stream(before)
                if now is not None:
                    it = now.it
                    pool.wait_ge(sq_done, it * 5 + 5)
                    pool.tensor_tensor(ssm[:, :], ssm[:, :], inv[:, :], ALU.mult).then_inc(r_step, 1)
                    hold(pool, r_step, it * 2 + 1, pool_held)
                    pool.tensor_scalar(ssm[:, :], ssm[:, :], EPS, None, ALU.add).then_inc(r_step, 1)
                    pool.wait_ge(r_step, it * 2 + 2)
                    pool.tensor_tensor(ssm[:, :], ssm[:, :], mhalf[:, :], ALU.pow).then_inc(r_done, 1)
                if before is not None:
                    stream_norm(before)

            def tail(s):
                it = s.it
                pool.wait_ge(xh_done, it + 1)
                if s.later:
                    hold(pool, row_stored, it * 16, pool_held)
                pool.tensor_tensor(h_row[:, :], xh[s.buf][:, :], scale_bc[:, :], ALU.mult).then_inc(row_scaled, 1)
                pool.wait_ge(row_scaled, it + 1)
                pool.tensor_tensor(h_row[:, :], h_row[:, :], shift_bc[:, :], ALU.add).then_inc(row_done, 1)
                hold(pool, row_done, it + 1, pool_held)
                pool.dma_start(h_t[it], h_row[:, :]).then_inc(row_stored, 16)

            pipeline(pool, ahead, front, output, tail)
            for b in range(2):
                pool.wait_ge(x1_stored[b], 16 * (LT // 2))
            pool.wait_ge(row_stored, 16 * LT)

        @block.scalar
        def _(act):
            act.wait_ge(setup, 16 * (KT + 5))
            act.activation(nega[:, :], nega[:, :], ACT.Exp).then_inc(a_exp, 1)

            def ahead(s):
                it = s.it
                act.wait_ge(small_ps, it + 1)
                if s.later:
                    act.wait_ge(next_done, it)
                act.activation(ex[:, :], small[:, 0:288], ACT.Exp).then_inc(ex_done, 1)
                act.activation(a_sb[:, :], small[:, 272:288], ACT.Copy).then_inc(a_copied, 1)

            def decays(s, r):
                act.wait_ge(seg_done, s.it * 4 + (r + 1))
                act.activation(seg[r % 2][:, :, :], seg[r % 2][:, :, :], ACT.Exp).then_inc(seg_exp, 1)

            def gains(s):
                act.wait_ge(t_ps, s.it * 7 + (R_MT + 1))
                for j in range(4):
                    i = act.activation(mT[:, j, :], tr[0][:, P * j:P * (j + 1)], ACT.Copy,
                                       scale=C["cols"][:, R_SG + j:R_SG + j + 1])
                i.then_inc(t_a, 1)

            def front(now, before, done):
                if done is not None:
                    normed(done)
                if now is not None:
                    decays(now, 0)
                    decays(now, 1)
                if done is not None:
                    routed(done)
                if now is not None:
                    decays(now, 2)
                if before is not None:
                    gains(before)
                if now is not None:
                    it = now.it
                    decays(now, 3)
                    act.wait_ge(f_ps, it * 14 + (R_BT + 1))
                    if now.later:
                        act.wait_ge(qk_done, it * 2)
                    act.activation(eb[:, :, :], fr[R_BT % 2][:, :].rearrange("p (a b) -> p a b", a=4), ACT.Exp).then_inc(eb_done, 1)
                    act.activation(enb[:, :, :], fr[R_BT % 2][:, :].rearrange("p (a b) -> p a b", a=4), ACT.Exp, scale=-1.0).then_inc(eb_done, 1)
                    act.wait_ge(eb_done, it * 2 + 2)
                    act.sem_inc(f_a, 1)

            def normed(s):
                act.wait_ge(rx_done, s.it + 1)
                if s.later:
                    act.wait_ge(x_buf_free, s.it)
                act.activation(xh[s.buf][:, :], x1[s.buf][:, :], ACT.Copy, scale=rsx[:, :]).then_inc(xh_done, 1)

            def output(now, before, after):
                if now is not None:
                    it = now.it
                    act.wait_ge(o_ps, it * 2 + 2)
                    if now.later:
                        act.wait_ge(mix_done, it)
                    if before is not None and before.later:
                        act.wait_ge(sx_done, before.it)
                    for h in range(GH):
                        if h or now.later:
                            act.wait_ge(sq_done, it * 5 + h)
                        act.activation(junk[:, 0:GV], po[h % 2][:, h // 2, :], ACT.Square, accum_out=ssm[:, h:h + 1]).then_inc(sq_done, 1)
                    act.wait_ge(y_gated, it + 1)
                    act.wait_ge(sq_done, it * 5 + 4)
                    act.activation(junk[:, 0:SW], y[:, :], ACT.Square, accum_out=ssm[:, 4:5]).then_inc(sq_done, 1)
                if before is not None:
                    it = before.it
                    act.wait_ge(xadd_done, it + 1)
                    act.wait_ge(sq_done, it * 5 + (5 if now is None else 10))
                    if before.later:
                        act.wait_ge(rx_step, it)
                    act.activation(junk[:, :], x1[before.buf][:, :], ACT.Square, accum_out=ssx[:, :]).then_inc(sx_done, 1)

            def routed(s):
                it = s.it
                if s.later:
                    act.wait_ge(log_done, it)
                act.wait_ge(t_ps, it * 7 + (R_XT + 1))
                for k in range(4):
                    i = act.activation(h2T[:, k, :], tr[0][:, P * k:P * (k + 1)], ACT.Identity,
                                       scale=mod[:, 4 * KT + k, 0:1], bias=mod[:, 3 * KT + k, 0:1])
                i.then_inc(t_a, 1)

            def tail(s):
                normed(s)
                routed(s)

            pipeline(act, ahead, front, output, tail)

        @block.tensor
        def _(pe):
            for n, part in enumerate((2, 4, 3)):
                if n:
                    pe.wait_ge(gate_done, 2 * n)
                for j in range(KT):
                    pe.matmul(tr[j // 4][:, P * (j % 4):P * (j % 4 + 1)], mod[:, part * KT + j, 0:1].to_broadcast([P, P]), ident[:, :],
                              start=True, stop=True).then_inc(gate_ps, 1)
            pe.wait_ge(gate_done, 6)
            pe.wait_ge(setup, 16 * (KT + 5))

            def ahead(s):
                it, r, f = s.it, rec[s.buf], feat[s.buf]
                pe.wait_ge(rec_loaded[s.buf], s.use * 48 + 48)
                pe.wait_ge(dta_done, it + 1)
                if s.later:
                    pe.wait_ge(a_copied, it)
                state_products(pe, C, 0, r, dta[:, 0:SH], small)
                pe.matmul(small[:, 272:280], C["le"][:, :], dta[:, 0:SH], start=True, stop=True)
                pe.matmul(small[:, 280:288], C["ge"][:, :], dta[:, SH:], start=True, stop=True).then_inc(small_ps, 1)
                for g in range(2):
                    bank_free(pe, FRONT, R_SC + g, s, f_v, f_a)
                    pe.matmul(fr[g][:, 0:P], f[64 * g:64 * g + 64, 0, :], f[64 * g:64 * g + 64, 1, :],
                              start=True, stop=True).then_inc(f_ps, 1)

            def sums(s, n):
                d, g = n // 2, n % 2
                bank_free(pe, FRONT, R_BC + n, s, f_v, f_a)
                for h in range(4):
                    c = SH * d + 4 * g + h
                    mm = pe.matmul(fr[g][:, P * h:P * (h + 1)], dta[:, c:c + 1].to_broadcast([P, P]),
                                   C["ge" if d else "le"][:, :], start=True, stop=True)
                mm.then_inc(f_ps, 1)

            def gate_sums(s):
                r = rec[s.buf]
                bank_free(pe, FRONT, R_BT, s, f_v, f_a)
                for d in range(2):
                    for pair in range(2):
                        c0 = T_GF + GQK * d + P * pair
                        mm = pe.matmul(fr[R_BT % 2][:, P * (2 * d + pair):P * (2 * d + pair + 1)], r[:, c0:c0 + P],
                                       C["ge_bd" if d else "le_bd"][:, :], start=True, stop=True)
                mm.then_inc(f_ps, 1)

            def turned(s):
                pe.wait_ge(mix_done, s.it + 1)
                for n in range(2):
                    bank_free(pe, TAIL, R_MT + n, s, t_v, t_a)
                    for j in range(4):
                        mm = pe.transpose(tr[n][:, P * j:P * (j + 1)], m[:, P * (4 * n + j):P * (4 * n + j + 1)], ident[:, :])
                    mm.then_inc(t_ps, 1)

            def project(s, k):
                if s is None:
                    return
                if k == 0:
                    pe.wait_ge(t_a, count(TAIL, R_MT, "a", s.it))
                    pe.wait_ge(t_v, count(TAIL, R_MT + 1, "v", s.it))
                for n in range(2):
                    mm = pe.matmul(tr[n][:, :], mT[:, k, :], w_out[:, k, 512 * n:512 * (n + 1)], start=(k == 0), stop=(k == KT - 1))
                    if k == KT - 1:
                        mm.then_inc(t_ps, 1)

            def front(now, before, done):
                if now is not None:
                    sums(now, 0)
                    sums(now, 1)
                if done is not None:
                    turned_x(done)
                if now is not None:
                    sums(now, 2)
                    sums(now, 3)
                if done is not None:
                    router(done)
                if before is not None:
                    turned(before)
                if now is not None:
                    project(before, 0)
                    gate_sums(now)
                    project(before, 1)

            def output(now, before, after):
                if now is None:
                    for k in range(KT):
                        project(before, k)
                    return
                s = now
                it, r, f = s.it, rec[s.buf], feat[s.buf]
                pe.wait_ge(qk_done, it * 2 + 2)
                for hh in range(2):
                    bank_free(pe, FRONT, R_AT + hh, s, f_v, f_a)
                    for dp in range(4):
                        mm = pe.matmul(fr[(R_AT + hh) % 2][:, P * dp:P * (dp + 1)], ki[64 * hh:64 * hh + 64, dp, :],
                                       qd[64 * hh:64 * hh + 64, dp, :], start=True, stop=True)
                    mm.then_inc(f_ps, 1)
                project(before, 2)
                if s.later:
                    pe.wait_ge(next_done, it)
                for g in range(2):
                    bank_free(pe, FRONT, R_PI + g, s, f_v, f_a)
                    for d, h_in in enumerate((st[s.buf], bst[s.buf])):
                        mm = pe.matmul(fr[(R_PI + g) % 2][:, 256 * d:256 * d + 256], f[64 * g:64 * g + 64, 1, :],
                                       h_in[64 * g:64 * g + 64, 0, :], start=True, stop=True)
                    mm.then_inc(f_ps, 1)
                project(before, 3)
                pe.wait_ge(xw_done, it + 1)
                bank_free(pe, FRONT, R_PS, s, f_v, f_a)
                for g in range(2):
                    mm = pe.matmul(fr[R_PS % 2][64 * g:64 * g + 64, 0:256], r[:, T_B + 64 * g:T_B + 64 * g + 64],
                                   xw[:, 256 * g:256 * g + 256], start=True, stop=True)
                mm.then_inc(f_ps, 1)
                pe.wait_ge(kend_done, it + 1)
                for c in range(2):
                    if c:
                        project(before, 4)
                    bank_free(pe, FRONT, R_PG + c, s, f_v, f_a)
                    for h in range(GH):
                        mm = pe.matmul(fr[(R_PG + c) % 2][64 * (h % 2):64 * (h % 2) + 64, P * (h // 2):P * (h // 2 + 1)],
                                       kend[64 * c:64 * c + 64, 64 * h:64 * h + 64],
                                       r[64 * c:64 * c + 64, T_V + GV * h:T_V + GV * (h + 1)], start=True, stop=True)
                    mm.then_inc(f_ps, 1)
                pe.wait_ge(m_ready, it * 4 + 4)
                pe.wait_ge(xd_done, it * 2 + 2)
                if s.later:
                    pe.wait_ge(y_raw, it)
                for h in range(SH):
                    if h == SH // 2:
                        project(before, 5)
                    for d in range(2):
                        mm = pe.matmul(py[:, 64 * h:64 * h + 64], M[2 * d + h // 4][:, h % 4, :], xd[:, d, 64 * h:64 * h + 64],
                                       start=(d == 0), stop=(d == 1))
                mm.then_inc(y_ps, 1)
                project(before, 6)
                pe.wait_ge(am_done, it * 2 + 2)
                pe.wait_ge(mid_done, it + 1)
                if s.later:
                    pe.wait_ge(mix_done, it)
                for hh in range(2):
                    if hh:
                        project(before, 7)
                    for pair in range(2):
                        h = 2 * pair + hh
                        for d in range(2):
                            pe.matmul(po[hh][:, pair, :], am[hh][:, 2 * d + pair, :], r[:, T_V + GV * h:T_V + GV * (h + 1)],
                                      start=(d == 0), stop=False, skip_group_check=True)
                        for d, s_in in enumerate((st[s.buf], bst[s.buf])):
                            for c in range(2):
                                mm = pe.matmul(po[hh][64 * c:64 * c + 64, pair, :],
                                               qd[64 * hh:64 * hh + 64, 2 * d + pair, 64 * c:64 * c + 64],
                                               s_in[64 * hh:64 * hh + 64, 1 + c, P * pair:P * (pair + 1)],
                                               start=False, stop=(d == 1), skip_group_check=True)
                    mm.then_inc(o_ps, 1)

            def turned_x(s):
                pe.wait_ge(xh_done, s.it + 1)
                for n in range(2):
                    bank_free(pe, TAIL, R_XT + n, s, t_v, t_a)
                    for j in range(4):
                        mm = pe.transpose(tr[n][:, P * j:P * (j + 1)], xh[s.buf][:, P * (4 * n + j):P * (4 * n + j + 1)], ident[:, :])
                    mm.then_inc(t_ps, 1)

            def router(s):
                pe.wait_ge(t_a, count(TAIL, R_XT, "a", s.it))
                pe.wait_ge(t_v, count(TAIL, R_XT + 1, "v", s.it))
                for k in range(KT):
                    mm = pe.matmul(tr[R_RT % 2][:, 0:NE], h2T[:, k, :], w_rt[:, k, :], start=(k == 0), stop=(k == KT - 1))
                mm.then_inc(t_ps, 1)

            def tail(s):
                turned_x(s)
                router(s)

            pipeline(pe, ahead, front, output, tail)

        @block.vector
        def _(dve):
            dve.wait_ge(a_exp, 1)
            dve.tensor_scalar(nega[:, :], nega[:, :], -1.0, None, ALU.mult).then_inc(setup_done, 1)
            for n, spread in enumerate((gate_bc, scale_bc, shift_bc)):
                dve.wait_ge(gate_ps, KT * (n + 1))
                for h in range(2):
                    dve.tensor_copy(spread[:, 512 * h:512 * h + 512], tr[h][:, :]).then_inc(gate_done, 1)
            dve.wait_ge(setup_done, 1)
            dve.wait_ge(gate_done, 6)
            dve.wait_ge(setup_pool, 4)
            incl = C["incl"]
            incl_bd = C["incl_bd"]

            def log_decays(s):
                dve.wait_ge(rec_loaded[s.buf], s.use * 48 + 48)
                dve.tensor_tensor(dta[:, :], rec[s.buf][:, T_DT:T_DT + 2 * SH], nega[:, :], ALU.mult).then_inc(dta_done, 1)

            def scores(s):
                for g in range(2):
                    dve.wait_ge(f_ps, s.it * 14 + (R_SC + g + 1))
                    dve.tensor_tensor(scm[:, :, g, :], fr[g][:, 0:P].unsqueeze(1).to_broadcast([P, 2, P]), incl[:, :, :],
                                      ALU.mult).then_inc(f_v, 1)

            def segment(s, n):
                it, d, g = s.it, n // 2, n % 2
                dve.wait_ge(f_ps, it * 14 + (R_BC + n + 1))
                if n == 0:
                    dve.wait_ge(a_copied, it + 1)
                if n >= 2:
                    dve.wait_ge(m_ready, it * 4 + (n - 1))
                for h in range(4):
                    c = SH * d + 4 * g + h
                    i = dve.tensor_scalar(seg[n % 2][:, h, :], fr[g][:, P * h:P * (h + 1)], a_sb[:, c:c + 1], 0.0,
                                          ALU.subtract, ALU.min)
                i.then_inc(seg_done, 1)
                dve.wait_ge(seg_done, it * 4 + (n + 1))
                dve.sem_inc(f_v, 1)

            def decay(s, n):
                it, d, g = s.it, n // 2, n % 2
                dve.wait_ge(seg_exp, it * 4 + (n + 1))
                if n == 0:
                    dve.wait_ge(f_v, it * 13 + 2)
                dve.tensor_tensor(M[n][:, :, :], seg[n % 2][:, :, :], scm[:, d, g, :].unsqueeze(1).to_broadcast([P, 4, P]),
                                  ALU.mult).then_inc(m_ready, 1)

            def decayed_qk(s):
                f = feat[s.buf]
                dve.wait_ge(eb_done, s.it * 2 + 2)
                for dst, e, lo in ((qd, eb, 2), (ki, enb, 4)):
                    src = f[:, lo:lo + 2, :].rearrange("p a b -> p (a b)").unsqueeze(1).to_broadcast([P, 2, 2 * P])
                    dve.tensor_tensor(dst[:, :, :].rearrange("p (d a) b -> p d (a b)", d=2), src,
                                      e[:, :, :].rearrange("p (d a) b -> p d (a b)", d=2), ALU.mult).then_inc(qk_done, 1)

            def gated(s, n):
                it = s.it
                if s.later and n == 0:
                    dve.wait_ge(x_buf_free, it)
                dve.wait_ge(t_ps, it * 7 + (R_OP + n + 1))
                dve.tensor_tensor(x1[s.buf][:, 512 * n:512 * n + 512], tr[n][:, :], gate_bc[:, 512 * n:512 * n + 512],
                                  ALU.mult).then_inc(xg_done, 1)
                dve.wait_ge(xg_done, it * 2 + (n + 1))
                dve.sem_inc(t_v, 1)

            def gains(s):
                dve.wait_ge(t_ps, s.it * 7 + (R_MT + 2))
                dve.tensor_scalar(mT[:, 4:8, :], tr[1][:, :].rearrange("p (a b) -> p a b", a=4), C["cols"][:, R_GG:R_GG + 1],
                                  None, ALU.mult).then_inc(t_v, 1)

            def routed(s):
                dve.wait_ge(t_ps, s.it * 7 + (R_XT + 2))
                for k in range(4, KT):
                    i = dve.tensor_scalar(h2T[:, k, :], tr[1][:, P * (k - 4):P * (k - 3)], mod[:, 4 * KT + k, 0:1],
                                          mod[:, 3 * KT + k, 0:1], ALU.mult, ALU.add)
                i.then_inc(t_v, 1)

            def logits(s):
                it = s.it
                dve.wait_ge(t_ps, it * 7 + (R_RT + 1))
                dve.tensor_copy(route["logits"][:, bass.ds(it, 1), :], tr[R_RT % 2][:, 0:NE].unsqueeze(1)).then_inc(log_done, 1)
                dve.wait_ge(log_done, it + 1)
                dve.sem_inc(t_v, 1)

            def front(now, before, done):
                if now is not None:
                    segment(now, 0)
                    segment(now, 1)
                    decay(now, 0)
                if done is not None:
                    routed(done)
                if now is not None:
                    decay(now, 1)
                    segment(now, 2)
                    segment(now, 3)
                if done is not None:
                    logits(done)
                if before is not None:
                    gains(before)
                if now is not None:
                    decay(now, 2)
                    decay(now, 3)
                    decayed_qk(now)

            def output(now, before, after):
                if now is None:
                    gated(before, 0)
                    gated(before, 1)
                    return
                s = now
                it, r = s.it, rec[s.buf]
                for hh in range(2):
                    dve.wait_ge(f_ps, it * 14 + (R_AT + hh + 1))
                    mask = incl_bd[:, :, :].unsqueeze(2).to_broadcast([P, 2, 2, P])
                    dve.tensor_tensor(am[hh][:, :, :].rearrange("p (d a) b -> p d a b", d=2),
                                      fr[(R_AT + hh) % 2][:, :].rearrange("p (d a b) -> p d a b", d=2, a=2), mask,
                                      ALU.mult).then_inc(am_done, 1)
                    dve.wait_ge(am_done, it * 2 + (hh + 1))
                    dve.sem_inc(f_v, 1)
                for g in range(2):
                    dve.wait_ge(f_ps, it * 14 + (R_PI + g + 1))
                    ea = ex[:, 272:288].rearrange("p (d h) -> p d h", d=2)[:, :, 4 * g:4 * g + 4].unsqueeze(3).to_broadcast([P, 2, 4, SP_])
                    dve.tensor_tensor(yi[:, :, 256 * g:256 * g + 256].rearrange("p d (h c) -> p d h c", h=4),
                                      fr[(R_PI + g) % 2][:, :].rearrange("p (d h c) -> p d h c", d=2, h=4), ea,
                                      ALU.mult).then_inc(pi_done, 1)
                    dve.wait_ge(pi_done, it * 2 + (g + 1))
                    dve.sem_inc(f_v, 1)
                now, nxt = st[s.buf], st[1 - s.buf]
                dve.tensor_tensor(nxt[:, 0, :].rearrange("p (h c) -> p h c", h=4), now[:, 0, :].rearrange("p (h c) -> p h c", h=4),
                                  ex[:, 264:268].unsqueeze(2).to_broadcast([P, 4, SP_]), ALU.mult).then_inc(decayed, 1)
                dve.wait_ge(f_ps, it * 14 + (R_PS + 1))
                dve.wait_ge(decayed, it + 1)
                dve.tensor_tensor(nxt[:, 0, :], nxt[:, 0, :], fr[R_PS % 2][:, 0:256], ALU.add).then_inc(f_v, 1)
                for c in range(2):
                    dve.wait_ge(f_ps, it * 14 + (R_PG + c + 1))
                    if c:
                        dve.wait_ge(mid_done, it + 1)
                    to = now[:, 2, :] if c == 0 else nxt[:, 1, :]
                    for pair in range(2):
                        cs = slice(P * pair, P * (pair + 1))
                        i = dve.scalar_tensor_tensor(out=to[:, cs], in0=now[:, 1 + c, cs],
                                                     scalar=ex[:, 268 + 2 * pair + c:269 + 2 * pair + c],
                                                     in1=fr[(R_PG + c) % 2][:, cs], op0=ALU.mult, op1=ALU.add)
                    i.then_inc(next_done if c else mid_done, 1)
                    dve.wait_ge(next_done if c else mid_done, it + 1)
                    dve.sem_inc(f_v, 1)
                dve.wait_ge(y_ps, it + 1)
                dve.wait_ge(ysum_done, it + 1)
                dve.tensor_tensor(y[:, :], py[:, :], yi[:, 0, :], ALU.add).then_inc(y_raw, 1)
                dve.wait_ge(y_raw, it + 1)
                dve.tensor_tensor(y[:, :], y[:, :], r[:, T_Z:T_Z + SW], ALU.mult).then_inc(y_gated, 1)
                if after is not None:
                    log_decays(after)
                if before is not None:
                    gated(before, 0)
                    gated(before, 1)
                if after is not None:
                    scores(after)
                dve.wait_ge(r_done, it + 1)
                dve.tensor_scalar(m[:, 0:SW], y[:, :], ssm[:, 4:5], None, ALU.mult)
                for hh in range(2):
                    mo = m[:, SW:D].rearrange("p (a b c) -> p a b c", a=2, b=2)[:, :, hh, :]
                    rs = ssm[:, 0:4].rearrange("p (a b) -> p a b", b=2)[:, :, hh:hh + 1].to_broadcast([P, 2, P])
                    dve.tensor_tensor(mo, po[hh][:, :, :], rs, ALU.mult).then_inc(m_step, 1)
                dve.wait_ge(m_step, it * 2 + 2)
                dve.tensor_tensor(m[:, SW:D], m[:, SW:D], r[:, T_GO:T_GO + GW], ALU.mult).then_inc(mix_done, 1)

            def first(s):
                if not s.later:
                    log_decays(s)
                    scores(s)

            def tail(s):
                routed(s)
                logits(s)

            pipeline(dve, first, front, output, tail)


TAB = MAXB + 4
PL_ORDER, PL_PAR, PL_NEXT, PL_LOAD, PL_PAIRS = 0, TAB, 2 * TAB, 3 * TAB, 4 * TAB
PL_FIRST = PL_PAIRS + 1
PL_LEN = PL_FIRST + 1


def load_part(sp, A, weights, w_loaded, n, e, place):
    sp.dma_start(weights[n][:, place, :].rearrange("p a (k f) -> p (a k) f", k=FF // P if n == 2 else KT),
                 A[("w_gate", "w_up", "w_down")[n]][0][e].rearrange("(k p) f -> p k f", p=P)).then_inc(w_loaded[n], 16)


def slots(nc, A, C, route, slot_tok, weights, w_loaded):
    logits, plan = route["logits"], route["plan"]
    with ExitStack() as ctx:
        sem = Names(nc, ctx, "slt")

        def sb(name, shape, dt=F32):
            return ctx.enter_context(nc.sbuf_tensor(f"{name}_r", shape, dt))

        def ps(name, shape):
            return ctx.enter_context(nc.psum_tensor(f"{name}_r", shape, F32))

        s, sel, selm, eq = (sb(n, [P, LT, NE]) for n in ("sig", "sel", "selm", "eq"))
        hot = [sb(f"hot{j}", [P, LT, NE]) for j in range(2)]
        both, base = sb("both", [P, LT, NE]), sb("base", [P, LT, NE])
        bias = sb("bias", [P, NE])
        hi, lo = sb("hi", [P, LT * NG, 2]), sb("lo", [P, LT * NG, 2])
        gscore, geq, goff = (sb(n, [P, LT, NG]) for n in ("gscore", "geq", "goff"))
        t1, t2 = sb("t1", [P, LT * NG]), sb("t2", [P, LT * NG])
        down_g, down_e = sb("down_g", [P, NG]), sb("down_e", [P, NE])
        best = sb("best", [P, LT])
        wsum = sb("wsum", [P, LT])
        prior = sb("prior", [P, LT + 1, NE])
        limits = sb("limits", [P, 16])
        over = sb("over", [P, NE, 16])
        nblk, bend, bstart = sb("nblk", [P, NE]), sb("bend", [P, NE]), sb("bstart", [P, NE])
        diag, ncol, lec = sb("diag", [NE, NE]), sb("ncol", [NE, 1]), sb("lec", [NE, NE])
        past, ends = sb("past", [1, TAB, NE]), sb("ends", [1, TAB, NE])
        held = sb("held", [1, NE])
        blk, eb, order, end = (sb(n, [1, TAB]) for n in ("blk", "eb", "order", "end"))
        due, more = sb("due", [1, TAB]), sb("more", [1, TAB])
        last = sb("last", [1, 1])
        bnum = sb("bnum", [1, TAB])
        npf = sb("npf", [1, MAXB // 2])
        slot_f = sb("slot_f", [P, LT, 2])
        zero_i = sb("zero_i", [P, TAB * 16], I32)
        tok_id = sb("tok_id", [P, LT, 16], I32)
        excl, tot, pb = ps("excl", [P, LT, NE]), ps("tot", [P, LT, NE]), ps("pb", [P, 512])
        bias_loaded, made, sig_done, both_done, ranks_ps, lec_done, bend_ps, slot_done, cleared, scattered, chain = (
            sem(n) for n in ("bias_loaded", "made", "sigmoid_done", "both_done", "ranks_product", "lec_done", "bend_product",
                             "slots_done", "table_cleared", "scattered", "chain"))
        plan_done = sem("plan_done")
        block = ctx.enter_context(nc.Block())

        @block.sync
        def _(sp):
            sp.dma_start(bias[:, :], A["router_bias"].rearrange("(a e) -> a e", a=1).to_broadcast([P, NE])).then_inc(bias_loaded, 16)
            sp.wait_ge(plan_done, 1)
            first = sp.value_load(plan[0:1, PL_FIRST:PL_FIRST + 1], min_val=0, max_val=NE - 1)
            load_part(sp, A, weights, w_loaded, 0, first, slice(0, 1))

        @block.scalar
        def _(act):
            act.activation(s[:, :, :], logits[:, :, :], ACT.Sigmoid).then_inc(sig_done, 1)

        @block.tensor
        def _(pe):
            pe.wait_ge(both_done, 1)
            pe.matmul(excl[:, :, :], C["lt"][:, :], both[:, :, :], start=True, stop=True)
            pe.matmul(tot[:, :, :], C["ones"][:, :], both[:, :, :], start=True, stop=True).then_inc(ranks_ps, 1)
            pe.wait_ge(lec_done, 1)
            pe.matmul(pb[:, 0:NE], C["ones"][0:NE, :], lec[:, :], start=True, stop=True).then_inc(bend_ps, 1)

        @block.gpsimd
        def _(pool):
            pool.iota(down_g[:, :], pattern=[[-1, NG]], base=NG, channel_multiplier=0,
                      allow_small_or_imprecise_dtypes=True).then_inc(made, 1)
            pool.iota(down_e[:, :], pattern=[[-1, NE]], base=NE, channel_multiplier=0,
                      allow_small_or_imprecise_dtypes=True).then_inc(made, 1)
            pool.iota(limits[:, :], pattern=[[P, 16]], base=0, channel_multiplier=0,
                      allow_small_or_imprecise_dtypes=True).then_inc(made, 1)
            pool.iota(bnum[:, :], pattern=[[1, TAB]], base=0, channel_multiplier=0,
                      allow_small_or_imprecise_dtypes=True).then_inc(made, 1)
            pool.iota(tok_id[:, :, :], pattern=[[P, LT], [0, 16]], base=0, channel_multiplier=1).then_inc(made, 1)
            pool.memset(zero_i[:, :], 0).then_inc(made, 1)
            pool.wait_ge(made, 6)
            pool.dma_start(slot_tok.rearrange("(b p) c -> p b c", p=P), zero_i[:, :].rearrange("p (b c) -> p b c", c=16)).then_inc(cleared, 16)
            pool.wait_ge(cleared, 16)
            pool.wait_ge(slot_done, 1)
            for t in range(LT):
                for j in range(2):
                    pool.indirect_dma_start(out=slot_tok, out_offset=bass.IndirectOffsetOnAxis(ap=route["slot"][:, t, j:j + 1], axis=0),
                                            in_=tok_id[:, t, :], in_offset=None).then_inc(scattered, 16)
            pool.wait_ge(scattered, 16 * 2 * LT)

        @block.vector
        def _(dve):
            done = [0]

            def then(ins):
                done[0] += 1
                ins.then_inc(chain, 1)
                dve.wait_ge(chain, done[0])

            def over_e(x):
                return x.unsqueeze(2).to_broadcast([P, LT, NE])

            dve.wait_ge(made, 6)
            dve.wait_ge(bias_loaded, 16)
            dve.wait_ge(sig_done, 1)
            then(dve.tensor_tensor(sel[:, :, :], s[:, :, :], bias[:, :].unsqueeze(1).to_broadcast([P, LT, NE]), ALU.add))
            g4 = sel[:, :, :].rearrange("p t (g e) -> p (t g) e", e=EG)
            then(dve.tensor_tensor(hi[:, :, :], g4[:, :, 0:2], g4[:, :, 2:4], ALU.max))
            then(dve.tensor_tensor(lo[:, :, :], g4[:, :, 0:2], g4[:, :, 2:4], ALU.min))
            then(dve.tensor_tensor(t1[:, :], hi[:, :, 0], hi[:, :, 1], ALU.min))
            then(dve.tensor_tensor(t2[:, :], lo[:, :, 0], lo[:, :, 1], ALU.max))
            then(dve.tensor_tensor(t1[:, :], t1[:, :], t2[:, :], ALU.max))
            then(dve.tensor_tensor(t2[:, :], hi[:, :, 0], hi[:, :, 1], ALU.max))
            gs = gscore[:, :, :].rearrange("p t g -> p (t g)")
            then(dve.tensor_tensor(gs, t1[:, :], t2[:, :], ALU.add))
            then(dve.tensor_reduce(best[:, :], gscore[:, :, :], AX, ALU.max))
            bg = best[:, :].unsqueeze(2).to_broadcast([P, LT, NG])
            then(dve.tensor_tensor(geq[:, :, :], gscore[:, :, :], bg, ALU.is_equal))
            then(dve.tensor_tensor(geq[:, :, :], geq[:, :, :], down_g[:, :].unsqueeze(1).to_broadcast([P, LT, NG]), ALU.mult))
            then(dve.tensor_reduce(best[:, :], geq[:, :, :], AX, ALU.max))
            then(dve.tensor_tensor(geq[:, :, :], geq[:, :, :], bg, ALU.is_equal))
            then(dve.tensor_scalar(goff[:, :, :], geq[:, :, :], -1.0, BIG, ALU.add, ALU.mult))
            in_group = geq[:, :, :].rearrange("p t g -> p (t g)").unsqueeze(2).to_broadcast([P, LT * NG, EG])
            off_group = goff[:, :, :].rearrange("p t g -> p (t g)").unsqueeze(2).to_broadcast([P, LT * NG, EG])
            sm4 = selm[:, :, :].rearrange("p t (g e) -> p (t g) e", e=EG)
            then(dve.tensor_tensor(sm4, g4, in_group, ALU.mult))
            then(dve.tensor_tensor(sm4, sm4, off_group, ALU.add))
            for j in range(2):
                then(dve.tensor_reduce(best[:, :], selm[:, :, :], AX, ALU.max))
                then(dve.tensor_tensor(eq[:, :, :], selm[:, :, :], over_e(best[:, :]), ALU.is_equal))
                then(dve.tensor_tensor(eq[:, :, :], eq[:, :, :], down_e[:, :].unsqueeze(1).to_broadcast([P, LT, NE]), ALU.mult))
                then(dve.tensor_reduce(best[:, :], eq[:, :, :], AX, ALU.max))
                then(dve.tensor_tensor(hot[j][:, :, :], eq[:, :, :], over_e(best[:, :]), ALU.is_equal))
                if j == 0:
                    then(dve.scalar_tensor_tensor(out=selm[:, :, :], in0=hot[0][:, :, :], scalar=-2.0 * BIG, in1=selm[:, :, :],
                                                  op0=ALU.mult, op1=ALU.add))
            dve.tensor_tensor(both[:, :, :], hot[0][:, :, :], hot[1][:, :, :], ALU.add).then_inc(both_done, 1)
            for j in range(2):
                then(dve.tensor_tensor(eq[:, :, :], hot[j][:, :, :], s[:, :, :], ALU.mult))
                then(dve.tensor_reduce(route["gate"][:, :, j], eq[:, :, :], AX, ALU.add))
            then(dve.tensor_tensor(wsum[:, :], route["gate"][:, :, 0], route["gate"][:, :, 1], ALU.add))
            then(dve.reciprocal(wsum[:, :], wsum[:, :]))
            then(dve.tensor_tensor(route["gate"][:, :, :], route["gate"][:, :, :], wsum[:, :].unsqueeze(2).to_broadcast([P, LT, 2]), ALU.mult))
            then(dve.memset(prior[:, 0, :], 0.0))
            dve.wait_ge(ranks_ps, 1)
            for t in range(LT):
                then(dve.tensor_tensor(prior[:, t + 1, :], prior[:, t, :], tot[:, t, :], ALU.add))
            then(dve.tensor_tensor(over[:, :, :], prior[:, LT, :].unsqueeze(2).to_broadcast([P, NE, 16]),
                                   limits[:, :].unsqueeze(1).to_broadcast([P, NE, 16]), ALU.is_gt))
            then(dve.tensor_reduce(nblk[:, :], over[:, :, :], AX, ALU.add))
            then(dve.tensor_tensor(diag[:, :], nblk[0:NE, :], C["ident"][0:NE, 0:NE], ALU.mult))
            then(dve.tensor_reduce(ncol[:, :], diag[:, :], AX, ALU.add))
            dve.tensor_scalar(lec[:, :], C["le"][0:NE, 0:NE], ncol[:, :], None, ALU.mult).then_inc(lec_done, 1)
            dve.wait_ge(bend_ps, 1)
            then(dve.tensor_copy(bend[:, :], pb[:, 0:NE]))
            then(dve.tensor_tensor(bstart[:, :], bend[:, :], nblk[:, :], ALU.subtract))
            then(dve.tensor_scalar(bstart[:, :], bstart[:, :], float(P), None, ALU.mult))
            then(dve.tensor_tensor(base[:, :, :], excl[:, :, :], prior[:, 0:LT, :], ALU.add))
            then(dve.tensor_tensor(base[:, :, :], base[:, :, :], bstart[:, :].unsqueeze(1).to_broadcast([P, LT, NE]), ALU.add))
            for j in range(2):
                then(dve.tensor_tensor(eq[:, :, :], hot[j][:, :, :], base[:, :, :], ALU.mult))
                then(dve.tensor_reduce(slot_f[:, :, j], eq[:, :, :], AX, ALU.add))
            then(dve.tensor_copy(route["slot"][:, :, :], slot_f[:, :, :]))
            dve.sem_inc(slot_done, 1)
            def by_block(x):
                return x.unsqueeze(2).to_broadcast([1, TAB, NE])

            def by_expert(x):
                return x.unsqueeze(1).to_broadcast([1, TAB, NE])
            then(dve.tensor_scalar(last[:, :], bend[0:1, NE - 1:NE], -1.0, None, ALU.add))
            then(dve.tensor_tensor(blk[:, :], bnum[:, :], last[:, :].to_broadcast([1, TAB]), ALU.min))
            then(dve.tensor_tensor(past[:, :, :], by_block(blk[:, :]), by_expert(bend[0:1, :]), ALU.is_ge))
            then(dve.tensor_reduce(eb[:, :], past[:, :, :], AX, ALU.add))
            then(dve.tensor_scalar(ends[:, :, :], past[:, :, :], float(8 * MAXB), None, ALU.mult))
            then(dve.tensor_tensor(ends[:, :, :], ends[:, :, :], by_expert(bend[0:1, :]), ALU.add))
            then(dve.tensor_reduce(end[:, :], ends[:, :, :], AX, ALU.min))
            then(dve.tensor_scalar(held[:, :], nblk[0:1, :], 0.0, None, ALU.is_gt))
            then(dve.tensor_tensor(past[:, :, :], past[:, :, :], by_expert(held[:, :]), ALU.mult))
            then(dve.tensor_reduce(order[:, :], past[:, :, :], AX, ALU.add))
            then(dve.tensor_tensor(past[:, :, :], by_block(end[:, :]), by_expert(bend[0:1, :]), ALU.is_ge))
            then(dve.tensor_reduce(more[:, :], past[:, :, :], AX, ALU.add))
            then(dve.tensor_scalar(more[:, :], more[:, :], float(NE - 1), None, ALU.min))
            then(dve.tensor_copy(plan[:, PL_NEXT:PL_NEXT + TAB], more[:, :]))
            then(dve.memset(due[:, 0:1], 1.0))
            then(dve.tensor_tensor(due[:, 1:TAB], eb[:, 1:TAB], eb[:, 0:TAB - 1], ALU.not_equal))
            then(dve.tensor_tensor(more[:, :], end[:, :], bend[0:1, NE - 1:NE].to_broadcast([1, TAB]), ALU.is_lt))
            then(dve.tensor_tensor(due[:, :], due[:, :], more[:, :], ALU.mult))
            then(dve.tensor_copy(plan[:, PL_LOAD:PL_LOAD + TAB], due[:, :]))
            then(dve.tensor_copy(plan[:, PL_ORDER:PL_ORDER + TAB], order[:, :]))
            then(dve.tensor_scalar(plan[:, PL_PAR:PL_PAR + TAB], plan[:, PL_ORDER:PL_ORDER + TAB], 1, None, ALU.bitwise_and))
            then(dve.tensor_copy(plan[:, PL_FIRST:PL_FIRST + 1], eb[:, 0:1]))
            then(dve.tensor_tensor(npf[:, :], bnum[:, 0:MAXB].rearrange("p (a b) -> p a b", b=2)[:, :, 0],
                                   bend[0:1, NE - 1:NE].to_broadcast([1, MAXB // 2]), ALU.is_lt))
            then(dve.tensor_reduce(eb[:, 0:1], npf[:, :], AX, ALU.add))
            then(dve.tensor_copy(plan[:, PL_PAIRS:PL_PAIRS + 1], eb[:, 0:1]))
            dve.sem_inc(plan_done, 1)


def experts(nc, A, C, route, slot_tok, parts, w_loaded, h_rows, y_slots):
    mod, ident, plan = C["mod"], C["ident"], route["plan"]
    KF = FF // P
    PIECE = KT // 2 * FF
    CREDIT = 8
    F32R = mybir.dt.float32r
    y_b = y_slots.rearrange("(b p) d -> b p d", p=P)
    with ExitStack() as ctx:
        sem = Names(nc, ctx, "exp")

        def sb(name, shape, dt=F32):
            return ctx.enter_context(nc.sbuf_tensor(f"{name}_e", shape, dt))

        def ps(name, shape):
            return ctx.enter_context(nc.psum_tensor(f"{name}_e", shape, F32))

        w_hi, w_lo = sb("w_hi", [P, 3, PIECE], F32R), sb("w_lo", [P, 3, PIECE], F32R)
        toks = sb("toks", [P, TAB, 16], I32)
        idx = [sb(f"idx{b}", [P, 1], I32) for b in range(2)]
        xg = [sb(f"xg{b}", [P, D]) for b in range(2)]
        x_hi, x_lo = ([sb(f"{n}{b}", [P, KT, P], F32R) for b in range(2)] for n in ("x_hi", "x_lo"))
        hs, h = sb("hs", [P, FF]), sb("h", [P, FF])
        h_hi, h_lo = sb("h_hi", [P, KF, P], F32R), sb("h_lo", [P, KF, P], F32R)
        yb = sb("yb", [P, D])
        gate_bc = sb("gate_bc", [P, D])
        tx = [ps(f"tx{b}", [P, 512]) for b in range(2)]
        pg, pu, ph = ps("pg", [P, 512]), ps("pu", [P, 512]), ps("ph", [P, 512])
        pd = [ps(f"pd{b}", [P, 512]) for b in range(2)]
        gathered = [sem(f"x{b}_gathered") for b in range(2)]
        (pool_held, sync_held, act_held, rest_written, toks_loaded, idx_ready, gate_ps, gate_done, hi_done, lo_done, used, xt_ps,
         xhi_done, xlo_done, silu_done, h_done, ht_ps, hhi_done, hlo_done, y_copied, y_free, y_done, stored) = (
            sem(n) for n in ("pool_held", "sync_held", "act_held", "rest_written", "toks_loaded", "idx_ready", "gate_spread",
                             "gate_done", "w_hi_done", "w_lo_done", "piece_used", "x_transposed", "x_hi_done", "x_lo_done",
                             "silu_done", "h_done", "h_transposed", "h_hi_done", "h_lo_done",
                             "y_copied", "y_free", "y_done", "y_stored"))
        block = ctx.enter_context(nc.Block())

        def entry(eng, b, table, most):
            return eng.value_load(plan[0:1, bass.ds(b + table, 1)], min_val=0, max_val=most)

        def pairs(eng, body, unused=None):
            n = eng.value_load(plan[0:1, PL_PAIRS:PL_PAIRS + 1], min_val=1, max_val=MAXB // 2)
            with eng.Fori(0, MAXB // 2) as r:
                with eng.If(r < n):
                    for u in range(2):
                        body(r, u)
                if unused is not None:
                    with eng.Else():
                        for u in range(2):
                            unused(r, u)
            return n

        @block.sync
        def _(sp):
            sp.wait_ge(gate_done, 2)
            for u in range(2):
                sp.wait_ge(gathered[u], 16)
            first = sp.value_load(plan[0:1, PL_FIRST:PL_FIRST + 1], min_val=0, max_val=NE - 1)
            for n in (1, 2):
                load_part(sp, A, parts, w_loaded, n, first, slice(0, 1))

            def body(r, u):
                b = r * 2 + u
                sp.sem_inc(rest_written, 16)
                with sp.If(entry(sp, b, PL_LOAD, 1) > 0):
                    order, par, e = entry(sp, b, PL_ORDER, NE - 1), entry(sp, b, PL_PAR, 1), entry(sp, b, PL_NEXT, NE - 1)
                    for n, split in enumerate((-6, -2, 2)):
                        hold(sp, w_loaded[n], order * 16 + 16, sync_held)
                        hold(sp, lo_done, b * 6 + (CREDIT + split), sync_held)
                        load_part(sp, A, parts, w_loaded, n, e, bass.ds(1 - par, 1))

            def unused(r, u):
                sp.dma_start(y_b[r * 2 + u], gate_bc[:, :]).then_inc(rest_written, 16)
            pairs(sp, body, unused)
            sp.wait_ge(rest_written, MAXB * 16)

        @block.gpsimd
        def _(pool):
            pool.sem_inc(y_free, 1)

            def fetch(b, u):
                pool.tensor_copy(idx[u][:, :], toks[:, bass.ds(b, 1), 0]).then_inc(idx_ready, 1)
                hold(pool, idx_ready, b + 1, pool_held)
                pool.indirect_dma_start(out=xg[u][:, :], out_offset=None, in_=h_rows,
                                        in_offset=bass.IndirectOffsetOnAxis(ap=idx[u][:, 0:1], axis=0)).then_inc(gathered[u], 16)
            pool.dma_start(toks[:, :, :], slot_tok.rearrange("(b p) c -> p b c", p=P)).then_inc(toks_loaded, 16)
            pool.wait_ge(toks_loaded, 16)
            fetch(0, 0)
            fetch(1, 1)
            for b in range(2, 4):
                pool.wait_ge(xt_ps, 2 * b - 2)
                pool.wait_ge(gathered[b % 2], 16)
                fetch(b, b % 2)
            pool.wait_ge(gate_done, 2)

            def body(r, u):
                b = r * 2 + u
                hold(pool, xt_ps, b * 2 + 6, pool_held)
                hold(pool, gathered[u], r * 16 + 32, pool_held)
                fetch(b + 4, u)
                pool.wait_ge(y_copied, b * 2 + 4)
                pool.tensor_tensor(yb[:, :], yb[:, :], gate_bc[:, :], ALU.mult).then_inc(y_done, 1)
                hold(pool, y_done, b + 1, pool_held)
                pool.dma_start(y_b[b], yb[:, :]).then_inc(stored, 16)
                pool.wait_ge(stored, b * 16 + 16)
                pool.sem_inc(y_free, 1)

            n = pairs(pool, body)
            for u in range(2):
                pool.wait_ge(gathered[u], n * 16 + 32)

        SPLITS = {5: (0, 1, 1), 6: (2, 0, 0), 7: (2, 1, 0), 8: (1, 0, 1), 9: (1, 1, 1), 10: (0, 0, 2)}

        def raw(part, half, place):
            return parts[part][:, place, PIECE * half:PIECE * (half + 1)]

        @block.scalar
        def _(act):
            act.wait_ge(gate_done, 2)
            act.sem_inc(y_copied, 2)

            def high(s, part, half, place):
                act.activation(w_hi[:, s % 3:s % 3 + 1, :], raw(part, half, place), ACT.Copy).then_inc(hi_done, 1)

            def features(b, u):
                for q in range(2):
                    act.wait_ge(xt_ps, b * 2 + (q + 1))
                    act.activation(x_hi[u][:, 4 * q:4 * q + 4, :], tx[q][:, :].rearrange("p (a b) -> p a b", a=4),
                                   ACT.Copy).then_inc(xhi_done, 1)

            for s, part, half in ((0, 0, 0), (1, 0, 1), (2, 1, 0), (3, 1, 1)):
                act.wait_ge(w_loaded[part], 16)
                if s == 3:
                    act.wait_ge(used, 1)
                high(s, part, half, slice(0, 1))
                if s == 1:
                    features(0, 0)
                    features(1, 1)
            act.wait_ge(used, 2)
            act.activation(hs[:, :], pg[:, :], ACT.Silu).then_inc(silu_done, 1)
            order = entry(act, 1, PL_ORDER, NE - 1)
            par = entry(act, 1, PL_PAR, 1)
            hold(act, w_loaded[0], order * 16 + 16, act_held)
            high(4, 0, 0, bass.ds(par, 1))

            def body(r, u):
                b = r * 2 + u
                pars = [entry(act, b + n, PL_PAR, 1) for n in range(3)]
                orders = [entry(act, b + n, PL_ORDER, NE - 1) for n in range(3)]

                def piece(s):
                    part, half, n = SPLITS[s]
                    if half == 0:
                        hold(act, w_loaded[part], orders[n] * 16 + 16, act_held)
                    hold(act, used, b * 6 + (s - 2), act_held)
                    high(s, part, half, bass.ds(pars[n], 1))
                piece(5)
                piece(6)
                act.wait_ge(ht_ps, b + 1)
                act.activation(h_hi[:, :, :], ph[:, :].rearrange("p (k c) -> p k c", k=KF), ACT.Copy).then_inc(hhi_done, 1)
                piece(7)
                act.wait_ge(used, b * 6 + 6)
                act.wait_ge(h_done, b + 1)
                act.activation(hs[:, :], pg[:, :], ACT.Silu).then_inc(silu_done, 1)
                piece(8)
                features(b + 2, u)
                piece(9)
                piece(10)
                act.wait_ge(y_free, b + 1)
                for n in range(2):
                    act.activation(yb[:, 512 * n:512 * n + 512], pd[n][:, :], ACT.Copy).then_inc(y_copied, 1)
            pairs(act, body)

        @block.tensor
        def _(pe):
            for j in range(KT):
                pe.matmul(pd[j // 4][:, P * (j % 4):P * (j % 4 + 1)], mod[:, 5 * KT + j, 0:1].to_broadcast([P, P]), ident[:, :],
                          start=True, stop=True).then_inc(gate_ps, 1)
            pe.wait_ge(gate_done, 2)

            def turn(b, use, u):
                pe.wait_ge(gathered[u], use * 16 + 16)
                for q in range(2):
                    if type(b) is not int or b:
                        pe.wait_ge(xlo_done, b * 2 + (q - 1))
                    for j in range(4):
                        mm = pe.transpose(tx[q][:, P * j:P * (j + 1)], xg[u][:, P * (4 * q + j):P * (4 * q + j + 1)], ident[:, :])
                    mm.then_inc(xt_ps, 1)

            def product(s, b, acc, a_hi, a_lo, k, at, start, stop):
                c = slice(at, at + 512)
                for n, (a, w) in enumerate(((a_hi, w_hi), (a_lo, w_hi), (a_hi, w_lo))):
                    mm = pe.matmul(acc[:, :], a[:, k, :], w[:, s % 3, c], start=start and n == 0, stop=stop and n == 2)
                return mm

            def wide(b, s, half, u, acc):
                pe.wait_ge(lo_done, b * 6 + (s + 1 + CREDIT))
                for k in range(4):
                    mm = product(s, b, acc, x_hi[u], x_lo[u], 4 * half + k, FF * k, half + k == 0, half == 1 and k == 3)
                mm.then_inc(used, 1)

            turn(0, 0, 0)
            turn(1, 0, 1)
            pe.wait_ge(xlo_done, 2)
            wide(0, 0, 0, 0, pg)
            wide(0, 1, 1, 0, pg)

            def body(r, u):
                b = r * 2 + u
                wide(b, 2, 0, u, pu)
                wide(b, 3, 1, u, pu)
                pe.wait_ge(xlo_done, b * 2 + 4)
                pe.wait_ge(silu_done, b + 1)
                wide(b, 4, 0, 1 - u, pg)
                pe.wait_ge(h_done, b + 1)
                for j in range(KF):
                    mm = pe.transpose(ph[:, P * j:P * (j + 1)], h[:, P * j:P * (j + 1)], ident[:, :])
                mm.then_inc(ht_ps, 1)
                wide(b, 5, 1, 1 - u, pg)
                turn(b + 2, r + 1, u)
                pe.wait_ge(hlo_done, b + 1)
                pe.wait_ge(y_copied, b * 2 + 2)
                for half in range(2):
                    s = 6 + half
                    pe.wait_ge(lo_done, b * 6 + (s + 1 + CREDIT))
                    for k in range(2):
                        for n in range(2):
                            mm = product(s, b, pd[n], h_hi, h_lo, 2 * half + k, D * k + 512 * n, half + k == 0, half + k == 2)
                    mm.then_inc(used, 1)
            pairs(pe, body)

        @block.vector
        def _(dve):
            for n in range(2):
                dve.wait_ge(gate_ps, KT)
                dve.tensor_copy(gate_bc[:, 512 * n:512 * n + 512], pd[n][:, :]).then_inc(gate_done, 1)
            dve.wait_ge(gate_done, 2)
            dve.sem_inc(lo_done, CREDIT)

            def low(s, part, half, place):
                dve.tensor_tensor(w_lo[:, s % 3:s % 3 + 1, :], raw(part, half, place), w_hi[:, s % 3:s % 3 + 1, :].bitcast(F32),
                                  ALU.subtract).then_inc(lo_done, 1)

            def features(b, u):
                for q in range(2):
                    dve.wait_ge(xhi_done, b * 2 + (q + 1))
                    dve.tensor_tensor(x_lo[u][:, 4 * q:4 * q + 4, :], tx[q][:, :].rearrange("p (a b) -> p a b", a=4),
                                      x_hi[u][:, 4 * q:4 * q + 4, :].bitcast(F32), ALU.subtract).then_inc(xlo_done, 1)

            for s, part, half in ((0, 0, 0), (1, 0, 1), (2, 1, 0), (3, 1, 1)):
                dve.wait_ge(hi_done, s + 1)
                low(s, part, half, slice(0, 1))
                if s == 1:
                    features(0, 0)
                    features(1, 1)
            par = entry(dve, 1, PL_PAR, 1)
            dve.wait_ge(hi_done, 5)
            low(4, 0, 0, bass.ds(par, 1))

            def body(r, u):
                b = r * 2 + u
                pars = [entry(dve, b + n, PL_PAR, 1) for n in range(3)]

                def piece(s):
                    part, half, n = SPLITS[s]
                    dve.wait_ge(hi_done, b * 6 + (s + 1))
                    low(s, part, half, bass.ds(pars[n], 1))
                piece(5)
                dve.wait_ge(used, b * 6 + 4)
                dve.wait_ge(silu_done, b + 1)
                dve.tensor_tensor(h[:, :], pu[:, :], hs[:, :], ALU.mult).then_inc(h_done, 1)
                piece(6)
                dve.wait_ge(hhi_done, b + 1)
                dve.tensor_tensor(h_lo[:, :, :], ph[:, :].rearrange("p (k c) -> p k c", k=KF), h_hi[:, :, :].bitcast(F32),
                                  ALU.subtract).then_inc(hlo_done, 1)
                piece(7)
                piece(8)
                features(b + 2, u)
                piece(9)
                piece(10)
            pairs(dve, body)


def combine(nc, A, C, route, y_slots, x_mid, out):
    out_t = out.rearrange("b (t p) d -> (b t) p d", p=P)
    with ExitStack() as ctx:
        sem = Names(nc, ctx, "cmb")

        def sb(name, shape, dt=F32):
            return ctx.enter_context(nc.sbuf_tensor(f"{name}_c", shape, dt))

        idx = [sb(f"idx{b}", [P, 2], I32) for b in range(2)]
        gates = [sb(f"gates{b}", [P, 2]) for b in range(2)]
        yr = [[sb(f"y{b}{j}", [P, D]) for j in range(2)] for b in range(2)]
        xr = [sb(f"x{b}", [P, D]) for b in range(2)]
        o = [sb(f"o{b}", [P, D]) for b in range(2)]
        junk, fg = sb("junk", [P, D]), sb("fg", [P, D])
        ss = [sb(f"ss{b}", [P, 1]) for b in range(2)]
        mhalf = sb("mhalf", [P, 1])
        sp_held = sem("sp_held")
        pool_held = sem("pool_held")
        x_loaded, gathered, stored = ([sem(f"{n}{b}") for b in range(2)] for n in ("x_loaded", "gathered", "stored"))
        (fg_loaded, half_done, idx_done, added, sum_done, ss_done, r_step, r_done, o_done, o_free) = (sem(n) for n in (
            "fg_loaded", "half_done", "idx_done", "added", "sum_done", "ss_done", "r_step", "r_done", "o_done", "o_free"))
        block = ctx.enter_context(nc.Block())

        def tiles(eng, body):
            with eng.Fori(0, LT // 2 - 1) as r:
                for u in range(2):
                    body(r, u, True)
            for u in range(2):
                body(LT // 2 - 1, u, False)

        @block.sync
        def _(sp):
            sp.dma_start(fg[:, :], A["final_norm_g"].rearrange("(a d) -> a d", a=1).to_broadcast([P, D])).then_inc(fg_loaded, 16)
            sp.sem_inc(o_free, 2)
            for u in range(2):
                sp.dma_start(xr[u][:, :], x_mid[u]).then_inc(x_loaded[u], 16)

            def body(r, u, more):
                it = r * 2 + u
                hold(sp, o_done, it + 1, sp_held)
                if more:
                    sp.dma_start(xr[u][:, :], x_mid[it + 2]).then_inc(x_loaded[u], 16)
                sp.dma_start(out_t[it], o[u][:, :]).then_inc(stored[u], 16)
                sp.wait_ge(stored[u], r * 16 + 16)
                sp.sem_inc(o_free, 1)
            tiles(sp, body)

        @block.gpsimd
        def _(pool):
            pool.memset(mhalf[:, :], -0.5).then_inc(half_done, 1)
            pool.wait_ge(half_done, 1)

            def gather(it, u):
                hold(pool, idx_done, it + 1, pool_held)
                for j in range(2):
                    pool.indirect_dma_start(out=yr[u][j][:, :], out_offset=None, in_=y_slots,
                                            in_offset=bass.IndirectOffsetOnAxis(ap=idx[u][:, j:j + 1], axis=0)).then_inc(gathered[u], 16)

            for u in range(2):
                gather(u, u)

            def body(r, u, more):
                it = r * 2 + u
                hold(pool, ss_done, it + 1, pool_held)
                pool.tensor_scalar(ss[u][:, :], ss[u][:, :], 1.0 / D, EPS, ALU.mult, ALU.add).then_inc(r_step, 1)
                pool.wait_ge(r_step, it + 1)
                pool.tensor_tensor(ss[u][:, :], ss[u][:, :], mhalf[:, :], ALU.pow).then_inc(r_done, 1)
                if more:
                    gather(it + 2, u)
            tiles(pool, body)

        @block.scalar
        def _(act):
            def body(r, u, more):
                it = r * 2 + u
                act.wait_ge(sum_done, it + 1)
                act.activation(junk[:, :], xr[u][:, :], ACT.Square, accum_out=ss[u][:, :]).then_inc(ss_done, 1)
                act.wait_ge(ss_done, it + 1)
            tiles(act, body)

        @block.vector
        def _(dve):
            def indices(it, u):
                dve.tensor_copy(idx[u][:, :], route["slot"][:, bass.ds(it, 1), :].rearrange("p a b -> p (a b)"))
                dve.tensor_copy(gates[u][:, :], route["gate"][:, bass.ds(it, 1), :].rearrange("p a b -> p (a b)")).then_inc(idx_done, 1)

            for u in range(2):
                indices(u, u)
            dve.wait_ge(fg_loaded, 16)

            def body(r, u, more):
                it = r * 2 + u
                dve.wait_ge(idx_done, it + 1)
                dve.wait_ge(x_loaded[u], r * 16 + 16)
                dve.wait_ge(gathered[u], r * 32 + 32)
                dve.scalar_tensor_tensor(out=xr[u][:, :], in0=yr[u][0][:, :], scalar=gates[u][:, 0:1], in1=xr[u][:, :],
                                         op0=ALU.mult, op1=ALU.add).then_inc(added, 1)
                dve.wait_ge(added, it + 1)
                dve.scalar_tensor_tensor(out=xr[u][:, :], in0=yr[u][1][:, :], scalar=gates[u][:, 1:2], in1=xr[u][:, :],
                                         op0=ALU.mult, op1=ALU.add).then_inc(sum_done, 1)
                dve.wait_ge(sum_done, it + 1)
                if more:
                    indices(it + 2, u)
                dve.wait_ge(r_done, it + 1)
                dve.wait_ge(o_free, it + 1)
                dve.scalar_tensor_tensor(out=o[u][:, :], in0=xr[u][:, :], scalar=ss[u][:, :], in1=fg[:, :],
                                         op0=ALU.mult, op1=ALU.mult).then_inc(o_done, 1)
            tiles(dve, body)


_INS = ['x', 'c', 'ctx', 'c_ctx', 'w_mod', 'b_mod', 'norm1_g', 'norm2_g', 'w_in', 'conv_w', 'conv_b', 'dt_bias_f', 'dt_bias_b',
        'a_log_f', 'a_log_b', 'd_skip', 'ssd_norm_g', 'gk_up_f', 'gk_bias_f', 'gk_up_b', 'gk_bias_b', 'gla_norm_g', 'w_out',
        'w_router', 'router_bias', 'w_gate', 'w_up', 'w_down', 'final_norm_g']
_OUTS = [((1, SEQ, D), 'float32')]


def kernel(**inputs):
    import numpy as _np
    import concourse.bacc as _bacc
    from concourse import mybir as _mybir
    from concourse.bass_utils import run_bass_kernel_spmd as _run

    nc = _bacc.Bacc("TRN2", target_bir_lowering=False, num_devices=1)
    arrays, args = {}, {}
    for name in _INS:
        a = _np.ascontiguousarray(inputs[name])
        arrays[f"in_{name}_dram"] = a
        args[name] = nc.dram_tensor(f"in_{name}_dram", a.shape, _mybir.dt.from_np(a.dtype), kind="ExternalInput").ap()
    shape, dtype = _OUTS[0]
    out = nc.dram_tensor("out_0_dram", shape, _mybir.dt.from_np(_np.dtype(dtype)), kind="ExternalOutput").ap()
    build(nc, args, out)
    r = _run(nc, [arrays], core_ids=[0])
    return r.results[0]["out_0_dram"]
```
